# Optimizing a Trainium2 kernel written in Bass

```python
import jax, jax.numpy as jnp
from jax import lax
import numpy as np
import math

D_MODEL = 1024
BATCH = 1
SEQ = 512
DEPTH = 1

N_MEM = 256
HEAD_DIM = 64
ATTN_WIDTH = D_MODEL // 2
CONV_WIDTH = D_MODEL // 4
XATTN_WIDTH = D_MODEL // 4
N_ATTN_HEADS = ATTN_WIDTH // HEAD_DIM
N_XATTN_HEADS = 4
XATTN_HEAD_DIM = XATTN_WIDTH // N_XATTN_HEADS
MIX_WIDTH = ATTN_WIDTH + CONV_WIDTH + XATTN_WIDTH
IN_PROJ_WIDTH = 3 * ATTN_WIDTH + 3 * CONV_WIDTH + XATTN_WIDTH
DILATED_PATTERNS = ((128, 1), (512, 4), (2048, 16))
CONV_K = 3
D_FF = 4 * D_MODEL
ROPE_THETA = 10000.0
EPS = 1e-6
NEG_INF = -1e30


def rms_norm(x, g):
    xf = x.astype(jnp.float32)
    y = xf * lax.rsqrt(jnp.mean(xf * xf, axis=-1, keepdims=True) + EPS)
    return (y * g.astype(jnp.float32)).astype(x.dtype)

def apply_rope(t, positions):
    dh = t.shape[-1]
    half = dh // 2
    inv_freq = jnp.float32(ROPE_THETA) ** (-(jnp.arange(half, dtype=jnp.float32) * 2.0 / dh))
    ang = positions.astype(jnp.float32)[..., None] * inv_freq
    cos = jnp.cos(ang)[:, :, None, :]
    sin = jnp.sin(ang)[:, :, None, :]
    tf = t.astype(jnp.float32)
    t1, t2 = tf[..., :half], tf[..., half:]
    out = jnp.concatenate([t1 * cos - t2 * sin, t1 * sin + t2 * cos], axis=-1)
    return out.astype(t.dtype)

def dilated_window_attention(q, k, v, window, dilation):
    B, S, H, Dh = q.shape
    L = S // dilation
    n_back = window // dilation
    blk = n_back
    nb = -(-L // blk)
    Lp = nb * blk

    def to_blocks(t):
        t = t.reshape(B, L, dilation, H, Dh).transpose(0, 2, 1, 3, 4)
        t = jnp.pad(t, ((0, 0), (0, 0), (0, Lp - L), (0, 0), (0, 0)))
        return t.reshape(B, dilation, nb, blk, H, Dh)

    qb, kb, vb = to_blocks(q), to_blocks(k), to_blocks(v)

    def with_prev(t):
        prev = jnp.pad(t, ((0, 0), (0, 0), (1, 0), (0, 0), (0, 0), (0, 0)))[:, :, :-1]
        return jnp.concatenate([prev, t], axis=3)

    kw, vw = with_prev(kb), with_prev(vb)
    scale = Dh ** -0.5
    s = jnp.einsum('bdnqhc,bdnkhc->bdnhqk', qb, kw,
                   preferred_element_type=jnp.float32) * scale
    qi = jnp.arange(blk)[:, None]
    kj = jnp.arange(2 * blk)[None, :]
    band = (kj >= qi) & (kj <= qi + n_back)
    valid = band[None] & ((jnp.arange(nb)[:, None, None] > 0) | (kj[None] >= blk))
    s = jnp.where(valid[None, None, :, None], s, NEG_INF)
    lse = jax.nn.logsumexp(s, axis=-1)
    p = jnp.exp(s - lse[..., None])
    o = jnp.einsum('bdnhqk,bdnkhc->bdnqhc', p.astype(v.dtype), vw,
                   preferred_element_type=jnp.float32)
    o = o.reshape(B, dilation, Lp, H, Dh)[:, :, :L]
    o = o.transpose(0, 2, 1, 3, 4).reshape(B, S, H, Dh)
    lse = lse.transpose(0, 1, 2, 4, 3).reshape(B, dilation, Lp, H)[:, :, :L]
    lse = lse.transpose(0, 2, 1, 3).reshape(B, S, H)
    return o, lse

def dilated_mixture_attention(q, k, v):
    outs, lses = [], []
    for window, dilation in DILATED_PATTERNS:
        o, lse = dilated_window_attention(q, k, v, window, dilation)
        outs.append(o)
        lses.append(lse)
    w = jax.nn.softmax(jnp.stack(lses, axis=0), axis=0)
    o = jnp.sum(w[..., None] * jnp.stack(outs, axis=0), axis=0)
    return o.astype(q.dtype)

def short_gated_conv(b_gate, c_gate, u, conv_w):
    z = c_gate * u
    S = z.shape[1]
    zp = jnp.pad(z, ((0, 0), (CONV_K - 1, 0), (0, 0)))
    y = zp[:, 0:S] * conv_w[0]
    for tap in range(1, CONV_K):
        y = y + zp[:, tap:tap + S] * conv_w[tap]
    return b_gate * y

def memory_cross_attention(qx, mem_kv):
    B, S, _ = qx.shape
    q = qx.reshape(B, S, N_XATTN_HEADS, XATTN_HEAD_DIM)
    km, vm = jnp.split(mem_kv, 2, axis=-1)
    km = km.reshape(B, -1, N_XATTN_HEADS, XATTN_HEAD_DIM)
    vm = vm.reshape(B, -1, N_XATTN_HEADS, XATTN_HEAD_DIM)
    s = jnp.einsum('bshc,bmhc->bhsm', q, km,
                   preferred_element_type=jnp.float32) * (XATTN_HEAD_DIM ** -0.5)
    p = jax.nn.softmax(s, axis=-1)
    o = jnp.einsum('bhsm,bmhc->bshc', p.astype(vm.dtype), vm)
    return o.reshape(B, S, XATTN_WIDTH)

def first_inputs(seed: int = 0) -> dict:
    key = jax.random.key(seed)
    ks = jax.random.split(key, 20)
    f32 = jnp.float32

    def w(k, shape, fan_in):
        return jax.random.normal(k, shape, f32) * (fan_in ** -0.5)

    def gain(k, width):
        return 1.0 + 0.05 * jax.random.normal(k, (DEPTH, width), f32)

    x = jax.random.normal(ks[0], (BATCH, SEQ, D_MODEL), f32)
    mem = jax.random.normal(ks[1], (BATCH, N_MEM, D_MODEL), f32)
    offset = jax.random.randint(ks[2], (BATCH, 1), 0, 1024, dtype=jnp.int32)
    positions = offset + jnp.arange(SEQ, dtype=jnp.int32)[None, :]
    return {
        "x": x,
        "mem": mem,
        "positions": positions,
        "g_pre_mix": gain(ks[3], D_MODEL),
        "g_mem": gain(ks[4], D_MODEL),
        "w_in": w(ks[5], (DEPTH, D_MODEL, IN_PROJ_WIDTH), D_MODEL),
        "w_mem_kv": w(ks[6], (DEPTH, D_MODEL, 2 * XATTN_WIDTH), D_MODEL),
        "conv_w": w(ks[7], (DEPTH, CONV_K, CONV_WIDTH), CONV_K),
        "g_attn_out": gain(ks[8], ATTN_WIDTH),
        "g_conv_out": gain(ks[9], CONV_WIDTH),
        "g_xattn_out": gain(ks[10], XATTN_WIDTH),
        "w_out": w(ks[11], (DEPTH, MIX_WIDTH, D_MODEL), MIX_WIDTH),
        "g_post_mix": gain(ks[12], D_MODEL),
        "g_pre_mlp": gain(ks[13], D_MODEL),
        "w_up": w(ks[14], (DEPTH, D_MODEL, D_FF), D_MODEL),
        "w_down": w(ks[15], (DEPTH, D_FF, D_MODEL), D_FF),
        "g_post_mlp": gain(ks[16], D_MODEL),
    }

def first_block(x, mem, positions, g_pre_mix, g_mem, w_in, w_mem_kv, conv_w,
              g_attn_out, g_conv_out, g_xattn_out, w_out, g_post_mix,
              g_pre_mlp, w_up, w_down, g_post_mlp):
    B, S, _ = x.shape
    a0 = ATTN_WIDTH
    c0 = 3 * ATTN_WIDTH
    x0 = 3 * ATTN_WIDTH + 3 * CONV_WIDTH
    for l in range(DEPTH):
        h = rms_norm(x, g_pre_mix[l])
        proj = jnp.einsum('bsd,de->bse', h, w_in[l])

        q = proj[..., 0:a0].reshape(B, S, N_ATTN_HEADS, HEAD_DIM)
        k = proj[..., a0:2 * a0].reshape(B, S, N_ATTN_HEADS, HEAD_DIM)
        v = proj[..., 2 * a0:3 * a0].reshape(B, S, N_ATTN_HEADS, HEAD_DIM)
        q = apply_rope(q, positions)
        k = apply_rope(k, positions)
        y_attn = dilated_mixture_attention(q, k, v).reshape(B, S, ATTN_WIDTH)

        b_gate = proj[..., c0:c0 + CONV_WIDTH]
        c_gate = proj[..., c0 + CONV_WIDTH:c0 + 2 * CONV_WIDTH]
        u = proj[..., c0 + 2 * CONV_WIDTH:c0 + 3 * CONV_WIDTH]
        y_conv = short_gated_conv(b_gate, c_gate, u, conv_w[l])

        qx = proj[..., x0:x0 + XATTN_WIDTH]
        mem_kv = jnp.einsum('bmd,de->bme', rms_norm(mem, g_mem[l]), w_mem_kv[l])
        y_x = memory_cross_attention(qx, mem_kv)

        y = jnp.concatenate([rms_norm(y_attn, g_attn_out[l]),
                             rms_norm(y_conv, g_conv_out[l]),
                             rms_norm(y_x, g_xattn_out[l])], axis=-1)
        y = jnp.einsum('bse,ed->bsd', y, w_out[l])
        x = x + rms_norm(y, g_post_mix[l])

        h2 = rms_norm(x, g_pre_mlp[l])
        f = jnp.square(jax.nn.relu(jnp.einsum('bsd,df->bsf', h2, w_up[l])))
        f = jnp.einsum('bsf,fd->bsd', f, w_down[l])
        x = x + rms_norm(f, g_post_mlp[l])
    return x


RWKV_HEADS = 6
RWKV_W = RWKV_HEADS * HEAD_DIM
D_DECAY_LORA = 64
D_AAA_LORA = 64
D_GATE_LORA = 128
RWKV_SPLITS = (RWKV_W, RWKV_W, RWKV_W, D_DECAY_LORA, D_AAA_LORA, D_GATE_LORA)
RWKV_COLS = sum(RWKV_SPLITS)
GN_EPS = 64e-5
NSA_Q_HEADS = 6
NSA_KV_GROUPS = 2
NSA_Q_PER_KV = NSA_Q_HEADS // NSA_KV_GROUPS
NSA_W = NSA_Q_HEADS * HEAD_DIM
NSA_KV_W = NSA_KV_GROUPS * HEAD_DIM
NSA_N_BRANCH = 3
NSA_SPLITS = (NSA_W,) + (NSA_KV_W,) * 6 + (NSA_Q_HEADS * NSA_N_BRANCH,)
NSA_COLS = sum(NSA_SPLITS)
CMP_LEN = 32
CMP_STRIDE = 16
CMP_HIDDEN = 128
SEL_LEN = 64
SEL_TOPK = 16
WINDOW = 512
Q_BLOCK = 64
FORCED_BONUS = 1e3
NEG_INF_2 = -1e30
S5_GROUPS = 16
S5_CH = 16
S5_W = S5_GROUPS * S5_CH
S5_STATE = 64
DT_MIN = 0.001
DT_MAX = 0.1
D_MIX = RWKV_W + NSA_W + S5_W
N_IN = RWKV_COLS + NSA_COLS + S5_W
D_FF_2 = 2816
CONV_W = 3
PLE_DIM = 256
NORM_EPS = 1e-6


def _split(z, sizes):
    cuts = [int(c) for c in np.cumsum(sizes)[:-1]]
    return jnp.split(z, cuts, axis=-1)

def rms_norm_2(x, g):
    xf = x.astype(jnp.float32)
    y = xf * lax.rsqrt(jnp.mean(xf * xf, axis=-1, keepdims=True) + NORM_EPS)
    return (y * g.astype(jnp.float32)).astype(x.dtype)

def masked_softmax(s, mask):
    s = jnp.where(mask, s, NEG_INF_2)
    return jnp.where(mask, jax.nn.softmax(s, axis=-1), 0.0)

def alibi_slopes(n):
    def pow2(m):
        start = 2.0 ** (-8.0 / m)
        return [start ** (i + 1) for i in range(m)]
    if math.log2(n).is_integer():
        return pow2(n)
    c = 2 ** math.floor(math.log2(n))
    return pow2(c) + pow2(2 * c)[0::2][: n - c]

def token_shift(z, mu):
    prev = jnp.pad(z, ((0, 0), (1, 0), (0, 0)))[:, :-1]
    return z + (prev - z) * mu

def rwkv7_mixer(z, w0, w2, a0, a2, g2, k_k, k_a, r_k, gn_w, gn_b):
    B, T, _ = z.shape
    H, N = RWKV_HEADS, HEAD_DIM
    z = z.astype(jnp.float32)
    r, k, v, wl, al, gl = _split(z, RWKV_SPLITS)
    w = -jax.nn.softplus(-(w0 + jnp.tanh(wl) @ w2)) - 0.5
    a = jax.nn.sigmoid(a0 + al @ a2)
    g = jax.nn.sigmoid(gl) @ g2
    heads = lambda t: t.reshape(B, T, H, N)
    kk = heads(k * k_k)
    kk = kk / jnp.maximum(jnp.sqrt(jnp.sum(kk * kk, axis=-1, keepdims=True)), 1e-12)
    k = k * (1.0 + (a - 1.0) * k_a)
    decay = jnp.exp(-jnp.exp(w))
    r_h, k_h, v_h, a_h, d_h = (heads(t) for t in (r, k, v, a, decay))

    def step(S, inp):
        r_t, d_t, k_t, v_t, kk_t, a_t = inp
        sa = jnp.einsum('bhij,bhj->bhi', S, -kk_t)
        S = S * d_t[:, :, None, :] + sa[..., None] * (kk_t * a_t)[:, :, None, :] + v_t[..., None] * k_t[:, :, None, :]
        return S, jnp.einsum('bhij,bhj->bhi', S, r_t)

    tm = lambda t: jnp.moveaxis(t, 1, 0)
    S0 = jnp.zeros((B, H, N, N), jnp.float32)
    _, o = lax.scan(step, S0, tuple(tm(t) for t in (r_h, d_h, k_h, v_h, kk, a_h)))
    o = jnp.moveaxis(o, 0, 1)
    mu = jnp.mean(o, axis=-1, keepdims=True)
    var = jnp.mean(jnp.square(o - mu), axis=-1, keepdims=True)
    o = ((o - mu) * lax.rsqrt(var + GN_EPS)).reshape(B, T, RWKV_W) * gn_w + gn_b
    bonus = jnp.sum(r_h * k_h * r_k.reshape(H, N), axis=-1, keepdims=True) * v_h
    return (o + bonus.reshape(B, T, RWKV_W)) * g

def nsa_mixer(z, pe_k, pe_v, w1_k, w2_k, w1_v, w2_v):
    B, T, _ = z.shape
    G, R, Dh = NSA_KV_GROUPS, NSA_Q_PER_KV, HEAD_DIM
    f32 = jnp.float32
    z = z.astype(f32)
    q, kc, vc, ks, vs, kw, vw, gl = _split(z, NSA_SPLITS)
    kv_heads = lambda t: t.reshape(B, T, G, Dh).transpose(0, 2, 1, 3)
    kc, vc, ks, vs, kw, vw = (kv_heads(t) for t in (kc, vc, ks, vs, kw, vw))

    n_cmp = (T - CMP_LEN) // CMP_STRIDE + 1
    cmp_start = jnp.arange(n_cmp) * CMP_STRIDE
    cmp_end = cmp_start + CMP_LEN - 1
    cmp_idx = cmp_start[:, None] + jnp.arange(CMP_LEN)[None, :]

    def compress(t, pe, w1, w2):
        blocks = (t[:, :, cmp_idx] + pe.astype(f32)).reshape(B, G, n_cmp, CMP_LEN * Dh)
        return jax.nn.gelu(blocks @ w1.astype(f32)) @ w2.astype(f32)

    k_cmp = compress(kc, pe_k, w1_k, w2_k)
    v_cmp = compress(vc, pe_v, w1_v, w2_v)

    n_sel = T // SEL_LEN
    k_top = min(SEL_TOPK, n_sel)
    ks_blk = ks.reshape(B, G, n_sel, SEL_LEN, Dh)
    vs_blk = vs.reshape(B, G, n_sel, SEL_LEN, Dh)
    blk_ids = jnp.arange(n_sel)
    blk_start = blk_ids * SEL_LEN
    overlap = ((cmp_start[:, None] < blk_start[None, :] + SEL_LEN)
               & (cmp_end[:, None] >= blk_start[None, :])).astype(f32)
    gather_blocks = jax.vmap(jax.vmap(lambda blk, sel: blk[sel]))

    win_len = WINDOW + Q_BLOCK - 1
    kw_pad = jnp.pad(kw, ((0, 0), (0, 0), (WINDOW, 0), (0, 0)))
    vw_pad = jnp.pad(vw, ((0, 0), (0, 0), (WINDOW, 0), (0, 0)))

    slopes = jnp.asarray(alibi_slopes(NSA_Q_HEADS), f32).reshape(G, R)[None, :, :, None, None]
    scale = HEAD_DIM ** -0.5
    n_qb = T // Q_BLOCK
    q_blocks = q.reshape(B, n_qb, Q_BLOCK, G, R, Dh).transpose(1, 0, 3, 4, 2, 5)
    g_blocks = jax.nn.sigmoid(gl).reshape(B, n_qb, Q_BLOCK, G, R, NSA_N_BRANCH).transpose(1, 0, 3, 4, 2, 5)

    def query_block(args):
        qb, gb, bi = args
        t0 = bi * Q_BLOCK
        t = t0 + jnp.arange(Q_BLOCK)
        d_c = t[:, None] - cmp_end[None, :]
        s_c = jnp.einsum('bgrqd,bgnd->bgrqn', qb, k_cmp) * scale - slopes * jnp.abs(d_c).astype(f32)
        p_c = masked_softmax(s_c, d_c >= 0)
        o_c = jnp.einsum('bgrqn,bgnd->bgrqd', p_c, v_cmp)
        imp = jnp.einsum('bgrqn,nj->bgqj', p_c, overlap)
        cur = t // SEL_LEN
        valid = blk_start[None, :] <= t[:, None]
        forced = (blk_ids[None, :] == 0) | (blk_ids[None, :] == cur[:, None]) | (blk_ids[None, :] == cur[:, None] - 1)
        score = jnp.where(valid, imp + FORCED_BONUS * forced.astype(f32), -jnp.inf)
        _, sel = lax.top_k(score, k_top)
        k_sel = gather_blocks(ks_blk, sel)
        v_sel = gather_blocks(vs_blk, sel)
        pos = sel[..., None] * SEL_LEN + jnp.arange(SEL_LEN)
        d_s = (t[:, None, None] - pos)[:, :, None]
        s_s = jnp.einsum('bgrqd,bgqnld->bgrqnl', qb, k_sel) * scale - slopes[..., None] * jnp.abs(d_s).astype(f32)
        p_s = masked_softmax(s_s.reshape(B, G, R, Q_BLOCK, k_top * SEL_LEN),
                             (d_s >= 0).reshape(B, G, 1, Q_BLOCK, k_top * SEL_LEN))
        o_s = jnp.einsum('bgrqnl,bgqnld->bgrqd', p_s.reshape(s_s.shape), v_sel)
        k_win = lax.dynamic_slice_in_dim(kw_pad, t0 + 1, win_len, axis=2)
        v_win = lax.dynamic_slice_in_dim(vw_pad, t0 + 1, win_len, axis=2)
        pos_w = t0 - WINDOW + 1 + jnp.arange(win_len)
        d_w = t[:, None] - pos_w[None, :]
        mask_w = (d_w >= 0) & (d_w < WINDOW) & (pos_w[None, :] >= 0)
        s_w = jnp.einsum('bgrqd,bgkd->bgrqk', qb, k_win) * scale - slopes * jnp.abs(d_w).astype(f32)
        o_w = jnp.einsum('bgrqk,bgkd->bgrqd', masked_softmax(s_w, mask_w), v_win)
        return gb[..., 0:1] * o_c + gb[..., 1:2] * o_s + gb[..., 2:3] * o_w

    o = lax.map(query_block, (q_blocks, g_blocks, jnp.arange(n_qb)))
    return o.transpose(1, 0, 4, 2, 3, 5).reshape(B, T, NSA_W)

def _complex_linear_combine(e1, e2):
    a1r, a1i, b1r, b1i = e1
    a2r, a2i, b2r, b2i = e2
    return (a1r * a2r - a1i * a2i, a1r * a2i + a1i * a2r,
            a2r * b1r - a2i * b1i + b2r, a2r * b1i + a2i * b1r + b2i)

def s5_mixer(u, lam_re, lam_im, log_dt, b_re, b_im, c_re, c_im, d_skip, w_glu):
    B, T, _ = u.shape
    f32 = jnp.float32
    u = u.astype(f32).reshape(B, T, S5_GROUPS, S5_CH)
    lam_re, lam_im = lam_re.astype(f32), lam_im.astype(f32)
    b_re, b_im, c_re, c_im = (t.astype(f32) for t in (b_re, b_im, c_re, c_im))
    dt = jnp.exp(log_dt.astype(f32))[:, None]
    mag = jnp.exp(lam_re * dt)
    ab_re, ab_im = mag * jnp.cos(lam_im * dt), mag * jnp.sin(lam_im * dt)
    den = lam_re * lam_re + lam_im * lam_im
    f_re = ((ab_re - 1.0) * lam_re + ab_im * lam_im) / den
    f_im = (ab_im * lam_re - (ab_re - 1.0) * lam_im) / den
    bb_re = f_re[..., None] * b_re - f_im[..., None] * b_im
    bb_im = f_re[..., None] * b_im + f_im[..., None] * b_re
    bu_re = jnp.einsum('gpc,btgc->btgp', bb_re, u)
    bu_im = jnp.einsum('gpc,btgc->btgp', bb_im, u)
    a_re = jnp.broadcast_to(ab_re, bu_re.shape)
    a_im = jnp.broadcast_to(ab_im, bu_im.shape)
    _, _, s_re, s_im = lax.associative_scan(_complex_linear_combine, (a_re, a_im, bu_re, bu_im), axis=1)
    y = (jnp.einsum('gcp,btgp->btgc', c_re, s_re) - jnp.einsum('gcp,btgp->btgc', c_im, s_im)
         + d_skip.astype(f32).reshape(S5_GROUPS, S5_CH) * u)
    y = jax.nn.gelu(y.reshape(B, T, S5_W))
    val, gate = jnp.split(y @ w_glu, 2, axis=-1)
    return val * jax.nn.sigmoid(gate)

def conv_ffn(x, w_up, conv_w, conv_b, w_down):
    hu = x @ w_up
    c = hu.shape[-1]
    hu = lax.conv_general_dilated(hu, conv_w[:, None, :], window_strides=(1,), padding=[(CONV_W - 1, 0)],
                                  dimension_numbers=('NWC', 'WIO', 'NWC'), feature_group_count=c) + conv_b
    gate, up = jnp.split(hu, 2, axis=-1)
    return (jax.nn.gelu(gate, approximate=True) * up) @ w_down

def second_inputs(seed: int = 0) -> dict:
    key = jax.random.key(seed)
    keys = iter(jax.random.split(key, 48))
    f32 = jnp.float32

    def nrm(shape, scale):
        return scale * jax.random.normal(next(keys), shape, f32)

    def gain(shape):
        return 1.0 + 0.02 * jax.random.normal(next(keys), shape, f32)

    def unif(shape, lo, hi):
        return jax.random.uniform(next(keys), shape, f32, lo, hi)

    L = DEPTH
    n = jnp.arange(S5_STATE, dtype=f32)
    return {
        'x': nrm((BATCH, SEQ, D_MODEL), 1.0),
        'p': nrm((DEPTH, BATCH, SEQ, PLE_DIM), 1.0),
        'pre_mix_norm': gain((L, D_MODEL)),
        'post_mix_norm': gain((L, D_MODEL)),
        'pre_ffn_norm': gain((L, D_MODEL)),
        'post_ffn_norm': gain((L, D_MODEL)),
        'w_in': nrm((L, D_MODEL, N_IN), D_MODEL ** -0.5),
        'w_out': nrm((L, D_MIX, D_MODEL), D_MIX ** -0.5),
        'shift_mu': unif((L, RWKV_COLS), 0.0, 1.0),
        'rw_w0': unif((L, RWKV_W), -5.0, -1.0),
        'rw_w2': nrm((L, D_DECAY_LORA, RWKV_W), 0.1),
        'rw_a0': nrm((L, RWKV_W), 0.1),
        'rw_a2': nrm((L, D_AAA_LORA, RWKV_W), 0.3 * D_AAA_LORA ** -0.5),
        'rw_g2': nrm((L, D_GATE_LORA, RWKV_W), D_GATE_LORA ** -0.5),
        'rw_k_k': 0.85 + nrm((L, RWKV_W), 0.02),
        'rw_k_a': gain((L, RWKV_W)),
        'rw_r_k': nrm((L, RWKV_W), 0.1),
        'rw_gn_w': gain((L, RWKV_W)),
        'rw_gn_b': nrm((L, RWKV_W), 0.02),
        'cmp_pe_k': nrm((L, CMP_LEN, HEAD_DIM), 0.02),
        'cmp_pe_v': nrm((L, CMP_LEN, HEAD_DIM), 0.02),
        'cmp_w1_k': nrm((L, CMP_LEN * HEAD_DIM, CMP_HIDDEN), (CMP_LEN * HEAD_DIM) ** -0.5),
        'cmp_w2_k': nrm((L, CMP_HIDDEN, HEAD_DIM), CMP_HIDDEN ** -0.5),
        'cmp_w1_v': nrm((L, CMP_LEN * HEAD_DIM, CMP_HIDDEN), (CMP_LEN * HEAD_DIM) ** -0.5),
        'cmp_w2_v': nrm((L, CMP_HIDDEN, HEAD_DIM), CMP_HIDDEN ** -0.5),
        's5_lam_re': -0.5 + nrm((L, S5_GROUPS, S5_STATE), 0.01),
        's5_lam_im': math.pi * n + nrm((L, S5_GROUPS, S5_STATE), 0.01),
        's5_log_dt': unif((L, S5_GROUPS), math.log(DT_MIN), math.log(DT_MAX)),
        's5_b_re': nrm((L, S5_GROUPS, S5_STATE, S5_CH), (2 * S5_CH) ** -0.5),
        's5_b_im': nrm((L, S5_GROUPS, S5_STATE, S5_CH), (2 * S5_CH) ** -0.5),
        's5_c_re': nrm((L, S5_GROUPS, S5_CH, S5_STATE), (2 * S5_STATE) ** -0.5),
        's5_c_im': nrm((L, S5_GROUPS, S5_CH, S5_STATE), (2 * S5_STATE) ** -0.5),
        's5_d': nrm((L, S5_W), 1.0),
        's5_w_glu': nrm((L, S5_W, 2 * S5_W), S5_W ** -0.5),
        'w_up': nrm((L, D_MODEL, 2 * D_FF_2), D_MODEL ** -0.5),
        'conv_w': nrm((L, CONV_W, 2 * D_FF_2), CONV_W ** -0.5),
        'conv_b': nrm((L, 2 * D_FF_2), 0.02),
        'w_down': nrm((L, D_FF_2, D_MODEL), D_FF_2 ** -0.5),
        'w_ple': nrm((L, PLE_DIM, D_MODEL), PLE_DIM ** -0.5),
        'ple_norm': gain((L, D_MODEL)),
        'w_ple_gate': nrm((L, D_MODEL, D_MODEL), D_MODEL ** -0.5),
    }

def second_block(x, p, pre_mix_norm, post_mix_norm, pre_ffn_norm, post_ffn_norm, w_in, w_out,
              shift_mu, rw_w0, rw_w2, rw_a0, rw_a2, rw_g2, rw_k_k, rw_k_a, rw_r_k, rw_gn_w, rw_gn_b,
              cmp_pe_k, cmp_pe_v, cmp_w1_k, cmp_w2_k, cmp_w1_v, cmp_w2_v,
              s5_lam_re, s5_lam_im, s5_log_dt, s5_b_re, s5_b_im, s5_c_re, s5_c_im, s5_d, s5_w_glu,
              w_up, conv_w, conv_b, w_down, w_ple, ple_norm, w_ple_gate):
    h = x
    for i in range(DEPTH):
        z = rms_norm_2(h, pre_mix_norm[i]) @ w_in[i]
        z_rw, z_nsa, z_s5 = _split(z, (RWKV_COLS, NSA_COLS, S5_W))
        o_rw = rwkv7_mixer(token_shift(z_rw, shift_mu[i]), rw_w0[i], rw_w2[i], rw_a0[i], rw_a2[i], rw_g2[i],
                           rw_k_k[i], rw_k_a[i], rw_r_k[i], rw_gn_w[i], rw_gn_b[i])
        o_nsa = nsa_mixer(z_nsa, cmp_pe_k[i], cmp_pe_v[i], cmp_w1_k[i], cmp_w2_k[i], cmp_w1_v[i], cmp_w2_v[i])
        o_s5 = s5_mixer(z_s5, s5_lam_re[i], s5_lam_im[i], s5_log_dt[i], s5_b_re[i], s5_b_im[i],
                        s5_c_re[i], s5_c_im[i], s5_d[i], s5_w_glu[i])
        mix = jnp.concatenate([o_rw, o_nsa, o_s5], axis=-1).astype(h.dtype) @ w_out[i]
        h = h + rms_norm_2(mix, post_mix_norm[i])
        f = conv_ffn(rms_norm_2(h, pre_ffn_norm[i]), w_up[i], conv_w[i], conv_b[i], w_down[i])
        h = h + rms_norm_2(f, post_ffn_norm[i])
        e = rms_norm_2(p[i] @ w_ple[i], ple_norm[i])
        gate = jax.nn.sigmoid((h @ w_ple_gate[i]).astype(jnp.float32)).astype(h.dtype)
        h = h + gate * e
    return h


def setup_inputs(seed=0):
    out = dict(first_inputs(seed))
    for name, value in second_inputs(seed + 1).items():
        if name != "x":
            out[name + "_2"] = value
    return out


def reference(
    x, mem, positions, g_pre_mix, g_mem, w_in, w_mem_kv, conv_w, g_attn_out, g_conv_out,
    g_xattn_out, w_out, g_post_mix, g_pre_mlp, w_up, w_down, g_post_mlp, p_2, pre_mix_norm_2,
    post_mix_norm_2, pre_ffn_norm_2, post_ffn_norm_2, w_in_2, w_out_2, shift_mu_2, rw_w0_2,
    rw_w2_2, rw_a0_2, rw_a2_2, rw_g2_2, rw_k_k_2, rw_k_a_2, rw_r_k_2, rw_gn_w_2, rw_gn_b_2,
    cmp_pe_k_2, cmp_pe_v_2, cmp_w1_k_2, cmp_w2_k_2, cmp_w1_v_2, cmp_w2_v_2, s5_lam_re_2,
    s5_lam_im_2, s5_log_dt_2, s5_b_re_2, s5_b_im_2, s5_c_re_2, s5_c_im_2, s5_d_2, s5_w_glu_2,
    w_up_2, conv_w_2, conv_b_2, w_down_2, w_ple_2, ple_norm_2, w_ple_gate_2,
):
    x = first_block(
        x, mem, positions, g_pre_mix, g_mem, w_in, w_mem_kv, conv_w, g_attn_out, g_conv_out,
        g_xattn_out, w_out, g_post_mix, g_pre_mlp, w_up, w_down, g_post_mlp,
    )
    return second_block(
        x, p_2, pre_mix_norm_2, post_mix_norm_2, pre_ffn_norm_2, post_ffn_norm_2, w_in_2,
        w_out_2, shift_mu_2, rw_w0_2, rw_w2_2, rw_a0_2, rw_a2_2, rw_g2_2, rw_k_k_2, rw_k_a_2,
        rw_r_k_2, rw_gn_w_2, rw_gn_b_2, cmp_pe_k_2, cmp_pe_v_2, cmp_w1_k_2, cmp_w2_k_2,
        cmp_w1_v_2, cmp_w2_v_2, s5_lam_re_2, s5_lam_im_2, s5_log_dt_2, s5_b_re_2, s5_b_im_2,
        s5_c_re_2, s5_c_im_2, s5_d_2, s5_w_glu_2, w_up_2, conv_w_2, conv_b_2, w_down_2, w_ple_2,
        ple_norm_2, w_ple_gate_2,
    )


_drawn_inputs = setup_inputs


def setup_inputs(seed=0):
    import zlib

    import numpy as np

    out = dict(_drawn_inputs(seed))
    spreads = {}
    factors = {'pre_mix_norm_2': 3.147,
     'post_mix_norm_2': 5.266,
     'pre_ffn_norm_2': 4.597,
     'post_ffn_norm_2': 24.05,
     'rw_a0_2': 2.955,
     'rw_k_k_2': 16.538,
     'rw_k_a_2': 3.401,
     'rw_gn_w_2': 33.123,
     'rw_gn_b_2': 39.367,
     'cmp_pe_k_2': 64.0,
     'cmp_pe_v_2': 55.75,
     's5_lam_re_2': 64.0,
     's5_lam_im_2': 34.024,
     's5_log_dt_2': 42.208,
     's5_b_re_2': 49.8,
     's5_b_im_2': 53.592,
     's5_c_re_2': 43.056,
     's5_c_im_2': 47.72,
     'conv_b_2': 4.562,
     'ple_norm_2': 43.455}
    for name, (base, spread) in spreads.items():
        noise = np.random.default_rng([zlib.crc32(name.encode()), seed]).standard_normal(out[name].shape)
        drawn = base * np.exp(spread * noise) if base else spread * noise
        out[name] = __import__('jax').numpy.asarray(drawn.astype(out[name].dtype))
    for name, factor in factors.items():
        out[name] = (out[name] * factor).astype(out[name].dtype)
    return out
```

```python
from contextlib import ExitStack

import numpy as np

import concourse.bass as bass
from concourse import mybir

F32 = mybir.dt.float32
I32 = mybir.dt.int32
ALU = mybir.AluOpType
ACT = mybir.ActivationFunctionType
AX_X = mybir.AxisListType.X

P = 128
S = 512
TB = S // P
D = 1024
KD = D // P
NM = 256
HD = 64
EPS = 1e-6
GN_EPS = 64e-5
NEG = -1e30
SCALE = HD ** -0.5
AW, CW, XW = 512, 256, 256
FF1 = 4096
FF2 = 2816
NT2 = FF2 // P
RW = 384
PLE = 256
CMP_LEN, CMP_STRIDE = 32, 16
NC = (S - CMP_LEN) // CMP_STRIDE + 1
SLAB = 2048
TWO_PI = 2.0 * np.pi


def alibi(n):
    def pow2(m):
        return [2.0 ** (-8.0 / m * (i + 1)) for i in range(m)]
    c = 2 ** int(np.floor(np.log2(n)))
    return pow2(n) if c == n else pow2(c) + pow2(2 * c)[0::2][: n - c]


def constants():
    p = np.arange(P)[:, None]
    c = {}
    c["ident"] = np.eye(P)
    c["ones"] = np.ones((P, P))
    c["headsum"] = (p // HD == np.arange(P)[None] // HD) * 1.0
    rel = p + 384 - np.arange(S)[None]
    mult = ((rel >= 0) & (rel <= 128)) * 1 + ((rel >= 0) & (rel % 4 == 0)) * 1 + ((rel >= 0) & (rel % 16 == 0)) * 1
    c["band"] = np.where(mult > 0, np.log(np.maximum(mult, 1)) / SCALE, NEG / SCALE)
    c["nomask"] = np.zeros((P, NM))
    for h, sl in enumerate(alibi(6)):
        c[f"causal{h}"] = np.where(rel >= 0, -np.float32(sl) * np.maximum(rel, 0) / SCALE, NEG / SCALE)
    t = p[:, :, None] + P * np.arange(TB)[None, :, None]
    dist = t - (np.arange(NC) * CMP_STRIDE + CMP_LEN - 1)[None, None, :]
    c["cmp"] = np.stack([np.where(dist >= 0, -np.float32(sl) * np.abs(dist) / SCALE, NEG / SCALE) for sl in alibi(6)], 2).reshape(P, -1)
    c["anycmp"] = (p >= CMP_LEN - 1) * 1.0
    inv = (1e4 ** (-(np.arange(32) * 2.0 / HD)))[None, :].repeat(P, 0)
    c["invfreq"] = inv
    t = np.arange(P)[None]
    lt, le = (p < t) * 1.0, (p <= t) * 1.0
    c["chunkmask"] = np.concatenate([le, lt, le], 1)
    c["below"] = (p > t) * 1.0
    b = 1
    while b < P:
        c[f"join{b}"] = ((p // (2 * b) == t // (2 * b)) & (p % (2 * b) < b) & (t % (2 * b) >= b)) * 1.0
        b *= 2
    c["join1T"] = c["join1"].T
    c["headcol"] = (p // HD == np.arange(2)[None]) * 1.0
    c["pairsel"] = ((p // 16) % 2 == np.arange(2)[None]) * 1.0
    c["first"] = (np.arange(S)[None] % P != 0) * np.ones((P, 1))
    nsa = [name for name in c if name.startswith(("causal", "cmp"))]
    names, tables = {}, []
    for which, group in enumerate(([name for name in c if name not in nsa], nsa)):
        at = 0
        for name in group:
            names[name] = (which, at, c[name].shape[1])
            at += c[name].shape[1]
        tables.append(np.ascontiguousarray(np.concatenate([c[name].astype(np.float32) for name in group], 1)))
    return names, tables


class Tally:

    def __init__(self, sem):
        self.sem, self.base, self.total = sem, 0, 0

    def inc(self, times=1):
        self.total += times
        return self.sem, 1

    def dma(self, times=1):
        self.total += 16 * times
        return self.sem, 16

    def at(self, n):
        return self.sem, self.base + n

    def dma_at(self, n):
        return self.sem, self.base + 16 * n


VECTORS = [("g_pre_mix", 8), ("g_mem", 8), ("g_attn_out", 4), ("g_conv_out", 2), ("g_xattn_out", 2), ("g_post_mix", 8),
           ("g_pre_mlp", 8), ("g_post_mlp", 8), ("pre_mix_norm_2", 8), ("post_mix_norm_2", 8), ("pre_ffn_norm_2", 8),
           ("post_ffn_norm_2", 8), ("ple_norm_2", 8), ("shift_mu_2", 11), ("rw_w0_2", 3), ("rw_a0_2", 3), ("rw_k_k_2", 3),
           ("rw_k_a_2", 3), ("rw_r_k_2", 3), ("s5_d_2", 2), ("conv_w", 6), ("conv_b_2", 44), ("s5_lam_re_2", 8),
           ("s5_lam_im_2", 8), ("conv_w_2", 132)]


class Kit:

    def __init__(self, nc, ctx, io):
        self.nc, self.ctx, self.io, self.tallies = nc, ctx, io, {}
        self.names, tables = constants()
        self.widths = [t.shape[1] for t in tables]
        self.tables = [None, None]
        self.buffers = 0
        self.vec_at, at = {}, 0
        for name, n in VECTORS:
            if n < P and at // P != (at + n - 1) // P:
                at = -(-at // P) * P
            self.vec_at[name] = at
            at += n

    def phase(self):
        for t in self.tallies.values():
            t.base = t.total

    def sem(self, name):
        if name not in self.tallies:
            self.tallies[name] = Tally(self.ctx.enter_context(self.nc.semaphore(name)))
        return self.tallies[name]

    def unique(self, name):
        self.buffers += 1
        return f"{name}_{self.buffers}"

    def vec(self, name, n=None):
        return self.vecs[:, self.vec_at[name]:self.vec_at[name] + (n or dict(VECTORS)[name])]

    def const(self, name):
        which, a, n = self.names[name]
        return self.tables[which][:, a:a + n]



IN1, WO1, UP1, DN1, IN2, WO2, UP2, DN2, PLEW, GATEW, NSLABS = 0, 12, 16, 32, 48, 60, 64, 86, 98, 99, 103
Q2, KC2, KS2, GL2, S52 = 1408, 1792, 2048, 2560, 2578


def slab_parts(k, g):
    io = k.io
    slot = k.ring[:, g % 2, :]

    def cols(w, lo, n=256, rows=slice(0, D), at=0, width=256):
        kt = (rows.stop - rows.start) // P
        dst = slot[:, 0:kt * width].rearrange("p (k n) -> p k n", n=width)[:, :, at:at + n]
        return dst, w[rows, lo:lo + n].rearrange("(k p) n -> p k n", p=P)

    if g < 10:
        return [cols(io["w_in"][0], 256 * g)]
    if g < WO1:
        return [cols(io["w_mem_kv"][0], 256 * (g - 10))]
    if g < UP1:
        return [cols(io["w_out"][0], 256 * (g - WO1))]
    if g < DN1:
        return [cols(io["w_up"][0], 256 * (g - UP1))]
    if g < IN2:
        n, kg = divmod(g - DN1, 4)
        return [cols(io["w_down"][0], 256 * n, rows=slice(D * kg, D * kg + D))]
    w = io["w_in_2"][0]
    if g < WO2:
        n = g - IN2
        if n < 5:
            return [cols(w, 256 * n)]
        if n < 7:
            if n == 5:
                return [cols(w, 1280, 128)] + [cols(w, Q2 + HD * h, HD, at=128 + HD * j) for j, h in enumerate((0, 3))]
            return [cols(w, Q2 + HD * h, HD, at=HD * j) for j, h in enumerate((1, 4, 2, 5))]
        if n == 7:
            return [cols(w, KC2)]
        if n == 8:
            return [cols(w, KS2, 128), cols(w, KS2 + 256, 128, at=128)]
        if n == 9:
            return [cols(w, KS2 + 128, 128), cols(w, KS2 + 384, 128, at=128)]
        if n == 10:
            return [cols(w, S52)]
        return [cols(w, GL2, 18, width=18)]
    if g < UP2:
        return [cols(io["w_out_2"][0], 256 * (g - WO2))]
    if g < DN2:
        i, j = divmod(g - UP2, 2)
        return [cols(io["w_up_2"][0], FF2 * j + 256 * i)]
    if g < PLEW:
        n, kg = divmod(g - DN2, 3)
        return [cols(io["w_down_2"][0], 256 * n, rows=slice(D * kg, min(D * kg + D, FF2)))]
    if g == PLEW:
        return [cols(io["w_ple_2"][0], 0, D, rows=slice(0, PLE), width=D)]
    return [cols(io["w_ple_gate_2"][0], 256 * (g - GATEW))]


PARTS = {IN2 + 5: 3, IN2 + 6: 4, IN2 + 8: 2, IN2 + 9: 2}


def loaded_value(g):
    return 16 * sum(PARTS.get(q, 1) for q in range(g % 2, g + 1, 2))


def issue_slab(k, sp, g):
    if g >= NSLABS:
        return
    if g >= 2:
        sp.wait_ge(k.slab_done[g % 2], g // 2)
    for dst, src in slab_parts(k, g):
        sp.dma_start(dst, src).then_inc(k.slab_loaded[g % 2], 16)


def slab_view(k, g, width=256, kt=KD):
    return k.ring[:, g % 2, 0:kt * width].rearrange("p (k n) -> p k n", n=width)



def turn_phase(k, banks, load=(), need=0, gain=None, stream=()):
    nc = k.nc
    k.phase()
    loaded, turned = k.sem("turn_loaded"), k.sem("turned")
    emptied = [k.sem("turn_emptied_dve"), k.sem("turn_emptied_act")]
    nload = len(load)
    with nc.Block() as block:
        @block.sync
        def _(sp):
            for dst, src in load:
                sp.dma_start(dst, src).then_inc(*loaded.dma())
            for g in stream:
                issue_slab(k, sp, g)

        @block.tensor
        def _(pe):
            if nload:
                pe.wait_ge(*loaded.dma_at(nload))
            for b, (srcs, dst) in enumerate(banks):
                if b >= 4:
                    pe.wait_ge(*emptied[b % 2].at(b // 2 - 1))
                for j, s in enumerate(srcs):
                    rows, cols = s.shape
                    t = nc.tensor.transpose(k.pm[0:cols, b % 4, j * rows:(j + 1) * rows], s, k.ident[0:rows, 0:rows])
                t.then_inc(*turned.inc())

        def empty(eng, e):
            for b, (srcs, dst) in enumerate(banks):
                if b % 2 != e:
                    continue
                rows, cols = srcs[0].shape
                src = k.pm[0:cols, b % 4, 0:rows * len(srcs)]
                if len(dst.shape) == 3:
                    src = src.rearrange("p (a b) -> p a b", a=dst.shape[1])
                g = gain(b) if gain else None
                eng.wait_ge(*turned.at(b + 1))
                if e == 0:
                    i = nc.vector.tensor_copy(dst, src) if g is None else nc.vector.tensor_scalar(dst, src, g, None, ALU.mult)
                else:
                    i = nc.scalar.activation(dst, src, ACT.Copy) if g is None else nc.scalar.activation(dst, src, ACT.Copy, scale=g)
                i.then_inc(*emptied[e].inc())

        @block.vector
        def _(dve):
            empty(dve, 0)

        @block.scalar
        def _(act):
            empty(act, 1)


def norm_phase(k, src, dst, gain, kt=KD, n=S, width=D, add=None, then=None):
    nc = k.nc
    k.phase()
    sq_ready, sum_ready, rstd_ready = k.sem("norm_sq"), k.sem("norm_sum"), k.sem("norm_rstd")
    std_ready, scaled, added, out_ready = k.sem("norm_std"), k.sem("norm_scaled"), k.sem("norm_added"), k.sem("norm_out")
    rounds = 2 if then else 1
    with nc.sbuf_tensor(k.unique("sq"), [P, kt, n], F32) as sq, nc.sbuf_tensor(k.unique("std"), [P, 2, n], F32) as std, \
            nc.sbuf_tensor(k.unique("scaled"), [P, 2, n], F32) as tmp, nc.Block() as block:
        @block.scalar
        def _(act):
            for r in range(rounds):
                x = (src, add)[r]
                for i in range(kt):
                    if r:
                        act.wait_ge(*added.at(i + 1))
                        act.wait_ge(*sum_ready.at(1))
                    nc.scalar.activation(sq[:, i, :], x[:, i, 0:n], ACT.Square).then_inc(*sq_ready.inc())
                act.wait_ge(*sum_ready.at(r + 1))
                nc.scalar.activation(std[:, r, :], k.pm[:, r, 0:n], ACT.Sqrt, bias=k.eps[:, 0:1], scale=1.0 / width)\
                    .then_inc(*std_ready.inc())

        @block.tensor
        def _(pe):
            for r in range(rounds):
                for i in range(kt):
                    pe.wait_ge(*sq_ready.at(r * kt + i + 1))
                    m = nc.tensor.matmul(k.pm[:, r, 0:n], k.ones, sq[:, i, :], start=i == 0, stop=i == kt - 1)
                m.then_inc(*sum_ready.inc())

        @block.vector
        def _(dve):
            for r in range(rounds):
                x, g, y = ((src, gain, dst) if r == 0 else (add, then[1], then[0]))
                dve.wait_ge(*std_ready.at(r + 1))
                nc.vector.reciprocal(std[:, r, :], std[:, r, :]).then_inc(*rstd_ready.inc())
                dve.wait_ge(*rstd_ready.at(r + 1))
                for i in range(kt):
                    if add is not None and r == 0:
                        if i >= 2:
                            dve.wait_ge(*added.at(i - 1))
                        nc.vector.scalar_tensor_tensor(out=tmp[:, i % 2, :], in0=x[:, i, :], scalar=g[:, i:i + 1],
                                                       in1=std[:, r, :], op0=ALU.mult, op1=ALU.mult)\
                            .then_inc(*scaled.inc())
                    else:
                        nc.vector.scalar_tensor_tensor(out=y[:, i, 0:n], in0=x[:, i, 0:n], scalar=g[:, i:i + 1],
                                                       in1=std[:, r, :], op0=ALU.mult, op1=ALU.mult)\
                            .then_inc(*out_ready.inc())

        if add is not None:
            @block.gpsimd
            def _(pool):
                for i in range(kt):
                    pool.wait_ge(*scaled.at(i + 1))
                    nc.gpsimd.tensor_tensor(add[:, i, :], add[:, i, :], tmp[:, i % 2, :], ALU.add).then_inc(*added.inc())


def product_phase(k, g0, slabs, x=None):
    nc = k.nc
    k.phase()
    drained = [k.sem("drained_act"), k.sem("drained_dve")]
    n = len(slabs)
    assert True
    with nc.Block() as block:
        @block.sync
        def _(sp):
            for g in range(g0 + 2, g0 + n + 2):
                issue_slab(k, sp, g)

        @block.tensor
        def _(pe):
            seen = [0, 0]
            for i, s in enumerate(slabs):
                g = g0 + i
                j = g % 2
                src, width, kt, nt = s.get("x", x), s.get("width", 256), s.get("kt", KD), s.get("tokens", S)
                w = slab_view(k, g, width, kt)
                pe.wait_ge(k.slab_loaded[j], loaded_value(g))
                if seen[j]:
                    pe.wait_ge(*drained[j].at(seen[j]))
                seen[j] += 1
                if s["kind"] == "features":
                    for c in range(min(width, 256) // P):
                        for q in range(kt):
                            m = nc.tensor.matmul(k.pl[:, 2 * j + c, 0:nt], w[:, q, P * c:P * c + P], src[:, q, 0:nt],
                                                 start=q == 0, stop=q == kt - 1)
                else:
                    for b in range(nt // P):
                        for q in range(kt):
                            m = nc.tensor.matmul(k.pl[:, 2 * j + b // 2, 256 * (b % 2):256 * (b % 2) + width],
                                                 src[:, q, P * b:P * b + P], w[:, q, 0:width],
                                                 start=q == 0, stop=q == kt - 1)
                m.then_inc(k.slab_done[j], 1)

        def empty(eng, j):
            for i, s in enumerate(slabs):
                g = g0 + i
                if g % 2 != j:
                    continue
                width, nt = s.get("width", 256), s.get("tokens", S)
                eng.wait_ge(k.slab_done[j], g // 2 + 1)
                if s["kind"] == "features":
                    pairs = [(s["to"](c), k.pl[:, 2 * j + c, 0:nt]) for c in range(2)]
                else:
                    pairs = [(s["to"][:, b, :], k.pl[:, 2 * j + b // 2, 256 * (b % 2):256 * (b % 2) + width]) for b in range(nt // P)]
                for dst, src in pairs:
                    m = nc.scalar.activation(dst, src, ACT.Copy) if j == 0 else nc.vector.tensor_copy(dst, src)
                m.then_inc(*drained[j].inc())

        @block.scalar
        def _(act):
            empty(act, 0)

        @block.vector
        def _(dve):
            empty(dve, 1)


def down_phase(k, g0, f, y, groups, ktiles, w):
    nc = k.nc
    k.phase()
    drained = [k.sem("drained_act"), k.sem("drained_dve")]
    body = 2 * groups
    turns = D // 512
    with nc.Block() as block:
        @block.sync
        def _(sp):
            for g in range(g0 + 2, g0 + turns * body + 2):
                issue_slab(k, sp, g)

        @block.tensor
        def _(pe):
            def turn(i):
                for n in range(2):
                    if turns > 1:
                        pe.wait_ge(*drained[n].at(i))
                    for q in range(groups):
                        s = n * groups + q
                        j = s % 2
                        g = g0 + s
                        pe.wait_ge(k.slab_loaded[j], loaded_value(g) + 16 * (body // 2) * i)
                        wv = slab_view(k, g)
                        for c in range(2):
                            kt = min(8, ktiles - 8 * q)
                            for t in range(kt):
                                m = nc.tensor.matmul(k.pl[:, 2 * n + c, :], wv[:, t, P * c:P * c + P], f[:, 8 * q + t, :],
                                                     start=q == 0 and t == 0, stop=q == groups - 1 and t == kt - 1)
                        m.then_inc(k.slab_done[j], 1)
            with pe.Fori(0, turns) as i:
                turn(i)

        def empty(eng, n):
            last = n * groups + groups - 1
            with eng.Fori(0, turns) as i:
                eng.wait_ge(k.slab_done[last % 2], (g0 + last) // 2 + 1 + (body // 2) * i)
                out = y[:, bass.ds(4 * i + 2 * n, 2), :]
                if n == 0:
                    nc.scalar.activation(out, k.pl[:, 0:2, :], ACT.Copy).then_inc(*drained[0].inc(turns))
                else:
                    nc.vector.tensor_copy(out, k.pl[:, 2:4, :]).then_inc(*drained[1].inc(turns))

        @block.scalar
        def _(act):
            empty(act, 0)

        @block.vector
        def _(dve):
            empty(dve, 1)


def up_phase(k, g0, x, f):
    nc = k.nc
    k.phase()
    drained = [k.sem("drained_act"), k.sem("drained_dve")]
    relu_ready = k.sem("relu_ready")
    turns = FF1 // 512
    w_up = k.io["w_up"][0]
    with nc.sbuf_tensor(k.unique("relu"), [P, 2, 2, S], F32) as relu, nc.Block() as block:
        @block.sync
        def _(sp):
            with sp.Fori(0, turns - 1) as i:
                for j in range(2):
                    sp.wait_ge(k.slab_done[j], g0 // 2 + 1 + i)
                    src = w_up[:, bass.ds(512 * i + 512 + 256 * j, 256)].rearrange("(k p) n -> p k n", p=P)
                    sp.dma_start(slab_view(k, j), src).then_inc(k.slab_loaded[j], 16)
            for g in range(g0 + 2 * turns, g0 + 2 * turns + 2):
                issue_slab(k, sp, g)

        @block.tensor
        def _(pe):
            with pe.Fori(0, turns) as i:
                for j in range(2):
                    pe.wait_ge(k.slab_loaded[j], loaded_value(g0 + j) + 16 * i)
                    pe.wait_ge(*drained[j].at(i))
                    w = slab_view(k, j)
                    for c in range(2):
                        for q in range(KD):
                            m = nc.tensor.matmul(k.pl[:, 2 * j + c, :], w[:, q, P * c:P * c + P], x[:, q, :],
                                                 start=q == 0, stop=q == KD - 1)
                    m.then_inc(k.slab_done[j], 1)

        @block.scalar
        def _(act):
            with act.Fori(0, turns) as i:
                for j in range(2):
                    act.wait_ge(k.slab_done[j], g0 // 2 + 1 + i)
                    act.wait_ge(*drained[j].at(i))
                    nc.scalar.activation(relu[:, j], k.pl[:, 2 * j:2 * j + 2, :], ACT.Relu)\
                        .then_inc(*relu_ready.inc(turns))

        @block.vector
        def _(dve):
            with dve.Fori(0, turns) as i:
                for j in range(2):
                    dve.wait_ge(*relu_ready.at(2 * i + j + 1))
                    nc.vector.tensor_tensor(f[:, bass.ds(4 * i + 2 * j, 2), :], relu[:, j], k.pl[:, 2 * j:2 * j + 2, :],
                                            ALU.mult).then_inc(*drained[j].inc(turns))


def conv_up_phase(k, g0, x, f):
    nc = k.nc
    k.phase()
    tap2, tap1, conv = k.sem("conv_tap2"), k.sem("conv_tap1"), [k.sem("conv_gate_ready"), k.sem("conv_up_ready")]
    gelu_ready, f_ready = k.sem("gelu_ready"), k.sem("ffn_ready")
    turns = FF2 // 256
    w_up = k.io["w_up_2"][0]
    cw, cb = k.vec("conv_w_2").rearrange("p (t n) -> p t n", t=3), k.vec("conv_b_2")
    with nc.sbuf_tensor(k.unique("conv"), [P, 2, 2, S], F32) as cv, nc.sbuf_tensor(k.unique("gelu"), [P, 2, S], F32) as ge, \
            nc.Block() as block:
        @block.sync
        def _(sp):
            with sp.Fori(0, turns - 1) as i:
                for j in range(2):
                    sp.wait_ge(k.slab_done[j], g0 // 2 + 1 + i)
                    src = w_up[:, bass.ds(256 * i + 256 + FF2 * j, 256)].rearrange("(k p) n -> p k n", p=P)
                    sp.dma_start(slab_view(k, j), src).then_inc(k.slab_loaded[j], 16)
            for g in range(g0 + 2 * turns, g0 + 2 * turns + 2):
                issue_slab(k, sp, g)

        @block.tensor
        def _(pe):
            with pe.Fori(0, turns) as i:
                for j in range(2):
                    pe.wait_ge(k.slab_loaded[j], loaded_value(g0 + j) + 16 * i)
                    pe.wait_ge(*conv[j].at(2 * i + 1))
                    w = slab_view(k, j)
                    for c in range(2):
                        for q in range(KD):
                            m = nc.tensor.matmul(k.pl[:, 2 * j + c, :], w[:, q, P * c:P * c + P], x[:, q, :],
                                                 start=q == 0, stop=q == KD - 1)
                    m.then_inc(k.slab_done[j], 1)

        @block.scalar
        def _(act):
            with act.Fori(0, turns) as i:
                for j in range(2):
                    act.wait_ge(k.slab_done[j], g0 // 2 + 1 + i)
                    act.wait_ge(*f_ready.at(2 * i + 1))
                    for c in range(2):
                        n = 2 * i + (NT2 * j + c)
                        nc.scalar.activation(cv[:, j, c, :], k.pl[:, 2 * j + c, :], ACT.Identity,
                                             scale=cw[:, 2, bass.ds(n, 1)], bias=cb[:, bass.ds(n, 1)])\
                            .then_inc(*tap2.inc(turns))
                for c in range(2):
                    act.wait_ge(*conv[0].at(2 * i + c + 2))
                    nc.scalar.activation(ge[:, c, :], cv[:, 0, c, :], ACT.Gelu_apprx_tanh).then_inc(*gelu_ready.inc(turns))

        @block.vector
        def _(dve):
            for j in range(2):
                dve.sem_inc(*conv[j].inc())
            with dve.Fori(0, turns) as i:
                for j in range(2):
                    for c in range(2):
                        n = 2 * i + (NT2 * j + c)
                        dve.wait_ge(*tap2.at(4 * i + 2 * j + c + 1))
                        nc.vector.scalar_tensor_tensor(out=cv[:, j, c, 1:S], in0=k.pl[:, 2 * j + c, 0:S - 1],
                                                       scalar=cw[:, 1, bass.ds(n, 1)], in1=cv[:, j, c, 1:S],
                                                       op0=ALU.mult, op1=ALU.add).then_inc(*tap1.inc(turns))
                    for c in range(2):
                        n = 2 * i + (NT2 * j + c)
                        dve.wait_ge(*tap1.at(4 * i + 2 * j + c + 1))
                        nc.vector.scalar_tensor_tensor(out=cv[:, j, c, 2:S], in0=k.pl[:, 2 * j + c, 0:S - 2],
                                                       scalar=cw[:, 0, bass.ds(n, 1)], in1=cv[:, j, c, 2:S],
                                                       op0=ALU.mult, op1=ALU.add).then_inc(*conv[j].inc(turns))

        @block.gpsimd
        def _(pool):
            pool.sem_inc(*f_ready.inc())
            with pool.Fori(0, turns) as i:
                for c in range(2):
                    pool.wait_ge(*gelu_ready.at(2 * i + c + 1))
                    pool.wait_ge(*conv[1].at(2 * i + c + 2))
                    nc.gpsimd.tensor_tensor(f[:, bass.ds(2 * i + c, 1), :], ge[:, c:c + 1, :], cv[:, 1, c:c + 1, :],
                                            ALU.mult).then_inc(*f_ready.inc(turns))


def attend(k, units):
    nc = k.nc
    k.phase()
    n = len(units)
    scored, masked, p_ready = k.sem("scored"), k.sem("masked"), k.sem("p_ready")
    turned, copied = k.sem("p_turned"), [k.sem("p_copied_dve"), k.sem("p_copied_act")]
    mixed, inverted, out_ready = k.sem("pv_mixed"), k.sem("sum_inverted"), k.sem("out_ready")
    LAG_T, LAG_V = 2, 3
    with nc.sbuf_tensor(k.unique("masked"), [P, 3, S], F32) as sm, nc.sbuf_tensor(k.unique("probs"), [P, 3, S], F32) as pr, \
            nc.sbuf_tensor(k.unique("probsT"), [P, 2, TB, P], F32) as pt, nc.sbuf_tensor(k.unique("rowneg"), [P, n], F32) as rn, \
            nc.sbuf_tensor(k.unique("rowsum"), [P, n], F32) as rs, nc.sbuf_tensor(k.unique("weight"), [P, n], F32) as wt, \
            nc.Block() as block:
        widths = [u["k"].shape[1] for u in units]
        pieces = [[(a, min(P, w - a)) for a in range(0, w, P)] for w in widths]

        @block.tensor
        def _(pe):
            for t in range(n + LAG_V):
                if t < n:
                    u = units[t]
                    if t >= 4:
                        pe.wait_ge(*masked.at(t - 3))
                    nc.tensor.matmul(k.pl[:, t % 4, 0:widths[t]], u["q"], u["k"], start=True, stop=True)\
                        .then_inc(*scored.inc())
                if 0 <= t - LAG_T < n:
                    s = t - LAG_T
                    pe.wait_ge(*p_ready.at(s + 1))
                    if s >= 2:
                        pe.wait_ge(*copied[s % 2].at(s // 2))
                    for b, (a, w) in enumerate(pieces[s]):
                        m = nc.tensor.transpose(k.pm[0:w, s % 2, P * b:P * b + P], pr[:, s % 3, a:a + w], k.ident)
                    m.then_inc(*turned.inc())
                if 0 <= t - LAG_V < n:
                    s = t - LAG_V
                    pe.wait_ge(*copied[s % 2].at(s // 2 + 1))
                    if s >= 2:
                        pe.wait_ge(*out_ready.at(s - 1))
                    for b, (a, w) in enumerate(pieces[s]):
                        m = nc.tensor.matmul(k.pm[:, 2 + s % 2, 0:HD], pt[0:w, s % 2, b, :], units[s]["v"](b),
                                             start=b == 0, stop=b == len(pieces[s]) - 1)
                    m.then_inc(*mixed.inc())

        def copy(eng, s, e):
            ps = pieces[s]
            w = ps[-1][1]
            eng.wait_ge(*turned.at(s + 1))
            if s >= 2:
                eng.wait_ge(*mixed.at(s - 1))
            dst, src = pt[0:w, s % 2, 0:len(ps), :], k.pm[0:w, s % 2, 0:P * len(ps)].rearrange("p (b q) -> p b q", q=P)
            if e == 0:
                nc.vector.tensor_copy(dst, src).then_inc(*copied[0].inc())
            else:
                nc.scalar.activation(dst, src, ACT.Copy).then_inc(*copied[1].inc())

        @block.vector
        def _(dve):
            for t in range(n + LAG_V):
                if t < n:
                    u = units[t]
                    dve.wait_ge(*scored.at(t + 1))
                    if t >= 3:
                        dve.wait_ge(*p_ready.at(t - 2))
                    nc.vector.tensor_tensor_reduce(sm[:, t % 3, 0:widths[t]], k.pl[:, t % 4, 0:widths[t]], u["mask"],
                                                   -SCALE, 3e38, ALU.add, ALU.min, rn[:, t:t + 1])\
                        .then_inc(*masked.inc())
                if 0 <= t - LAG_V < n:
                    s = t - LAG_V
                    dve.wait_ge(*p_ready.at(s + 1))
                    nc.vector.reciprocal(wt[:, s:s + 1], rs[:, s:s + 1]).then_inc(*inverted.inc())
                if 0 <= t - LAG_T < n and (t - LAG_T) % 2 == 0:
                    copy(dve, t - LAG_T, 0)
                if 0 <= t - LAG_V < n:
                    s = t - LAG_V
                    u = units[s]
                    dve.wait_ge(*inverted.at(u_inv(units, s)))
                    if u.get("gate") is not None:
                        nc.vector.tensor_tensor(wt[:, s:s + 1], wt[:, s:s + 1], u["gate"], ALU.mult).then_inc(*inverted.inc())
                        dve.wait_ge(*inverted.at(u_inv(units, s) + 1))
                    dve.wait_ge(*mixed.at(s + 1))
                    src = k.pm[:, 2 + s % 2, 0:HD]
                    if u.get("onto") is not None:
                        dve.wait_ge(*out_ready.at(u["onto"] + 1))
                        m = nc.vector.scalar_tensor_tensor(out=u["out"], in0=src, scalar=wt[:, s:s + 1], in1=u["out"],
                                                           op0=ALU.mult, op1=ALU.add)
                    else:
                        m = nc.vector.tensor_scalar(u["out"], src, wt[:, s:s + 1], None, ALU.mult)
                    m.then_inc(*out_ready.inc())

        @block.scalar
        def _(act):
            for t in range(n + LAG_V):
                if t < n:
                    act.wait_ge(*masked.at(t + 1))
                    if t >= 3:
                        act.wait_ge(*turned.at(t - 2))
                    nc.scalar.activation(pr[:, t % 3, 0:widths[t]], sm[:, t % 3, 0:widths[t]], ACT.Exp,
                                         bias=rn[:, t:t + 1], scale=-1.0, accum_out=rs[:, t:t + 1])\
                        .then_inc(*p_ready.inc())
                if 0 <= t - LAG_T < n and (t - LAG_T) % 2 == 1:
                    copy(act, t - LAG_T, 1)


def u_inv(units, s):
    return s + 1 + sum(u.get("gate") is not None for u in units[:s])


def sincos(k, dve, act, ang, out, tmp, steps, marks):
    nc = k.nc
    C1, C2 = 6.28125, float(np.float32(TWO_PI - 6.28125))
    C3 = float(TWO_PI - 6.28125 - np.float64(np.float32(TWO_PI - 6.28125)))
    MAGIC = 12582912.0
    if dve is not None:
        def step(i):
            i.then_inc(*steps.inc())
            dve.wait_ge(*steps.at(steps.total - steps.base))
        for q in range(2):
            y, t = out[:, q], tmp[:, q]
            step(nc.vector.tensor_scalar(t, ang, 1.0 / TWO_PI, 0.25 * q, ALU.mult, ALU.add))
            step(nc.vector.tensor_scalar(t, t, MAGIC, None, ALU.add))
            step(nc.vector.tensor_scalar(t, t, -MAGIC, None, ALU.add))
            step(nc.vector.scalar_tensor_tensor(out=y, in0=t, scalar=-C1, in1=ang, op0=ALU.mult, op1=ALU.add))
            step(nc.vector.scalar_tensor_tensor(out=y, in0=t, scalar=-C2, in1=y, op0=ALU.mult, op1=ALU.add))
            step(nc.vector.scalar_tensor_tensor(out=y, in0=t, scalar=-C3, in1=y, op0=ALU.mult, op1=ALU.add))
            if q:
                step(nc.vector.tensor_scalar(y, y, TWO_PI / 4, None, ALU.add))
            step(nc.vector.tensor_scalar(y, y, 3.1415925, -3.1415925, ALU.min, ALU.max))


def rope_phase(k, qkv):
    nc = k.nc
    k.phase()
    loaded, steps, sines, parts, roped = k.sem("pos_loaded"), k.sem("angle_steps"), k.sem("sines_ready"), k.sem("rope_parts"), k.sem("roped")
    qk = qkv[:, :, 0:2 * AW].rearrange("p b (h t c) -> p b h t c", t=2, c=32)
    with nc.sbuf_tensor(k.unique("posi"), [P, TB], I32) as posi, nc.sbuf_tensor(k.unique("posf"), [P, TB], F32) as posf, \
            nc.sbuf_tensor(k.unique("ang"), [P, TB, 32], F32) as ang, nc.sbuf_tensor(k.unique("angt"), [P, 2, TB, 32], F32) as angt, \
            nc.sbuf_tensor(k.unique("sc"), [P, 2, TB, 32], F32) as sc, nc.sbuf_tensor(k.unique("ropea"), [P, 4, TB, 16, 32], F32) as ra, \
            nc.Block() as block:
        @block.sync
        def _(sp):
            sp.dma_start(posi[:], k.io["positions"][0].rearrange("(b p) -> p b", p=P), allow_slow_non_contiguous=True).then_inc(*loaded.dma())

        def bc(q):
            return sc[:, q].unsqueeze(2).broadcast_to([P, TB, 16, 32])

        @block.vector
        def _(dve):
            dve.wait_ge(*loaded.dma_at(1))
            nc.vector.tensor_copy(posf[:], posi[:]).then_inc(*steps.inc())
            dve.wait_ge(*steps.at(1))
            for b in range(TB):
                nc.vector.tensor_scalar(ang[:, b, :], k.const("invfreq"), posf[:, b:b + 1], None, ALU.mult).then_inc(*steps.inc())
            dve.wait_ge(*steps.at(1 + TB))
            sincos(k, dve, None, ang[:], sc, angt, steps, None)
            dve.wait_ge(*sines.at(1))
            for b in range(TB):
                pass
            for b in range(TB):
                sn = sc[:, 0, b].unsqueeze(1).broadcast_to([P, 16, 32])
                cs = sc[:, 1, b].unsqueeze(1).broadcast_to([P, 16, 32])
                t1, t2 = qk[:, b, :, 0, :], qk[:, b, :, 1, :]
                nc.vector.tensor_tensor(ra[:, 0, b], t1, cs, ALU.mult).then_inc(*parts.inc())
                nc.vector.tensor_tensor(ra[:, 1, b], t2, sn, ALU.mult).then_inc(*parts.inc())
                dve.wait_ge(*k.sem("rope_parts_pool").at(2 * b + 2))
                dve.wait_ge(*parts.at(2 * b + 2))
                nc.vector.tensor_tensor(t1, ra[:, 0, b], ra[:, 1, b], ALU.subtract).then_inc(*roped.inc())

        @block.gpsimd
        def _(pool):
            pool.wait_ge(*sines.at(1))
            parts2 = k.sem("rope_parts_pool")
            for b in range(TB):
                sn = sc[:, 0, b].unsqueeze(1).broadcast_to([P, 16, 32])
                cs = sc[:, 1, b].unsqueeze(1).broadcast_to([P, 16, 32])
                t1, t2 = qk[:, b, :, 0, :], qk[:, b, :, 1, :]
                nc.gpsimd.tensor_tensor(ra[:, 2, b], t1, sn, ALU.mult).then_inc(*parts2.inc())
                nc.gpsimd.tensor_tensor(ra[:, 3, b], t2, cs, ALU.mult).then_inc(*parts2.inc())
                pool.wait_ge(*parts2.at(2 * b + 2))
                pool.wait_ge(*parts.at(2 * b + 2))
                nc.gpsimd.tensor_tensor(t2, ra[:, 2, b], ra[:, 3, b], ALU.add).then_inc(*k.sem("roped_pool").inc())

        @block.scalar
        def _(act):
            act.wait_ge(*steps.at(steps.total - steps.base))
            nc.scalar.activation(sc[:], sc[:], ACT.Sin).then_inc(*sines.inc())


def head_norm_phase(k, y, groups):
    nc = k.nc
    k.phase()
    squared, std_ready, inv_ready, out = k.sem("hn_squared"), k.sem("hn_std"), k.sem("hn_inv"), k.sem("hn_out")
    n = len(groups) * TB
    with nc.sbuf_tensor(k.unique("hsq"), [P, AW], F32) as sq, nc.sbuf_tensor(k.unique("hss"), [P, n], F32) as ss, nc.Block() as block:
        @block.scalar
        def _(act):
            for q, (lo, hi) in enumerate(groups):
                for b in range(TB):
                    i = q * TB + b
                    if i:
                        act.wait_ge(*squared.at(i))
                    nc.scalar.activation(sq[:, 0:hi - lo], y[:, b, lo:hi], ACT.Square, accum_out=ss[:, i:i + 1])\
                        .then_inc(*squared.inc())
            act.wait_ge(*squared.at(n))
            for q, (lo, hi) in enumerate(groups):
                nc.scalar.activation(ss[:, q * TB:q * TB + TB], ss[:, q * TB:q * TB + TB], ACT.Sqrt, bias=k.eps[:, 0:1],
                                     scale=1.0 / (hi - lo)).then_inc(*std_ready.inc())

        @block.vector
        def _(dve):
            dve.wait_ge(*std_ready.at(len(groups)))
            nc.vector.reciprocal(ss[:], ss[:]).then_inc(*inv_ready.inc())
            dve.wait_ge(*inv_ready.at(1))
            for q, (lo, hi) in enumerate(groups):
                for b in range(TB):
                    i = q * TB + b
                    nc.vector.tensor_scalar(y[:, b, lo:hi], y[:, b, lo:hi], ss[:, i:i + 1], None, ALU.mult).then_inc(*out.inc())


def short_conv_phase(k, z, out, gain):
    nc = k.nc
    with nc.sbuf_tensor(k.unique("cvz"), [P, 2, S], F32) as cz, nc.sbuf_tensor(k.unique("cvy"), [P, 2, S], F32) as cy, \
            ExitStack():
        cw = k.vec("conv_w").rearrange("p (t n) -> p t n", t=3)
        k.phase()
        steps = k.sem("conv_steps")
        with nc.Block() as block:
            @block.vector
            def _(dve):
                nc.vector.tensor_tensor(cz[:], z[:, 2:4, :], z[:, 4:6, :], ALU.mult).then_inc(*steps.inc())
                dve.wait_ge(*steps.at(1))
                for c in range(2):
                    nc.vector.tensor_scalar(cy[:, c, :], cz[:, c, :], cw[:, 2, c:c + 1], None, ALU.mult).then_inc(*steps.inc())
                dve.wait_ge(*steps.at(3))
                for tap in (1, 0):
                    for c in range(2):
                        n = S - 2 + tap
                        nc.vector.scalar_tensor_tensor(out=cy[:, c, S - n:S], in0=cz[:, c, 0:n], scalar=cw[:, tap, c:c + 1],
                                                       in1=cy[:, c, S - n:S], op0=ALU.mult, op1=ALU.add).then_inc(*steps.inc())
                    dve.wait_ge(*steps.at(5 if tap else 7))
                nc.vector.tensor_tensor(cy[:], cy[:], z[:, 0:2, :], ALU.mult).then_inc(*steps.inc())
        norm_phase(k, cy, out, gain, kt=2, width=CW)


def shift_phase(k, z, mu):
    nc = k.nc
    k.phase()
    diff, out = k.sem("shift_diff"), k.sem("shift_out")
    with nc.sbuf_tensor(k.unique("dz"), [P, 2, S], F32) as dz, nc.Block() as block:
        @block.gpsimd
        def _(pool):
            for i in range(11):
                if i >= 2:
                    pool.wait_ge(*out.at(i - 1))
                nc.gpsimd.tensor_tensor(dz[:, i % 2, :], z[:, i, 0:S], z[:, i, 1:S + 1], ALU.subtract).then_inc(*diff.inc())

        @block.vector
        def _(dve):
            for i in range(11):
                dve.wait_ge(*diff.at(i + 1))
                nc.vector.scalar_tensor_tensor(out=z[:, i, 1:S + 1], in0=dz[:, i % 2, :], scalar=mu[:, i:i + 1],
                                               in1=z[:, i, 1:S + 1], op0=ALU.mult, op1=ALU.add).then_inc(*out.inc())


def rwkv_phases(k, z, out, spare):
    nc, io = k.nc, k.io
    ctx = ExitStack()
    with ctx:
        def sb(name, shape):
            return ctx.enter_context(nc.sbuf_tensor(k.unique("rw_" + name), shape, F32))

        kr = sb("kr", [P, 3, 2, S])
        lam = sb("lam", [P, 3, TB, 2])
        tm = sb("tm", [P, TB, 4, RW])
        bonus = sb("bonus", [P, TB, 6])
        gate = sb("gate", [P, TB, RW])
        bh, kh = sb("bh", [P, 3 * S]), sb("kh", [P, 3 * S])
        bhat, khat = (t[:].rearrange("p (i t) -> p i t", t=S) for t in (bh, kh))
        A = z[:].rearrange("p i t -> p (i t)")[:, 0:24 * P].rearrange("p (q t) -> p q t", t=P)
        rwkv_prepare(k, z, kr, bhat, khat, lam, bonus, gate)
        with ExitStack() as products:
            banks = []
            for n, src in enumerate((kr[:, :, 0, :], bhat, khat, z[:, 6:9, 1:S + 1])):
                for i in range(3):
                    banks.append(([src[:, i, P * b:P * b + P] for b in range(TB)], tm[:, :, n, P * i:P * i + P]))
            turn_phase(k, banks)
            AT = products.enter_context(nc.sbuf_tensor(k.unique("rw_AT"), [P, 24, 3, P], F32))
            yx = products.enter_context(nc.sbuf_tensor(k.unique("rw_yx"), [P, 24, 2, P], F32))
            k.phase()
            made, masked = k.sem("rw_made"), k.sem("rw_masked")
            with nc.Block() as block:
                @block.tensor
                def _(pe):
                    for q in range(24):
                        h, b = q // 4, q % 4
                        i, p = h // 2, HD * (h % 2)
                        rows, cols = slice(p, p + HD), slice(P * b, P * b + P)
                        if q >= 2:
                            pe.wait_ge(*masked.at(3 * (q - 1)))
                        bank = k.pl[:, 2 * (q % 2), :]
                        nc.tensor.matmul(bank[:, 0:2 * P].rearrange("p (a b) -> p a b", a=2), bhat[rows, i, cols], kr[rows, i, :, cols], start=True, stop=True)
                        nc.tensor.matmul(bank[:, 2 * P:4 * P].rearrange("p (a b) -> p a b", a=2), khat[rows, i, cols], kr[rows, i, :, cols], start=True, stop=True)
                        nc.tensor.matmul(k.pl[:, 2 * (q % 2) + 1, 0:P], kr[rows, i, 0, cols], bhat[rows, i, cols], start=True, stop=True)\
                            .then_inc(*made.inc())

                @block.vector
                def _(dve):
                    for q in range(24):
                        dve.wait_ge(*made.at(q + 1))
                        nc.vector.tensor_tensor(AT[:, q].rearrange("p a b -> p (a b)"), k.pl[:, 2 * (q % 2), P:4 * P], k.const("chunkmask"), ALU.mult)\
                            .then_inc(*masked.inc())
                        nc.vector.tensor_tensor(yx[:, q, 0], k.pl[:, 2 * (q % 2), 0:P], k.const("join1"), ALU.mult).then_inc(*masked.inc())
                        nc.vector.tensor_tensor(A[:, q], k.pl[:, 2 * (q % 2) + 1, 0:P], k.const("below"), ALU.mult).then_inc(*masked.inc())

            invert_phase(k, A, yx, bh[:, 0:8 * P].rearrange("p (a b c) -> p a b c", a=2, b=4))
            wT = z[:].rearrange("p i t -> p (i t)")[:, 24 * P:24 * P + 3 * S].rearrange("p (i t) -> p i t", t=S)
            u = spare.rearrange("p i t -> p (i t)").rearrange("p (b f) -> p b f", f=RW)
            av = bh[:].rearrange("p (b f) -> p b f", f=RW)
            k.phase()
            w_made, w_out, av_made, av_out, u_made, u_out = (k.sem(s) for s in ("rw_w_made", "rw_w_out", "rw_av_made", "rw_av_out", "rw_u_made", "rw_u_out"))
            with nc.Block() as block:
                @block.tensor
                def _(pe):
                    for b in range(TB):
                        if b:
                            pe.wait_ge(*w_out.at(b))
                            pe.wait_ge(*av_out.at(b))
                            pe.wait_ge(*u_out.at(b))
                        for h in range(6):
                            q, i, p = 4 * h + b, h // 2, HD * (h % 2)
                            m = nc.tensor.matmul(k.pl[p:p + HD, 0, P * i:P * i + P], tm[:, b, 0, HD * h:HD * h + HD], yx[:, q, 0, :], start=True, stop=True)
                        m.then_inc(*w_made.inc())
                        for h in range(6):
                            q = 4 * h + b
                            m = nc.tensor.matmul(k.pl[:, 1, HD * h:HD * h + HD], AT[:, q, 1, :], tm[:, b, 3, HD * h:HD * h + HD], start=True, stop=True)
                        m.then_inc(*av_made.inc())
                        pe.wait_ge(*av_out.at(b + 1))
                        for h in range(6):
                            q = 4 * h + b
                            m = nc.tensor.matmul(k.pl[:, 2, HD * h:HD * h + HD], yx[:, q, 0, :], av[:, b, HD * h:HD * h + HD], start=True, stop=True)
                        m.then_inc(*u_made.inc())

                @block.scalar
                def _(act):
                    for b in range(TB):
                        act.wait_ge(*w_made.at(b + 1))
                        nc.scalar.activation(wT[:, :, P * b:P * b + P], k.pl[:, 0, 0:3 * P].rearrange("p (i t) -> p i t", i=3), ACT.Copy).then_inc(*w_out.inc())
                        act.wait_ge(*u_made.at(b + 1))
                        nc.scalar.activation(u[:, b, :], k.pl[:, 2, 0:RW], ACT.Copy).then_inc(*u_out.inc())

                @block.vector
                def _(dve):
                    for b in range(TB):
                        dve.wait_ge(*av_made.at(b + 1))
                        nc.vector.tensor_copy(av[:, b, :], k.pl[:, 1, 0:RW]).then_inc(*av_out.inc())

            sa = kh[:, 0:2 * RW].rearrange("p (b f) -> p b f", f=RW)
            st = kh[:, 2 * RW:3 * RW].rearrange("p (b i v) -> p b i v", b=2, v=HD)
            tmp = kh[:, 3 * RW:4 * RW].rearrange("p (b i v) -> p b i v", b=2, v=HD)
            k.phase()
            ws_made, sa_ready, st_made, st_ready, o_made, o_out = (k.sem(s) for s in ("rw_ws_made", "rw_sa_ready", "rw_st_made", "rw_st_ready", "rw_o_made", "rw_o_out"))
            st_sum, zeroed = k.sem("rw_st_sum"), k.sem("rw_zeroed")
            with nc.Block() as block:
                @block.tensor
                def _(pe):
                    for b in range(TB):
                        cur = st[:, b % 2]
                        if b == 0:
                            pe.wait_ge(*zeroed.at(1))
                        else:
                            pe.wait_ge(*st_ready.at(b))
                        cols = slice(P * b, P * b + P)
                        for h in (0, 2, 4, 1, 3, 5):
                            i, p = h // 2, HD * (h % 2)
                            m = nc.tensor.matmul(k.pl[:, h % 2, HD * i:HD * i + HD], wT[p:p + HD, i, cols], cur[p:p + HD, i, :], start=True, stop=True)
                        m.then_inc(*ws_made.inc())
                        pe.wait_ge(*sa_ready.at(2 * b + 2))
                        if b < TB - 1:
                            for h in range(6):
                                i, p, hc = h // 2, HD * (h % 2), slice(HD * h, HD * h + HD)
                                nc.tensor.matmul(k.pl[p:p + HD, 2, HD * i:HD * i + HD], tm[:, b, 2, hc], tm[:, b, 3, hc], start=True, stop=False)
                                m = nc.tensor.matmul(k.pl[p:p + HD, 2, HD * i:HD * i + HD], tm[:, b, 1, hc], sa[:, b % 2, hc], start=False, stop=True)
                            m.then_inc(*st_made.inc())
                        if b:
                            pe.wait_ge(*o_out.at(2 * b))
                        for h in (0, 2, 4, 1, 3, 5):
                            i, p, hc, q = h // 2, HD * (h % 2), slice(HD * h, HD * h + HD), 4 * h + b
                            o = k.pm[:, h % 2, HD * i:HD * i + HD]
                            nc.tensor.matmul(o, kr[p:p + HD, i, 1, cols], cur[p:p + HD, i, :], start=True, stop=False)
                            nc.tensor.matmul(o, AT[:, q, 0, :], sa[:, b % 2, hc], start=False, stop=False)
                            m = nc.tensor.matmul(o, AT[:, q, 2, :], tm[:, b, 3, hc], start=False, stop=True)
                        m.then_inc(*o_made.inc())

                def halves(t, b):
                    return t[:, b, :].rearrange("p (i e v) -> p e i v", e=2, v=HD)

                @block.vector
                def _(dve):
                    nc.vector.memset(st[:, 0], 0.0).then_inc(*zeroed.inc())
                    dve.wait_ge(*zeroed.at(1))
                    for b in range(TB):
                        dve.wait_ge(*ws_made.at(b + 1))
                        if b >= 2:
                            dve.wait_ge(*o_made.at(b - 1))
                        for e in range(2):
                            nc.vector.scalar_tensor_tensor(out=halves(sa, b % 2)[:, e], in0=k.pl[:, e, 0:3 * HD].rearrange("p (i v) -> p i v", v=HD),
                                                           scalar=-1.0, in1=halves(u, b)[:, e], op0=ALU.mult, op1=ALU.subtract)\
                                .then_inc(*sa_ready.inc())
                        if b < TB - 1:
                            dve.wait_ge(*st_made.at(b + 1))
                            if b:
                                dve.wait_ge(*o_made.at(b))
                            nc.vector.tensor_tensor(tmp[:, 0], st[:, b % 2], k.pl[:, 2, 0:3 * HD].rearrange("p (i v) -> p i v", v=HD), ALU.add).then_inc(*st_sum.inc())
                            dve.wait_ge(*st_sum.at(2 * b + 1))
                            nc.vector.tensor_tensor(tmp[:, 1], tmp[:, 0], lam[:, :, b, 1].unsqueeze(2).broadcast_to([P, 3, HD]), ALU.mult).then_inc(*st_sum.inc())
                            dve.wait_ge(*st_sum.at(2 * b + 2))
                            nc.vector.tensor_tensor(st[:, (b + 1) % 2], tmp[:, 1], lam[:, :, b + 1, 0].unsqueeze(2).broadcast_to([P, 3, HD]), ALU.mult).then_inc(*st_ready.inc())

                @block.scalar
                def _(act):
                    for b in range(TB):
                        act.wait_ge(*o_made.at(b + 1))
                        for e in range(2):
                            nc.scalar.activation(halves(out, b)[:, e], k.pm[:, e, 0:3 * HD].rearrange("p (i v) -> p i v", v=HD), ACT.Copy).then_inc(*o_out.inc())
        rwkv_finish(k, out, tm, bonus, gate)


def rwkv_prepare(k, z, kr, bh, kh, lam, bonus, gate):
    nc, io = k.nc, k.io
    ctx = ExitStack()
    with ctx:
        def sb(name, shape):
            return ctx.enter_context(nc.sbuf_tensor(k.unique("rp_" + name), shape, F32))
        w2a2 = sb("w2a2", [P, RW])
        g2 = sb("g2", [P, RW])
        vec = k.vec("rw_w0_2", 15).rearrange("p (n i) -> p n i", i=3)
        la = sb("la", [P, S])
        gl = sb("gl", [P, S])
        ld = sb("ld", [P, 3, S])
        L = sb("L", [P, 3, S])
        a = sb("a", [P, 3, S])
        kk = sb("kk", [P, 3, S])
        e = sb("e", [P, 3, S])
        t1 = sb("t1", [P, 3, S])
        k.phase()
        loaded, lora, gates_made, sig, scan = (k.sem(s) for s in ("rp_loaded", "rp_lora", "rp_made", "rp_sig", "rp_scan"))
        step, astep, pstep = k.sem("rp_step"), k.sem("rp_act_step"), k.sem("rp_pe_step")
        r, kz = z[:, 0:3, 1:S + 1], z[:, 3:6, 1:S + 1]
        with nc.Block() as block:
            @block.sync
            def _(sp):
                sp.dma_start(w2a2[0:64], io["rw_w2_2"][0]).then_inc(*loaded.dma())
                sp.dma_start(w2a2[64:128], io["rw_a2_2"][0]).then_inc(*loaded.dma())
                sp.dma_start(g2[:], io["rw_g2_2"][0]).then_inc(*loaded.dma())

            @block.tensor
            def _(pe):
                pe.wait_ge(*loaded.dma_at(3))
                pe.wait_ge(*lora.at(2))
                for i in range(3):
                    nc.tensor.matmul(k.pl[:, i, :], w2a2[0:64, P * i:P * i + P], la[0:64], start=True, stop=True)
                    m = nc.tensor.matmul(k.pm[:, i, :], w2a2[64:128, P * i:P * i + P], la[64:128], start=True, stop=True)
                m.then_inc(*gates_made.inc())
                pe.wait_ge(*sig.at(6))
                pe.wait_ge(*step.at(4))
                for i in range(3):
                    m = nc.tensor.matmul(k.pl[:, i, :], k.const("headsum"), t1[:, i, :], start=True, stop=True)
                m.then_inc(*pstep.inc())
                pe.wait_ge(*lora.at(3))
                for b in range(TB):
                    m = nc.tensor.matmul(k.pm[:, b, 0:RW], gl[:, P * b:P * b + P], g2[:], start=True, stop=True)
                m.then_inc(*pstep.inc())
                pe.wait_ge(*astep.at(7))
                pe.wait_ge(*step.at(16))
                for i in range(3):
                    for b in range(TB):
                        m = nc.tensor.matmul(k.pm[:, 0, 6 * b + 2 * i:6 * b + 2 * i + 2], t1[:, i, P * b:P * b + P], k.const("headcol"), start=True, stop=True)
                m.then_inc(*pstep.inc())

            @block.scalar
            def _(act):
                nc.scalar.activation(la[0:64], z[0:64, 9, 1:S + 1], ACT.Tanh).then_inc(*lora.inc())
                nc.scalar.activation(la[64:128], z[64:128, 9, 1:S + 1], ACT.Copy).then_inc(*lora.inc())
                nc.scalar.activation(gl[:], z[:, 10, 1:S + 1], ACT.Sigmoid).then_inc(*lora.inc())
                act.wait_ge(*gates_made.at(1))
                for i in range(3):
                    nc.scalar.activation(ld[:, i, :], k.pl[:, i, :], ACT.Sigmoid, bias=vec[:, 0, i:i + 1]).then_inc(*sig.inc())
                for i in range(3):
                    nc.scalar.activation(a[:, i, :], k.pm[:, i, :], ACT.Sigmoid, bias=vec[:, 1, i:i + 1]).then_inc(*sig.inc())
                act.wait_ge(*pstep.at(1))
                act.wait_ge(*step.at(4))
                nc.scalar.activation(t1[:], k.pl[:, 0:3, :], ACT.Sqrt).then_inc(*astep.inc())
                act.wait_ge(*k.sem("rp_L").at(2))
                act.wait_ge(*k.sem("rp_kk").at(1))
                nc.scalar.activation(e[:], L[:], ACT.Exp).then_inc(*astep.inc())
                act.wait_ge(*k.sem("rp_use").at(1))
                nc.scalar.activation(e[:], L[:], ACT.Exp, scale=-1.0).then_inc(*astep.inc())
                act.wait_ge(*k.sem("rp_prev").at(1))
                nc.scalar.activation(t1[:], t1[:], ACT.Exp).then_inc(*astep.inc())
                act.wait_ge(*k.sem("rp_L").at(3))
                nc.scalar.activation(lam[:], lam[:], ACT.Exp).then_inc(*astep.inc())
                act.wait_ge(*pstep.at(2))
                nc.scalar.activation(gate[:, 0:2, :], k.pm[:, 0:2, 0:RW], ACT.Copy).then_inc(*astep.inc())
                nc.scalar.activation(gate[:, 2:4, :], k.pm[:, 2:4, 0:RW], ACT.Copy).then_inc(*astep.inc())
                act.wait_ge(*pstep.at(3))
                nc.scalar.activation(bonus[:].rearrange("p b h -> p (b h)"), k.pm[:, 0, 0:24], ACT.Copy).then_inc(*astep.inc())

            @block.vector
            def _(dve):
                DEC = -float(np.exp(-0.5))
                for i in range(3):
                    nc.vector.tensor_scalar(kk[:, i, :], kz[:, i, :], vec[:, 2, i:i + 1], None, ALU.mult).then_inc(*step.inc())
                dve.wait_ge(*step.at(3))
                nc.vector.tensor_tensor(t1[:], kk[:], kk[:], ALU.mult).then_inc(*step.inc())
                dve.wait_ge(*sig.at(6))
                nc.vector.tensor_scalar(ld[:], ld[:], DEC, None, ALU.mult).then_inc(*scan.inc())
                dve.wait_ge(*scan.at(1))
                for i in range(3):
                    nc.vector.tensor_tensor_scan(L[:, i, :], k.const("first"), ld[:, i, :], 0.0, ALU.mult, ALU.add).then_inc(*scan.inc())
                dve.wait_ge(*scan.at(4))
                Lc = L[:].rearrange("p i (b t) -> p (i b) t", t=P)
                lm = lam[:].rearrange("p i b e -> p (i b) e")
                nc.vector.tensor_copy(lm[:, :, 0], Lc[:, :, P // 2]).then_inc(*k.sem("rp_L").inc())
                dve.wait_ge(*k.sem("rp_L").at(1))
                nc.vector.tensor_tensor(Lc, Lc, lm[:, :, 0:1].broadcast_to([P, 12, P]), ALU.subtract).then_inc(*k.sem("rp_L").inc())
                dve.wait_ge(*astep.at(1))
                nc.vector.tensor_scalar(t1[:], t1[:], 1e-12, None, ALU.max).then_inc(*step.inc())
                dve.wait_ge(*step.at(5))
                nc.vector.reciprocal(t1[:], t1[:]).then_inc(*step.inc())
                dve.wait_ge(*step.at(6))
                nc.vector.tensor_tensor(kk[:], kk[:], t1[:], ALU.mult).then_inc(*k.sem("rp_kk").inc())
                dve.wait_ge(*k.sem("rp_kk").at(1))
                dve.wait_ge(*k.sem("rp_L").at(2))
                nc.vector.tensor_tensor(t1[:], L[:], ld[:], ALU.subtract).then_inc(*k.sem("rp_prev").inc())
                nc.vector.tensor_copy(lm[:, :, 1], Lc[:, :, P - 1]).then_inc(*k.sem("rp_L").inc())
                dve.wait_ge(*k.sem("rp_L").at(3))
                dve.wait_ge(*astep.at(2))
                nc.vector.tensor_tensor(kr[:, :, 1, :], r, e[:], ALU.mult).then_inc(*k.sem("rp_use").inc())
                for i in range(3):
                    nc.vector.tensor_scalar(kh[:, i, :], a[:, i, :], -1.0, vec[:, 3, i:i + 1], ALU.add, ALU.mult).then_inc(*step.inc())
                dve.wait_ge(*step.at(9))
                nc.vector.scalar_tensor_tensor(out=kh[:], in0=kh[:], scalar=1.0, in1=kz, op0=ALU.add, op1=ALU.mult).then_inc(*step.inc())
                nc.vector.tensor_tensor(bh[:], kk[:], a[:], ALU.mult).then_inc(*step.inc())
                dve.wait_ge(*step.at(11))
                dve.wait_ge(*astep.at(4))
                nc.vector.tensor_tensor(kr[:, :, 0, :], kk[:], t1[:], ALU.mult).then_inc(*step.inc())
                nc.vector.tensor_tensor(bh[:], bh[:], e[:], ALU.mult).then_inc(*step.inc())
                dve.wait_ge(*step.at(12))
                for i in range(3):
                    nc.vector.scalar_tensor_tensor(out=t1[:, i, :], in0=r[:, i, :], scalar=vec[:, 4, i:i + 1], in1=kh[:, i, :],
                                                   op0=ALU.mult, op1=ALU.mult).then_inc(*step.inc())
                dve.wait_ge(*step.at(16))
                nc.vector.tensor_tensor(kh[:], kh[:], e[:], ALU.mult).then_inc(*step.inc())


def invert_phase(k, A, yx, tt):
    nc = k.nc
    k.phase()
    first, t_made, t_out, p_made, joined = (k.sem(s) for s in ("inv_first", "inv_t_made", "inv_t_out", "inv_p_made", "inv_joined"))
    with nc.Block() as block:
        sizes = [2, 4, 8, 16, 32, 64]
        rounds = [(b, g) for b in sizes for g in range(6)]

        def batch(t, g):
            return t[:, 4 * g:4 * g + 4]

        @block.vector
        def _(dve):
            j1t = k.const("join1T").unsqueeze(1).broadcast_to([P, 4, P])
            idb = k.ident.unsqueeze(1).broadcast_to([P, 4, P])
            for g in range(6):
                nc.vector.tensor_tensor(batch(yx, g)[:, :, 1], batch(A, g), j1t, ALU.mult).then_inc(*first.inc())
            for g in range(6):
                dve.wait_ge(*first.at(g + 1))
                for e in range(2):
                    nc.vector.tensor_tensor(batch(yx, g)[:, :, e], idb, batch(yx, g)[:, :, e], ALU.subtract).then_inc(*joined.inc())

            def out_t(n):
                b, g = rounds[n]
                dve.wait_ge(*t_made.at(n + 1))
                if n >= 2:
                    dve.wait_ge(*p_made.at(n - 1))
                m = k.const(f"join{b}").unsqueeze(1).broadcast_to([P, 4, P])
                nc.vector.tensor_tensor(tt[:, n % 2], k.pm[:, n % 2, :].rearrange("p (a b) -> p a b", a=4), m, ALU.mult).then_inc(*t_out.inc())

            def out_p(n):
                b, g = rounds[n]
                dve.wait_ge(*p_made.at(n + 1))
                v = batch(yx, g).rearrange("p (h a) e b -> p h a e b", h=2)
                nc.vector.tensor_tensor(batch(yx, g), batch(yx, g), k.pl[:, 2 * (n % 2):2 * (n % 2) + 2, :].rearrange("p h (a e b) -> p (h a) e b", e=2, a=2), ALU.subtract).then_inc(*joined.inc())

            for n in range(len(rounds) + 1):
                if n < len(rounds):
                    out_t(n)
                if n:
                    out_p(n - 1)

        @block.tensor
        def _(pe):
            def first_product(n):
                b, g = rounds[n]
                pe.wait_ge(*joined.at(2 * g + 2 if b == 2 else 12 + n - 6 + 1))
                if n >= 2:
                    pe.wait_ge(*t_out.at(n - 1))
                for a in range(4):
                    q = 4 * g + a
                    m = nc.tensor.matmul(k.pm[:, n % 2, P * a:P * a + P], A[:, q], yx[:, q, 0], start=True, stop=True)
                m.then_inc(*t_made.inc())

            def second_product(n):
                b, g = rounds[n]
                pe.wait_ge(*t_out.at(n + 1))
                if n >= 2:
                    pe.wait_ge(*joined.at(12 + n - 1))
                for a in range(4):
                    q = 4 * g + a
                    bank = k.pl[:, 2 * (n % 2) + a // 2, :]
                    at = 2 * P * (a % 2)
                    nc.tensor.matmul(bank[:, at:at + P], yx[:, q, 1], tt[:, n % 2, a], start=True, stop=True)
                    m = nc.tensor.matmul(bank[:, at + P:at + 2 * P], tt[:, n % 2, a], yx[:, q, 1], start=True, stop=True)
                m.then_inc(*p_made.inc())

            for n in range(len(rounds) + 1):
                if n < len(rounds):
                    first_product(n)
                if n:
                    second_product(n - 1)


def rwkv_finish(k, o, tm, bonus, gate):
    nc, io = k.nc, k.io
    ctx = ExitStack()
    with ctx:
        gw = ctx.enter_context(nc.sbuf_tensor(k.unique("rf_gw"), [P, 2, RW], F32))
        sq = ctx.enter_context(nc.sbuf_tensor(k.unique("rf_sq"), [P, TB * 6, HD], F32))
        mean = ctx.enter_context(nc.sbuf_tensor(k.unique("rf_mean"), [P, 2, TB * 6], F32))
        k.phase()
        loaded, step, std = k.sem("rf_loaded"), k.sem("rf_step"), k.sem("rf_std")
        with nc.Block() as block:
            @block.sync
            def _(sp):
                for n, name in enumerate(("rw_gn_w_2", "rw_gn_b_2")):
                    sp.dma_start(gw[:, n, :], io[name].broadcast_to([P, RW])).then_inc(*loaded.dma())

            oh = o[:].rearrange("p b (h v) -> p (b h) v", v=HD)

            def per_head(t):
                return t.unsqueeze(2).broadcast_to([P, TB * 6, HD])

            def per_channel(n):
                return gw[:, n, :].unsqueeze(1).broadcast_to([P, TB, RW])

            @block.vector
            def _(dve):
                def step_done(i):
                    i.then_inc(*step.inc())
                    dve.wait_ge(*step.at(step.total - step.base))
                dve.wait_ge(*loaded.dma_at(2))
                step_done(nc.vector.tensor_reduce(mean[:, 0, :], oh, AX_X, ALU.add))
                step_done(nc.vector.tensor_scalar(mean[:, 0, :], mean[:, 0, :], 1.0 / HD, None, ALU.mult))
                step_done(nc.vector.tensor_tensor(oh, oh, per_head(mean[:, 0, :]), ALU.subtract))
                step_done(nc.vector.tensor_tensor(sq[:], oh, oh, ALU.mult))
                step_done(nc.vector.tensor_reduce(mean[:, 1, :], sq[:], AX_X, ALU.add))
                dve.wait_ge(*std.at(1))
                step_done(nc.vector.reciprocal(mean[:, 1, :], mean[:, 1, :]))
                step_done(nc.vector.tensor_tensor(oh, oh, per_head(mean[:, 1, :]), ALU.mult))
                step_done(nc.vector.tensor_tensor(o[:], o[:], per_channel(0), ALU.mult))
                step_done(nc.vector.tensor_tensor(o[:], o[:], per_channel(1), ALU.add))
                vh = tm[:, :, 3, :].rearrange("p b (h v) -> p b h v", v=HD)
                sqh = sq[:].rearrange("p (b h) v -> p b h v", b=TB)
                for b in range(TB):
                    step_done(nc.vector.tensor_tensor(sqh[:, b], vh[:, b], bonus[:, b, :].unsqueeze(2).broadcast_to([P, 6, HD]), ALU.mult))
                step_done(nc.vector.tensor_tensor(oh, oh, sq[:], ALU.add))
                step_done(nc.vector.tensor_tensor(o[:], o[:], gate[:], ALU.mult))

            @block.scalar
            def _(act):
                act.wait_ge(*step.at(5))
                nc.scalar.activation(mean[:, 1, :], mean[:, 1, :], ACT.Sqrt, bias=k.eps[:, 1:2], scale=1.0 / HD).then_inc(*std.inc())


def compress_phases(k, kc, vc, kcmp, vcmp):
    nc, io = k.nc, k.io
    with nc.sbuf_tensor(k.unique("cp_pe"), [P, CMP_LEN], F32) as pe_t, nc.sbuf_tensor(k.unique("cp_raw"), [CMP_LEN, 2, HD], F32) as raw, \
            nc.sbuf_tensor(k.unique("cp_w1"), [P, CMP_LEN, P], F32) as w1, nc.sbuf_tensor(k.unique("cp_w2"), [P, HD], F32) as w2, \
            nc.sbuf_tensor(k.unique("cp_win"), [P, CMP_LEN, NC], F32) as win, nc.sbuf_tensor(k.unique("cp_hid"), [P, 2, NC], F32) as hid:
        for x, name, last in ((kc, "k", False), (vc, "v", True)):
            k.phase()
            loaded, pe_turned, pe_out, windows, hid_made, hid_out, out_made, out = (k.sem("cp_" + s) for s in (
                "loaded", "pe_turned", "pe_out", "windows", "hid_made", "hid_out", "out_made", "out"))
            with nc.Block() as block:
                @block.sync
                def _(sp):
                    w = io[f"cmp_w1_{name}_2"][0].rearrange("(l d) n -> d l n", d=HD)
                    for g in range(2):
                        sp.dma_start(raw[:, g, :], io[f"cmp_pe_{name}_2"][0]).then_inc(*loaded.dma())
                        sp.dma_start(w1[HD * g:HD * g + HD], w).then_inc(*loaded.dma())
                    sp.dma_start(w2[:], io[f"cmp_w2_{name}_2"][0]).then_inc(*loaded.dma())

                @block.tensor
                def _(pe):
                    pe.wait_ge(*loaded.dma_at(5))
                    nc.tensor.transpose(k.pm[:, 2, 0:CMP_LEN], raw[:].rearrange("p g d -> p (g d)"), k.ident[0:CMP_LEN, 0:CMP_LEN]).then_inc(*pe_turned.inc())
                    pe.wait_ge(*windows.at(1))
                    for g in range(2):
                        for l in range(CMP_LEN):
                            m = nc.tensor.matmul(k.pm[:, g, 0:NC], w1[HD * g:HD * g + HD, l, :], win[HD * g:HD * g + HD, l, :], start=l == 0, stop=l == CMP_LEN - 1)
                    m.then_inc(*hid_made.inc())
                    pe.wait_ge(*hid_out.at(1))
                    for g in range(2):
                        if last:
                            m = nc.tensor.matmul(k.pm[0:NC, 3, HD * g:HD * g + HD], hid[:, g, :], w2[:], start=True, stop=True)
                        else:
                            m = nc.tensor.matmul(k.pm[HD * g:HD * g + HD, 3, 0:NC], w2[:], hid[:, g, :], start=True, stop=True)
                    m.then_inc(*out_made.inc())

                @block.scalar
                def _(act):
                    act.wait_ge(*hid_made.at(1))
                    nc.scalar.activation(hid[:], k.pm[:, 0:2, 0:NC], ACT.Gelu_apprx_tanh).then_inc(*hid_out.inc())

                @block.vector
                def _(dve):
                    dve.wait_ge(*pe_turned.at(1))
                    nc.vector.tensor_copy(pe_t[:], k.pm[:, 2, 0:CMP_LEN]).then_inc(*pe_out.inc())
                    dve.wait_ge(*pe_out.at(1))
                    xs = x.rearrange("p (n s) -> p s n", s=CMP_STRIDE)
                    for half in range(2):
                        lo = CMP_STRIDE * half
                        i = nc.vector.tensor_tensor(win[:, lo:lo + CMP_STRIDE, :], xs[:, :, half:half + NC],
                                                    pe_t[:, lo:lo + CMP_STRIDE].unsqueeze(2).broadcast_to([P, CMP_STRIDE, NC]), ALU.add)
                    i.then_inc(*windows.inc())
                    dve.wait_ge(*out_made.at(1))
                    if last:
                        nc.vector.tensor_copy(vcmp[0:NC].rearrange("p g d -> p (g d)"), k.pm[0:NC, 3, 0:P]).then_inc(*out.inc())
                    else:
                        nc.vector.tensor_copy(kcmp, k.pm[:, 3, 0:NC]).then_inc(*out.inc())


def s5_phases(k, u, out):
    nc, io = k.nc, k.io
    ctx = ExitStack()
    with ctx:
        def sb(name, shape):
            return ctx.enter_context(nc.sbuf_tensor(k.unique("s5_" + name), shape, F32))
        par = sb("par", [P, 16, 8])
        scs = sb("sincos", [P, 2, 8])
        tmp = sb("tmp", [P, 2, 8])
        bt = sb("bt", [P, 2, 2, P])
        ct = sb("ct", [P, 2, 2, P])
        rot = sb("rot", [P, 2, 8, S])
        dsk = k.vec("s5_d_2")
        wg = sb("wglu", [P, 2, 2 * CW])
        step = k.sem("s5_step")
        with ExitStack() as c2:
            braw = c2.enter_context(nc.sbuf_tensor(k.unique("s5_braw"), [P, 2, 8, 16], F32))
            bx = c2.enter_context(nc.sbuf_tensor(k.unique("s5_bx"), [P, 2, 8, 2, 16], F32))
            craw = c2.enter_context(nc.sbuf_tensor(k.unique("s5_craw"), [P, 2, 2, 2, HD], F32))
            btmp = c2.enter_context(nc.sbuf_tensor(k.unique("s5_btmp"), [P, 2, 8, 16], F32))
            rt = c2.enter_context(nc.sbuf_tensor(k.unique("s5_rt"), [P, 4, 8, S // 2], F32))
            pw = c2.enter_context(nc.sbuf_tensor(k.unique("s5_pw"), [P, 2, 2, 8], F32))
            k.phase()
            loaded, sines, exps = k.sem("s5_loaded"), k.sem("s5_sines"), k.sem("s5_exps")
            turned, emptied = k.sem("s5_turned"), k.sem("s5_emptied")
            with nc.Block() as block:
                @block.sync
                def _(sp):
                    for g in range(2):
                        row = io["s5_log_dt_2"].rearrange("o (i g) -> g o i", g=2)[g]
                        sp.dma_start(par[HD * g:HD * g + HD, 2, :], row.broadcast_to([HD, 8]), allow_slow_non_contiguous=True)\
                            .then_inc(*loaded.dma())
                    for n, name in enumerate(("s5_b_re_2", "s5_b_im_2")):
                        for g in range(2):
                            sp.dma_start(braw[HD * g:HD * g + HD, n], io[name][0].rearrange("(i g) p c -> g p i c", g=2)[g]).then_inc(*loaded.dma())
                    for n, name in enumerate(("s5_c_re_2", "s5_c_im_2")):
                        for g in range(2):
                            sp.dma_start(craw[:, n, :, g, :], io[name][0].rearrange("(h q) c p -> (q c) h p", h=2)).then_inc(*loaded.dma())
                    sp.dma_start(wg[:], io["s5_w_glu_2"][0].rearrange("(h p) n -> p h n", p=P)).then_inc(*loaded.dma())

                marks = {}

                @block.vector
                def _(dve):
                    def st(i):
                        i.then_inc(*step.inc())
                        dve.wait_ge(*step.at(step.total - step.base))
                    V = nc.vector
                    M, Ad, Su = ALU.mult, ALU.add, ALU.subtract
                    def q(n):
                        return (k.vec("s5_lam_re_2"), k.vec("s5_lam_im_2"))[n] if n < 2 else par[:, n, :]
                    dve.wait_ge(*loaded.at(loaded.total - loaded.base))
                    dve.wait_ge(*exps.at(1))
                    st(V.tensor_tensor(q(4), q(1), q(2), M))
                    st(V.tensor_tensor(q(3), q(0), q(2), M))
                    marks["exp"] = step.total - step.base
                    sincos(k, dve, None, q(4), scs, tmp, step, None)
                    marks["sine"] = step.total - step.base
                    dve.wait_ge(*sines.at(2))
                    sn, cs = scs[:, 0], scs[:, 1]
                    st(V.tensor_tensor(q(5), q(3), cs, M))
                    st(V.tensor_tensor(q(6), q(3), sn, M))
                    st(V.tensor_tensor(q(7), q(0), q(0), M))
                    st(V.tensor_tensor(q(8), q(1), q(1), M))
                    st(V.tensor_tensor(q(7), q(7), q(8), Ad))
                    st(V.reciprocal(q(7), q(7)))
                    st(V.tensor_scalar(q(8), q(5), -1.0, None, Ad))
                    st(V.tensor_tensor(q(9), q(8), q(0), M))
                    st(V.tensor_tensor(q(10), q(6), q(1), M))
                    st(V.tensor_tensor(q(9), q(9), q(10), Ad))
                    st(V.tensor_tensor(q(9), q(9), q(7), M))
                    st(V.tensor_tensor(q(10), q(6), q(0), M))
                    st(V.tensor_tensor(q(11), q(8), q(1), M))
                    st(V.tensor_tensor(q(10), q(10), q(11), Su))
                    st(V.tensor_tensor(q(10), q(10), q(7), M))
                    def over_c(n):
                        return q(n).unsqueeze(2).broadcast_to([P, 8, 16])
                    st(V.memset(bx[:], 0.0))
                    for part in range(2):
                        st(V.tensor_tensor(btmp[:, 0], braw[:, part], over_c(9), M))
                        st(V.tensor_tensor(btmp[:, 1], braw[:, 1 - part], over_c(10), M))
                        for g in range(2):
                            r = slice(HD * g, HD * g + HD)
                            st(V.tensor_tensor(bx[r, part, :, g, :], btmp[r, 0], btmp[r, 1], Ad if part else Su))
                    for part in range(2):
                        for g in range(2):
                            st(V.tensor_scalar(craw[:, part, :, g, :], craw[:, part, :, g, :], k.const("pairsel")[:, g:g + 1],
                                               -1.0 if part else 1.0, M, M))
                    marks["bc"] = step.total - step.base
                    dve.wait_ge(*turned.at(1))
                    V.tensor_copy(bt[:], k.pm[:, 0, :].rearrange("p (a h s) -> p a h s", a=2, h=2)).then_inc(*emptied.inc())
                    V.tensor_copy(ct[:], k.pm[:, 1, :].rearrange("p (a h s) -> p a h s", a=2, h=2)).then_inc(*emptied.inc())
                    st(V.memset(rot[:, 0, :, 0:1], 1.0))
                    st(V.memset(rot[:, 1, :, 0:1], 0.0))
                    st(V.tensor_copy(pw[:, 0, 0], cs))
                    st(V.tensor_copy(pw[:, 0, 1], sn))
                    n, cur = 1, 0
                    while n < S:
                        pr = pw[:, cur, 0].unsqueeze(2).broadcast_to([P, 8, n])
                        pi = pw[:, cur, 1].unsqueeze(2).broadcast_to([P, 8, n])
                        c0, s0 = rot[:, 0, :, 0:n], rot[:, 1, :, 0:n]
                        V.tensor_tensor(rt[:, 0, :, 0:n], c0, pr, M).then_inc(*step.inc())
                        V.tensor_tensor(rt[:, 1, :, 0:n], s0, pi, M).then_inc(*step.inc())
                        V.tensor_tensor(rt[:, 2, :, 0:n], c0, pi, M).then_inc(*step.inc())
                        st(V.tensor_tensor(rt[:, 3, :, 0:n], s0, pr, M))
                        V.tensor_tensor(rot[:, 0, :, n:2 * n], rt[:, 0, :, 0:n], rt[:, 1, :, 0:n], Su).then_inc(*step.inc())
                        st(V.tensor_tensor(rot[:, 1, :, n:2 * n], rt[:, 2, :, 0:n], rt[:, 3, :, 0:n], Ad))
                        n *= 2
                        if n < S:
                            o = pw[:, cur]
                            V.tensor_tensor(rt[:, 0, :, 0], o[:, 0], o[:, 0], M).then_inc(*step.inc())
                            V.tensor_tensor(rt[:, 1, :, 0], o[:, 1], o[:, 1], M).then_inc(*step.inc())
                            st(V.scalar_tensor_tensor(out=pw[:, 1 - cur, 1], in0=o[:, 0], scalar=2.0, in1=o[:, 1], op0=M, op1=M))
                            st(V.tensor_tensor(pw[:, 1 - cur, 0], rt[:, 0, :, 0], rt[:, 1, :, 0], Su))
                            cur = 1 - cur

                @block.scalar
                def _(act):
                    act.wait_ge(*loaded.at(loaded.total - loaded.base))
                    nc.scalar.activation(par[:, 2, :], par[:, 2, :], ACT.Exp).then_inc(*exps.inc())
                    act.wait_ge(*step.at(marks["exp"]))
                    nc.scalar.activation(par[:, 3, :], par[:, 3, :], ACT.Exp).then_inc(*sines.inc())
                    act.wait_ge(*step.at(marks["sine"]))
                    nc.scalar.activation(scs[:], scs[:], ACT.Sin).then_inc(*sines.inc())

                @block.tensor
                def _(pe):
                    pe.wait_ge(*step.at(marks["bc"]))
                    for part in range(2):
                        for h in range(2):
                            at = P * (2 * part + h)
                            nc.tensor.transpose(k.pm[:, 0, at:at + P], bx[:, part, 4 * h:4 * h + 4].rearrange("p i g c -> p (i g c)"), k.ident)
                            m = nc.tensor.transpose(k.pm[:, 1, at:at + P], craw[:, part, h].rearrange("p g s -> p (g s)"), k.ident)
                    m.then_inc(*turned.inc())

        bu = sb("bu", [P, 4, S])
        w = sb("w", [P, 2, 2, S])
        sc = sb("scan", [P, 2, S])
        yg = sb("y", [P, 2, S])
        k.phase()
        made, prod, turned_in, scanned, prod2, state, read = (k.sem("s5_" + s) for s in (
            "made", "prod", "turned_in", "scanned", "prod2", "state", "read"))
        ysum, ygelu, glu_made, gate_ready, out_done = (k.sem("s5_" + s) for s in ("ysum", "ygelu", "glu_made", "gate_ready", "out_done"))
        with nc.Block() as block:
            @block.tensor
            def _(pe):
                def project(i):
                    h, r = i // 4, slice(32 * (i % 4), 32 * (i % 4) + 32)
                    if i >= 2:
                        pe.wait_ge(*prod.at(4 * (i - 1)))
                    for part in range(2):
                        m = nc.tensor.matmul(k.pl[:, 2 * (i % 2) + part, :], bt[r, part, h, :], u[r, h, :], start=True, stop=True)
                    m.then_inc(*made.inc())

                def mix(i):
                    h, r = i // 4, slice(32 * (i % 4), 32 * (i % 4) + 32)
                    pe.wait_ge(*state.at(2 * i + 2))
                    for part in range(2):
                        m = nc.tensor.matmul(k.pm[r, h, :], ct[:, part, h, r], w[:, i % 2, part, :], start=part == 0, stop=part == 1)
                    m.then_inc(*read.inc())
                for i in range(9):
                    if i < 8:
                        project(i)
                    if i:
                        mix(i - 1)
                pe.wait_ge(*ygelu.at(2))
                for c in range(4):
                    for h in range(2):
                        m = nc.tensor.matmul(k.pl[:, c, :], wg[:, h, P * c:P * c + P], yg[:, h, :], start=h == 0, stop=h == 1)
                m.then_inc(*glu_made.inc())

            @block.vector
            def _(dve):
                V, M, Ad, Su = nc.vector, ALU.mult, ALU.add, ALU.subtract
                for i in range(8):
                    c, s = rot[:, 0, i, :], rot[:, 1, i, :]
                    dve.wait_ge(*made.at(i + 1))
                    re, im = k.pl[:, 2 * (i % 2), :], k.pl[:, 2 * (i % 2) + 1, :]
                    if i:
                        dve.wait_ge(*state.at(2 * i))
                    V.tensor_tensor(bu[:, 0], re, c, M).then_inc(*prod.inc())
                    V.tensor_tensor(bu[:, 1], im, s, M).then_inc(*prod.inc())
                    V.tensor_tensor(bu[:, 2], im, c, M).then_inc(*prod.inc())
                    V.tensor_tensor(bu[:, 3], re, s, M).then_inc(*prod.inc())
                    dve.wait_ge(*prod.at(4 * i + 4))
                    if i >= 2:
                        dve.wait_ge(*read.at(i - 1))
                    V.tensor_tensor(w[:, i % 2, 0], bu[:, 0], bu[:, 1], Ad).then_inc(*turned_in.inc())
                    V.tensor_tensor(w[:, i % 2, 1], bu[:, 2], bu[:, 3], Su).then_inc(*turned_in.inc())
                    dve.wait_ge(*turned_in.at(2 * i + 2))
                    mag = par[:, 3, i:i + 1].broadcast_to([P, S])
                    for part in range(2):
                        V.tensor_tensor_scan(sc[:, part], mag, w[:, i % 2, part], 0.0, M, Ad).then_inc(*scanned.inc())
                    dve.wait_ge(*scanned.at(2 * i + 2))
                    V.tensor_tensor(bu[:, 0], sc[:, 0], c, M).then_inc(*prod2.inc())
                    V.tensor_tensor(bu[:, 1], sc[:, 1], s, M).then_inc(*prod2.inc())
                    V.tensor_tensor(bu[:, 2], sc[:, 0], s, M).then_inc(*prod2.inc())
                    V.tensor_tensor(bu[:, 3], sc[:, 1], c, M).then_inc(*prod2.inc())
                    dve.wait_ge(*prod2.at(4 * i + 4))
                    V.tensor_tensor(w[:, i % 2, 0], bu[:, 0], bu[:, 1], Su).then_inc(*state.inc())
                    V.tensor_tensor(w[:, i % 2, 1], bu[:, 2], bu[:, 3], Ad).then_inc(*state.inc())
                dve.wait_ge(*read.at(8))
                for h in range(2):
                    V.scalar_tensor_tensor(out=yg[:, h], in0=u[:, h, :], scalar=dsk[:, h:h + 1], in1=k.pm[:, h, :], op0=M, op1=Ad).then_inc(*ysum.inc())
                dve.wait_ge(*gate_ready.at(2))
                for h in range(2):
                    V.tensor_tensor(out[:, h, :], k.pl[:, h, :], sc[:, h], M).then_inc(*out_done.inc())

            @block.scalar
            def _(act):
                for h in range(2):
                    act.wait_ge(*ysum.at(h + 1))
                    nc.scalar.activation(yg[:, h], yg[:, h], ACT.Gelu_apprx_tanh).then_inc(*ygelu.inc())
                act.wait_ge(*glu_made.at(1))
                for h in range(2):
                    nc.scalar.activation(sc[:, h], k.pl[:, 2 + h, :], ACT.Sigmoid).then_inc(*gate_ready.inc())


def add_rms_gate_phase(k, g0, xT, hT, eT):
    nc = k.nc
    k.phase()
    gate_ready, prod_ready, added = k.sem("plg_gate"), k.sem("plg_prod"), k.sem("plg_added")
    with nc.sbuf_tensor(k.unique("plg"), [P, 2, 2, S], F32) as ga, nc.Block() as block:
        @block.sync
        def _(sp):
            for g in range(g0 + 2, g0 + 6):
                issue_slab(k, sp, g)

        @block.tensor
        def _(pe):
            for i in range(4):
                g = g0 + i
                j = g % 2
                pe.wait_ge(k.slab_loaded[j], loaded_value(g))
                if i >= 2:
                    pe.wait_ge(*gate_ready.at(i - 1))
                w = slab_view(k, g)
                for c in range(2):
                    for q in range(KD):
                        m = nc.tensor.matmul(k.pl[:, 2 * j + c, :], w[:, q, P * c:P * c + P], xT[:, q, :], start=q == 0, stop=q == KD - 1)
                m.then_inc(k.slab_done[j], 1)

        @block.scalar
        def _(act):
            for i in range(4):
                g = g0 + i
                j = g % 2
                act.wait_ge(k.slab_done[j], g // 2 + 1)
                if i >= 2:
                    act.wait_ge(*prod_ready.at(i - 1))
                nc.scalar.activation(ga[:, j], k.pl[:, 2 * j:2 * j + 2, :], ACT.Sigmoid).then_inc(*gate_ready.inc())

        @block.vector
        def _(dve):
            for i in range(4):
                dve.wait_ge(*gate_ready.at(i + 1))
                nc.vector.tensor_tensor(eT[:, 2 * i:2 * i + 2, :], eT[:, 2 * i:2 * i + 2, :], ga[:, (g0 + i) % 2], ALU.mult).then_inc(*prod_ready.inc())

        @block.gpsimd
        def _(pool):
            for i in range(4):
                pool.wait_ge(*prod_ready.at(i + 1))
                nc.gpsimd.tensor_tensor(hT[:, 2 * i:2 * i + 2, :], eT[:, 2 * i:2 * i + 2, :], xT[:, 2 * i:2 * i + 2, :], ALU.add).then_inc(*added.inc())


def two_blocks(nc, io, out, probe=None):
    def see(name, ap):
        if probe:
            probe(name, ap)
    ctx = ExitStack()
    with ctx:
        k = Kit(nc, ctx, io)

        def sb(name, shape, dt=F32):
            return ctx.enter_context(nc.sbuf_tensor(name, shape, dt))

        k.tables[0] = sb("table", [P, k.widths[0]])
        k.ring = sb("ring", [P, 2, SLAB])
        xT, hT = sb("xT", [P, KD, S]), sb("hT", [P, KD, S])
        k.eps = sb("eps", [P, 2])
        k.vecs = sb("vecs", [P, 3 * P])
        k.pl = ctx.enter_context(nc.psum_tensor("pl", [P, 4, 512], F32))
        k.pm = ctx.enter_context(nc.psum_tensor("pm", [P, 4, 512], F32))
        k.slab_loaded = [ctx.enter_context(nc.semaphore(f"slab_loaded{j}")) for j in range(2)]
        k.slab_done = [ctx.enter_context(nc.semaphore(f"slab_done{j}")) for j in range(2)]
        k.ones, k.ident = k.const("ones"), k.const("ident")
        G = {n: k.vec(n) for n in ("g_pre_mix", "g_mem", "g_post_mix", "g_pre_mlp", "g_post_mlp", "pre_mix_norm_2",
                                   "post_mix_norm_2", "pre_ffn_norm_2", "post_ffn_norm_2")}
        G["mix"] = k.vec("g_attn_out", KD)
        gple, mu = k.vec("ple_norm_2"), k.vec("shift_mu_2")

        k.phase()
        eps_set, consts_loaded, rows_turned, rows_out = (k.sem(s) for s in ("eps_set", "consts_loaded", "rows_turned", "rows_out"))
        with nc.sbuf_tensor(k.unique("rows"), [P, 3, P], F32) as rows, nc.Block() as block:
            @block.gpsimd
            def _(pool):
                nc.gpsimd.memset(k.eps[:, 0:1], EPS).then_inc(*eps_set.inc())
                nc.gpsimd.memset(k.eps[:, 1:2], GN_EPS).then_inc(*eps_set.inc())
                nc.gpsimd.memset(rows[:], 0.0).then_inc(*eps_set.inc())

            @block.sync
            def _(sp):
                sp.dma_start(k.tables[0][:], io["table"]).then_inc(*consts_loaded.dma())
                sp.wait_ge(*eps_set.at(3))
                for name, n in VECTORS:
                    at, flat = k.vec_at[name], io[name]
                    while len(flat.shape) > 1:
                        flat = flat.rearrange("a b -> (a b)") if len(flat.shape) == 2 else flat.rearrange("a b c -> (a b) c")
                    flat = flat.rearrange("(n p) -> n p", p=P)
                    done = 0
                    while done < n:
                        r, c = (at + done) % P, (at + done) // P
                        m = min(n - done, P - r)
                        sp.dma_start(rows[r:r + m, c, :], flat[done:done + m]).then_inc(*consts_loaded.dma())
                        done += m

            @block.tensor
            def _(pe):
                pe.wait_ge(*consts_loaded.at(consts_loaded.total - consts_loaded.base))
                for r in range(3):
                    m = nc.tensor.transpose(k.pm[:, 0, P * r:P * r + P], rows[:, r, :], k.ident)
                m.then_inc(*rows_turned.inc())

            @block.vector
            def _(dve):
                dve.wait_ge(*rows_turned.at(1))
                nc.vector.tensor_copy(k.vecs[:], k.pm[:, 0, 0:3 * P]).then_inc(*rows_out.inc())

        memT = None
        with nc.sbuf_tensor(k.unique("y"), [P, TB, AW + XW], F32) as y:
            with nc.sbuf_tensor(k.unique("qkv"), [P, TB, 3 * AW], F32) as qkv, nc.sbuf_tensor(k.unique("cz6"), [P, 6, S], F32) as cz6, \
                    nc.sbuf_tensor(k.unique("qx"), [P, 2, S], F32) as qx, nc.sbuf_tensor(k.unique("kx"), [P, 2, NM], F32) as kx, \
                    nc.sbuf_tensor(k.unique("vx"), [P, 2, XW], F32) as vx:
                with nc.sbuf_tensor(k.unique("memT"), [P, KD, NM], F32) as memT:
                    with nc.sbuf_tensor(k.unique("xin"), [P, TB, D], F32) as xin, nc.sbuf_tensor(k.unique("memin"), [P, 2, D], F32) as memin:
                        banks = [([xin[:, b, P * f:P * f + P] for b in range(TB)], xT[:, f, :]) for f in range(KD)]
                        banks += [([memin[:, b, P * f:P * f + P] for b in range(2)], memT[:, f, :]) for f in range(KD)]
                        turn_phase(k, banks, load=[(xin[:], io["x"][0].rearrange("(b p) d -> p b d", p=P)),
                                                   (memin[:], io["mem"][0].rearrange("(b p) d -> p b d", p=P))], stream=(0, 1))
                    norm_phase(k, xT, hT, G["g_pre_mix"])
                    norm_phase(k, memT, memT, G["g_mem"], n=NM)
                    slabs = [dict(kind="tokens", to=qkv[:, :, 256 * i:256 * i + 256]) for i in range(6)]
                    slabs += [dict(kind="features", to=lambda c, i=i: cz6[:, 2 * i + c, :]) for i in range(3)]
                    slabs += [dict(kind="features", to=lambda c: qx[:, c, :])]
                    slabs += [dict(kind="features", to=lambda c: kx[:, c, :], x=memT, tokens=NM)]
                    slabs += [dict(kind="tokens", to=vx, x=memT, tokens=NM)]
                    product_phase(k, IN1, slabs, x=hT)
                rope_phase(k, qkv)
                see("qkv", qkv[:].rearrange("p b f -> p (b f)"))
                with nc.sbuf_tensor(k.unique("qT"), [P, 8, S], F32) as qT:
                    turn_phase(k, [([qkv[:, b, P * f:P * f + P] for b in range(TB)], qT[:, f, :]) for f in range(8)])
                    units = []
                    for i in range(4):
                        for b in range(TB):
                            for e in range(2):
                                h, r, w = 2 * i + e, slice(HD * e, HD * e + HD), P * (b + 1)
                                units.append(dict(q=qT[r, i, P * b:P * b + P], k=qT[r, 4 + i, 0:w], mask=k.const("band")[:, S - w:S],
                                                  v=lambda a, h=h: qkv[:, a, 2 * AW + HD * h:2 * AW + HD * h + HD],
                                                  out=y[:, b, HD * h:HD * h + HD]))
                    for i in range(2):
                        for b in range(TB):
                            for e in range(2):
                                h, r = 2 * i + e, slice(HD * e, HD * e + HD)
                                units.append(dict(q=qx[r, i, P * b:P * b + P], k=kx[r, i, :], mask=k.const("nomask"),
                                                  v=lambda a, h=h: vx[:, a, HD * h:HD * h + HD],
                                                  out=y[:, b, AW + HD * h:AW + HD * h + HD]))
                    attend(k, units)
                see("y", y[:].rearrange("p b f -> p (b f)"))
                short_conv_phase(k, cz6, hT[:, 4:6, :], G["mix"][:, 4:6])
            head_norm_phase(k, y, [(0, AW), (AW, AW + XW)])
            banks = [([y[:, b, P * f:P * f + P] for b in range(TB)], hT[:, f if f < 4 else f + 2, :]) for f in range(6)]
            turn_phase(k, banks, gain=lambda b: G["mix"][:, (b if b < 4 else b + 2):(b if b < 4 else b + 2) + 1])
        see("mix", hT[:].rearrange("p b f -> p (b f)"))
        with nc.sbuf_tensor(k.unique("yT"), [P, KD, S], F32) as yT:
            def pairs_to(t, n):
                return [dict(kind="features", to=lambda c, i=i: t[:, 2 * i + c, :]) for i in range(n)]
            product_phase(k, WO1, pairs_to(yT, 4), x=hT)
            norm_phase(k, yT, None, G["g_post_mix"], add=xT, then=(hT, G["g_pre_mlp"]))
            see("x_mix", xT[:].rearrange("p b f -> p (b f)"))
            with nc.sbuf_tensor(k.unique("f"), [P, FF1 // P, S], F32) as f:
                up_phase(k, UP1, hT, f)
                down_phase(k, DN1, f, yT, 4, 32, None)
            norm_phase(k, yT, None, G["g_post_mlp"], add=xT, then=(hT, G["pre_mix_norm_2"]))
            see("x_1", xT[:].rearrange("p b f -> p (b f)"))

        with nc.sbuf_tensor(k.unique("z"), [P, 11, S + 1], F32) as z:
            with nc.sbuf_tensor(k.unique("q2"), [P, 3, S], F32) as q2, nc.sbuf_tensor(k.unique("kv2"), [P, 4, S], F32) as kv2, \
                    nc.sbuf_tensor(k.unique("v2"), [P, TB, 256], F32) as v2, nc.sbuf_tensor(k.unique("u5"), [P, 2, S], F32) as u5, \
                    nc.sbuf_tensor(k.unique("gl2"), [P, TB, 18], F32) as gl2:
                tiles = [z[:, n, 1:S + 1] for n in range(11)] + [q2[:, n, :] for n in range(3)] + [kv2[:, n, :] for n in range(4)]
                slabs = [dict(kind="features", to=lambda c, i=i: tiles[2 * i + c]) for i in range(9)]
                slabs += [dict(kind="tokens", to=v2)]
                slabs += [dict(kind="features", to=lambda c: u5[:, c, :])]
                slabs += [dict(kind="tokens", to=gl2, width=18)]
                k.phase()
                zeroed = k.sem("z_zeroed")
                with nc.Block() as block:
                    @block.gpsimd
                    def _(pool):
                        nc.gpsimd.memset(z[:, :, 0:1], 0.0).then_inc(*zeroed.inc())
                product_phase(k, IN2, slabs, x=hT)
                shift_phase(k, z, mu)
                see("z", z[:].rearrange("p b f -> p (b f)"))
                s5_phases(k, u5, hT[:, 6:8, :])
                see("s5", hT[:, 6:8, :].rearrange("p b f -> p (b f)"))
                with nc.sbuf_tensor(k.unique("kcmp"), [P, NC], F32) as kcmp, nc.sbuf_tensor(k.unique("vcmp"), [NC, 2, HD], F32) as vcmp, \
                        nc.sbuf_tensor(k.unique("y2"), [P, TB, RW], F32) as y2, \
                        nc.sbuf_tensor(k.unique("nsa_table"), [P, k.widths[1]], F32) as k.tables[1]:
                    compress_phases(k, kv2[:, 0, :], kv2[:, 1, :], kcmp[:], vcmp)
                    k.phase()
                    sig, cut, table_loaded = k.sem("nsa_gate"), k.sem("nsa_gate_cut"), k.sem("nsa_table_loaded")
                    with nc.Block() as block:
                        @block.sync
                        def _(sp):
                            sp.dma_start(k.tables[1][:], io["nsa_table"]).then_inc(*table_loaded.dma())
                            sp.wait_ge(*table_loaded.dma_at(1))

                        @block.scalar
                        def _(act):
                            nc.scalar.activation(gl2[:], gl2[:], ACT.Sigmoid).then_inc(*sig.inc())

                        @block.vector
                        def _(dve):
                            dve.wait_ge(*sig.at(1))
                            c = gl2[:, 0, :].rearrange("p (h n) -> p h n", n=3)[:, :, 0]
                            nc.vector.tensor_scalar(c, c, k.const("anycmp"), None, ALU.mult).then_inc(*cut.inc())
                    units, first = [], {}
                    for branch in range(3):
                        for i in range(3):
                            for b in range(TB):
                                for e in range(2):
                                    h, r, w = i + 3 * e, slice(HD * e, HD * e + HD), P * (b + 1)
                                    un = dict(q=q2[r, i, P * b:P * b + P], out=y2[:, b, HD * h:HD * h + HD],
                                              gate=gl2[:, b, 3 * h + branch:3 * h + branch + 1])
                                    if branch == 0:
                                        at = NC * (6 * b + h)
                                        un.update(k=kcmp[r, :], mask=k.const("cmp")[:, at:at + NC], v=lambda a, e=e: vcmp[:, e, :])
                                    else:
                                        un.update(k=kv2[r, 1 + branch, 0:w], mask=k.const(f"causal{h}")[:, S - w:S], onto=first[h, b],
                                                  v=lambda a, e=e, n=branch - 1: v2[:, a, P * n + HD * e:P * n + HD * e + HD])
                                    first[h, b] = len(units)
                                    units.append(un)
                    attend(k, units)
                    turn_phase(k, [([y2[:, b, P * f:P * f + P] for b in range(TB)], hT[:, 3 + f, :]) for f in range(3)])
                    see("nsa", hT[:, 3:6, :].rearrange("p b f -> p (b f)"))
            with nc.sbuf_tensor(k.unique("y3"), [P, TB, RW], F32) as y3:
                rwkv_phases(k, z, y3, hT[:, 0:3, :])
                turn_phase(k, [([y3[:, b, P * f:P * f + P] for b in range(TB)], hT[:, f, :]) for f in range(3)])
        see("mix2", hT[:].rearrange("p b f -> p (b f)"))
        with nc.sbuf_tensor(k.unique("yT2"), [P, KD, S], F32) as yT:
            product_phase(k, WO2, [dict(kind="features", to=lambda c, i=i: yT[:, 2 * i + c, :]) for i in range(4)], x=hT)
            norm_phase(k, yT, None, G["post_mix_norm_2"], add=xT, then=(hT, G["pre_ffn_norm_2"]))
            see("h_mix", xT[:].rearrange("p b f -> p (b f)"))
            with nc.sbuf_tensor(k.unique("f2"), [P, NT2, S], F32) as f2:
                conv_up_phase(k, UP2, hT, f2)
                down_phase(k, DN2, f2, yT, 3, NT2, None)
            with nc.sbuf_tensor(k.unique("eT"), [P, KD, S], F32) as eT:
                with nc.sbuf_tensor(k.unique("pin"), [P, TB, PLE], F32) as pin, nc.sbuf_tensor(k.unique("pT"), [P, 2, S], F32) as pT:
                    turn_phase(k, [([pin[:, b, P * f:P * f + P] for b in range(TB)], pT[:, f, :]) for f in range(2)],
                               load=[(pin[:], io["p_2"][0, 0].rearrange("(b p) d -> p b d", p=P))])
                    ple_phase(k, pT, eT)
                norm_phase(k, eT, eT, gple)
                norm_phase(k, yT, None, G["post_ffn_norm_2"], add=xT)
                see("h_ffn", xT[:].rearrange("p b f -> p (b f)"))
                add_rms_gate_phase(k, GATEW, xT, hT, eT)
        with nc.sbuf_tensor(k.unique("xout"), [P, TB, D], F32) as xout:
            banks = []
            for b in range(TB):
                for half in range(2):
                    banks.append(([hT[:, 4 * half + f, P * b:P * b + P] for f in range(4)], xout[:, b, 512 * half:512 * half + 512]))
            turn_phase(k, banks)
            k.phase()
            stored = k.sem("stored")
            with nc.Block() as block:
                @block.sync
                def _(sp):
                    sp.dma_start(out[0].rearrange("(b p) d -> p b d", p=P), xout[:]).then_inc(*stored.dma())
                    sp.wait_ge(*stored.dma_at(1))


def ple_phase(k, pT, eT):
    nc = k.nc
    k.phase()
    made, out = k.sem("ple_made"), [k.sem("ple_out_act"), k.sem("ple_out_dve")]
    with nc.Block() as block:
        @block.sync
        def _(sp):
            issue_slab(k, sp, PLEW + 2)

        @block.tensor
        def _(pe):
            w = slab_view(k, PLEW, D, 2)
            pe.wait_ge(k.slab_loaded[PLEW % 2], loaded_value(PLEW))
            for n in range(KD):
                if n >= 4:
                    pe.wait_ge(*out[n % 2].at((n - 4) // 2 + 1))
                for q in range(2):
                    m = nc.tensor.matmul(k.pl[:, n % 4, :], w[:, q, P * n:P * n + P], pT[:, q, :], start=q == 0, stop=q == 1)
                if n < KD - 1:
                    m.then_inc(*made.inc())
            m.then_inc(k.slab_done[PLEW % 2], 1)

        def empty(eng, e):
            for n in range(e, KD, 2):
                if n < KD - 1:
                    eng.wait_ge(*made.at(n + 1))
                else:
                    eng.wait_ge(k.slab_done[PLEW % 2], PLEW // 2 + 1)
                if e == 0:
                    nc.scalar.activation(eT[:, n, :], k.pl[:, n % 4, :], ACT.Copy).then_inc(*out[0].inc())
                else:
                    nc.vector.tensor_copy(eT[:, n, :], k.pl[:, n % 4, :]).then_inc(*out[1].inc())

        @block.scalar
        def _(act):
            empty(act, 0)

        @block.vector
        def _(dve):
            empty(dve, 1)



_INS = ["x", "mem", "positions", "g_pre_mix", "g_mem", "w_in", "w_mem_kv", "conv_w", "g_attn_out", "g_conv_out", "g_xattn_out",
        "w_out", "g_post_mix", "g_pre_mlp", "w_up", "w_down", "g_post_mlp", "p_2", "pre_mix_norm_2", "post_mix_norm_2",
        "pre_ffn_norm_2", "post_ffn_norm_2", "w_in_2", "w_out_2", "shift_mu_2", "rw_w0_2", "rw_w2_2", "rw_a0_2", "rw_a2_2",
        "rw_g2_2", "rw_k_k_2", "rw_k_a_2", "rw_r_k_2", "rw_gn_w_2", "rw_gn_b_2", "cmp_pe_k_2", "cmp_pe_v_2", "cmp_w1_k_2",
        "cmp_w2_k_2", "cmp_w1_v_2", "cmp_w2_v_2", "s5_lam_re_2", "s5_lam_im_2", "s5_log_dt_2", "s5_b_re_2", "s5_b_im_2",
        "s5_c_re_2", "s5_c_im_2", "s5_d_2", "s5_w_glu_2", "w_up_2", "conv_w_2", "conv_b_2", "w_down_2", "w_ple_2",
        "ple_norm_2", "w_ple_gate_2"]


def kernel(**inputs):
    import numpy as _np
    import concourse.bacc as _bacc
    from concourse import mybir as _mybir
    from concourse.bass_utils import run_bass_kernel_spmd as _run

    nc = _bacc.Bacc("TRN2", target_bir_lowering=False, num_devices=1)
    arrays, io = {}, {}
    given = {name: _np.ascontiguousarray(inputs[name]) for name in _INS}
    given["table"], given["nsa_table"] = constants()[1]
    for name, a in given.items():
        arrays[f"in_{name}"] = a
        io[name] = nc.dram_tensor(f"in_{name}", a.shape, _mybir.dt.from_np(a.dtype), kind="ExternalInput").ap()
    out = nc.dram_tensor("out_0", (1, S, D), F32, kind="ExternalOutput").ap()
    two_blocks(nc, io, out)
    r = _run(nc, [arrays], core_ids=[0])
    return r.results[0]["out_0"]
```

```python
from contextlib import ExitStack, contextmanager

import numpy as np

import concourse.bass as bass
from concourse import mybir

F32 = mybir.dt.float32
F32R = mybir.dt.float32r
I32 = mybir.dt.int32
ALU = mybir.AluOpType
ACT = mybir.ActivationFunctionType
AX_X = mybir.AxisListType.X

P = 128
S = 512
TB = S // P
D = 1024
KD = D // P
NM = 256
HD = 64
EPS = 1e-6
GN_EPS = 64e-5
NEG = -1e30
SCALE = HD ** -0.5
AW, CW, XW = 512, 256, 256
FF1 = 4096
FF2 = 2816
NT2 = FF2 // P
RW = 384
PLE = 256
CMP_LEN, CMP_STRIDE = 32, 16
NC = (S - CMP_LEN) // CMP_STRIDE + 1
SLAB = 2048
TWO_PI = 2.0 * np.pi


def alibi(n):
    def pow2(m):
        return [2.0 ** (-8.0 / m * (i + 1)) for i in range(m)]
    c = 2 ** int(np.floor(np.log2(n)))
    return pow2(n) if c == n else pow2(c) + pow2(2 * c)[0::2][: n - c]


def constants():
    p = np.arange(P)[:, None]
    c = {}
    c["ident"] = np.eye(P)
    c["ones"] = np.ones((P, P))
    c["headsum"] = (p // HD == np.arange(P)[None] // HD) * 1.0
    rel = p + 384 - np.arange(S)[None]
    mult = ((rel >= 0) & (rel <= 128)) * 1 + ((rel >= 0) & (rel % 4 == 0)) * 1 + ((rel >= 0) & (rel % 16 == 0)) * 1
    c["band"] = np.where(mult > 0, np.log(np.maximum(mult, 1)) / SCALE, NEG / SCALE)
    c["nomask"] = np.zeros((P, NM))
    for h, sl in enumerate(alibi(6)):
        c[f"causal{h}"] = np.where(rel >= 0, -np.float32(sl) * np.maximum(rel, 0) / SCALE, NEG / SCALE)
    t = p[:, :, None] + P * np.arange(TB)[None, :, None]
    dist = t - (np.arange(NC) * CMP_STRIDE + CMP_LEN - 1)[None, None, :]
    c["cmp"] = np.stack([np.where(dist >= 0, -np.float32(sl) * np.abs(dist) / SCALE, NEG / SCALE) for sl in alibi(6)], 2).reshape(P, -1)
    c["anycmp"] = (p >= CMP_LEN - 1) * 1.0
    inv = (1e4 ** (-(np.arange(32) * 2.0 / HD)))[None, :].repeat(P, 0)
    c["invfreq"] = inv
    t = np.arange(P)[None]
    lt, le = (p < t) * 1.0, (p <= t) * 1.0
    c["chunkmask"] = np.concatenate([le, lt, le], 1)
    c["below"] = (p > t) * 1.0
    b = 1
    while b < P:
        c[f"join{b}"] = ((p // (2 * b) == t // (2 * b)) & (p % (2 * b) < b) & (t % (2 * b) >= b)) * 1.0
        b *= 2
    c["join1T"] = c["join1"].T
    for g in range(2):
        c[f"twice{g}"] = (p == HD * g + np.arange(P)[None] % HD) * 1.0
    c["headcol"] = (p // HD == np.arange(2)[None]) * 1.0
    c["pairsel"] = ((p // 16) % 2 == np.arange(2)[None]) * 1.0
    c["first"] = (np.arange(S)[None] % P != 0) * np.ones((P, 1))
    nsa = [name for name in c if name.startswith(("causal", "cmp"))]
    names, tables = {}, []
    for which, group in enumerate(([name for name in c if name not in nsa], nsa)):
        at = 0
        for name in group:
            names[name] = (which, at, c[name].shape[1])
            at += c[name].shape[1]
        tables.append(np.ascontiguousarray(np.concatenate([c[name].astype(np.float32) for name in group], 1)))
    return names, tables


class Tally:

    def __init__(self, sem):
        self.sem, self.base, self.total = sem, 0, 0

    def inc(self, times=1):
        self.total += times
        return self.sem, 1

    def dma(self, times=1):
        self.total += 16 * times
        return self.sem, 16

    def at(self, n):
        return self.sem, self.base + n

    def dma_at(self, n):
        return self.sem, self.base + 16 * n


VECTORS = [("g_pre_mix", 8), ("g_mem", 8), ("g_attn_out", 4), ("g_conv_out", 2), ("g_xattn_out", 2), ("g_post_mix", 8),
           ("g_pre_mlp", 8), ("g_post_mlp", 8), ("pre_mix_norm_2", 8), ("post_mix_norm_2", 8), ("pre_ffn_norm_2", 8),
           ("post_ffn_norm_2", 8), ("ple_norm_2", 8), ("shift_mu_2", 11), ("rw_w0_2", 3), ("rw_a0_2", 3), ("rw_k_k_2", 3),
           ("rw_k_a_2", 3), ("rw_r_k_2", 3), ("s5_d_2", 2), ("conv_w", 6), ("conv_b_2", 44), ("s5_lam_re_2", 8),
           ("s5_lam_im_2", 8), ("conv_w_2", 132)]


class Kit:

    def __init__(self, nc, ctx, io):
        self.nc, self.ctx, self.io, self.tallies = nc, ctx, io, {}
        self.names, tables = constants()
        self.widths = [t.shape[1] for t in tables]
        self.tables = [None, None]
        self.buffers = 0
        self.vec_at, at = {}, 0
        for name, n in VECTORS:
            if n < P and at // P != (at + n - 1) // P:
                at = -(-at // P) * P
            self.vec_at[name] = at
            at += n

    def phase(self):
        for t in self.tallies.values():
            t.base = t.total

    @contextmanager
    def splitting(self):
        with ExitStack() as ctx:
            self.split = [[ctx.enter_context(self.nc.sbuf_tensor(self.unique("slab_part"), [P, SLAB], F32R)) for _ in range(2)]
                          for _ in range(2)]
            yield

    def sem(self, name):
        if name not in self.tallies:
            self.tallies[name] = Tally(self.ctx.enter_context(self.nc.semaphore(name)))
        return self.tallies[name]

    def unique(self, name):
        self.buffers += 1
        return f"{name}_{self.buffers}"

    def vec(self, name, n=None):
        return self.vecs[:, self.vec_at[name]:self.vec_at[name] + (n or dict(VECTORS)[name])]

    def const(self, name):
        which, a, n = self.names[name]
        return self.tables[which][:, a:a + n]



IN1, WO1, FFN1, IN2, WO2, FFN2, PLEW, GATEW, NSLABS = 0, 12, 16, 48, 60, 64, 97, 98, 102
Q2, KC2, KS2, GL2, S52 = 1408, 1792, 2048, 2560, 2578
TURNS1, TURNS2 = FF1 // 512, FF2 // 256


def slab_parts(k, g):
    io = k.io
    slot = k.ring[:, g % 2, :]

    def cols(w, lo, n=256, rows=slice(0, D), at=0, width=256):
        kt = (rows.stop - rows.start) // P
        dst = slot[:, 0:kt * width].rearrange("p (k n) -> p k n", n=width)[:, :, at:at + n]
        return dst, w[rows, lo:lo + n].rearrange("(k p) n -> p k n", p=P)

    def rows_of(w, lo):
        return slot.rearrange("p (k n) -> p k n", n=D), w[lo:lo + 256, :].rearrange("(k p) n -> p k n", p=P)

    if g < 10:
        return [cols(io["w_in"][0], 256 * g)]
    if g < WO1:
        return [cols(io["w_mem_kv"][0], 256 * (g - 10))]
    if g < FFN1:
        return [cols(io["w_out"][0], 256 * (g - WO1))]
    if g < IN2:
        n = g - FFN1
        if n < 2:
            return [cols(io["w_up"][0], 256 * n)]
        return [rows_of(io["w_down"][0], 512 * (TURNS1 - 1) + 256 * (n - 4 * TURNS1 + 2))]
    w = io["w_in_2"][0]
    if g < WO2:
        n = g - IN2
        if n < 5:
            return [cols(w, 256 * n)]
        if n < 7:
            if n == 5:
                return [cols(w, 1280, 128)] + [cols(w, Q2 + HD * h, HD, at=128 + HD * j) for j, h in enumerate((0, 3))]
            return [cols(w, Q2 + HD * h, HD, at=HD * j) for j, h in enumerate((1, 4, 2, 5))]
        if n == 7:
            return [cols(w, KC2)]
        if n == 8:
            return [cols(w, KS2, 128), cols(w, KS2 + 256, 128, at=128)]
        if n == 9:
            return [cols(w, KS2 + 128, 128), cols(w, KS2 + 384, 128, at=128)]
        if n == 10:
            return [cols(w, S52)]
        return [cols(w, GL2, 18, width=18)]
    if g < FFN2:
        return [cols(io["w_out_2"][0], 256 * (g - WO2))]
    if g < PLEW:
        n = g - FFN2
        if n < 2:
            return [cols(io["w_up_2"][0], FF2 * n)]
        return [rows_of(io["w_down_2"][0], 256 * (TURNS2 - 1))]
    if g == PLEW:
        return [cols(io["w_ple_2"][0], 0, D, rows=slice(0, PLE), width=D)]
    return [cols(io["w_ple_gate_2"][0], 256 * (g - GATEW))]


PARTS = {IN2 + 5: 3, IN2 + 6: 4, IN2 + 8: 2, IN2 + 9: 2}


def loaded_value(g):
    return 16 * sum(PARTS.get(q, 1) for q in range(g % 2, g + 1, 2))


def issue_slab(k, sp, g):
    if g >= NSLABS:
        return
    if g >= 2:
        sp.wait_ge(k.slab_lo[g % 2], g // 2)
    for dst, src in slab_parts(k, g):
        sp.dma_start(dst, src).then_inc(k.slab_loaded[g % 2], 16)


def slab_size(g):
    return KD * 18 if g == WO2 - 1 else SLAB


def hi_of_slab(k, act, j, n, loaded, size=SLAB):
    act.wait_ge(k.slab_loaded[j], loaded)
    if not isinstance(n, int) or n > 0:
        act.wait_ge(k.slab_done[j], n)
    k.nc.scalar.activation(k.split[j][0][:, 0:size], k.ring[:, j, 0:size], ACT.Copy).then_inc(k.slab_hi[j], 1)


def lo_of_slab(k, pool, j, n, size=SLAB):
    pool.wait_ge(k.slab_hi[j], n + 1)
    k.nc.gpsimd.tensor_tensor(k.split[j][1][:, 0:size], k.ring[:, j, 0:size], k.split[j][0][:, 0:size].bitcast(F32),
                              ALU.subtract).then_inc(k.slab_lo[j], 1)


def split_ahead(k, n):
    first = k.split_done
    k.split_done = min(first + n, NSLABS)
    return range(first, k.split_done)


def use_slab(k, pe, j, n):
    pe.wait_ge(k.slab_lo[j], n + 1)


def slab_view(k, j, part, width=256, kt=KD):
    return k.split[j][part][:, 0:kt * width].rearrange("p (k n) -> p k n", n=width)


def product(nc, out, pairs, first=True, last=True):
    for i, (a, b) in enumerate(pairs):
        for n, (x, y) in enumerate(((0, 0), (0, 1), (1, 0))):
            m = nc.tensor.matmul(out, a[x], b[y], start=first and i == 0 and n == 0,
                                 stop=last and i == len(pairs) - 1 and n == 2)
    return m



def halves(dst, src):
    if isinstance(dst, tuple):
        return [(dst[0], src[0:HD]), (dst[1], src[HD:P])]
    return [(dst, src)]


def turn_phase(k, banks, load=(), gain=None, stream=(), zero=()):
    nc = k.nc
    k.phase()
    loaded, turned = k.sem("turn_loaded"), k.sem("turned")
    emptied = [k.sem("turn_emptied_dve"), k.sem("turn_emptied_act")]
    nload = len(load)
    with nc.Block() as block:
        @block.sync
        def _(sp):
            for dst, src in load:
                sp.dma_start(dst, src).then_inc(*loaded.dma())
            for g in stream:
                issue_slab(k, sp, g)

        @block.tensor
        def _(pe):
            if nload:
                pe.wait_ge(*loaded.dma_at(nload))
            for b, (srcs, dst) in enumerate(banks):
                if b >= 4:
                    pe.wait_ge(*emptied[b % 2].at(b // 2 - 1))
                for j, s in enumerate(srcs):
                    rows, cols = s.shape
                    t = nc.tensor.transpose(k.pm[0:cols, b % 4, j * rows:(j + 1) * rows], s, k.ident[0:rows, 0:rows])
                t.then_inc(*turned.inc())

        def empty(eng, e):
            for b, (srcs, dst) in enumerate(banks):
                if b % 2 != e:
                    continue
                rows, cols = srcs[0].shape
                src = k.pm[0:cols, b % 4, 0:rows * len(srcs)]
                if not isinstance(dst, tuple) and len(dst.shape) == 3:
                    src = src.rearrange("p (a b) -> p a b", a=dst.shape[1])
                g = gain(b) if gain else None
                eng.wait_ge(*turned.at(b + 1))
                for to, part in halves(dst, src):
                    if e == 0:
                        i = nc.vector.tensor_copy(to, part) if g is None else nc.vector.tensor_scalar(to, part, g, None, ALU.mult)
                    else:
                        i = nc.scalar.activation(to, part, ACT.Copy) if g is None else nc.scalar.activation(to, part, ACT.Copy, scale=g)
                i.then_inc(*emptied[e].inc())

        @block.vector
        def _(dve):
            for z in zero:
                nc.vector.memset(z, 0.0).then_inc(*k.sem("halves_zeroed").inc())
            empty(dve, 0)

        @block.scalar
        def _(act):
            empty(act, 1)


def norm_phase(k, src, dst, gain, kt=KD, n=S, width=D, add=None, then=None, ahead=0):
    nc = k.nc
    k.phase()
    sq_ready, sum_ready, rstd_ready = k.sem("norm_sq"), k.sem("norm_sum"), k.sem("norm_rstd")
    std_ready, scaled, added, out_ready = k.sem("norm_std"), k.sem("norm_scaled"), k.sem("norm_added"), k.sem("norm_out")
    rounds = 2 if then else 1
    ahead = split_ahead(k, ahead)
    with nc.sbuf_tensor(k.unique("sq"), [P, kt, n], F32) as sq, nc.sbuf_tensor(k.unique("std"), [P, 2, n], F32) as std, \
            nc.sbuf_tensor(k.unique("scaled"), [P, 2, n], F32) as tmp, nc.Block() as block:
        @block.scalar
        def _(act):
            for g in ahead:
                hi_of_slab(k, act, g % 2, g // 2, loaded_value(g), slab_size(g))
            for r in range(rounds):
                x = (src, add)[r]
                for i in range(kt):
                    if r:
                        act.wait_ge(*added.at(i + 1))
                        act.wait_ge(*sum_ready.at(1))
                    nc.scalar.activation(sq[:, i, :], x[:, i, 0:n], ACT.Square).then_inc(*sq_ready.inc())
                act.wait_ge(*sum_ready.at(r + 1))
                nc.scalar.activation(std[:, r, :], k.pm[:, r, 0:n], ACT.Sqrt, bias=k.eps[:, 0:1], scale=1.0 / width)\
                    .then_inc(*std_ready.inc())

        @block.tensor
        def _(pe):
            for r in range(rounds):
                for i in range(kt):
                    pe.wait_ge(*sq_ready.at(r * kt + i + 1))
                    m = nc.tensor.matmul(k.pm[:, r, 0:n], k.ones, sq[:, i, :], start=i == 0, stop=i == kt - 1)
                m.then_inc(*sum_ready.inc())

        @block.vector
        def _(dve):
            for r in range(rounds):
                x, g, y = ((src, gain, dst) if r == 0 else (add, then[1], then[0]))
                dve.wait_ge(*std_ready.at(r + 1))
                nc.vector.reciprocal(std[:, r, :], std[:, r, :]).then_inc(*rstd_ready.inc())
                dve.wait_ge(*rstd_ready.at(r + 1))
                for i in range(kt):
                    if add is not None and r == 0:
                        if i >= 2:
                            dve.wait_ge(*added.at(i - 1))
                        nc.vector.scalar_tensor_tensor(out=tmp[:, i % 2, :], in0=x[:, i, :], scalar=g[:, i:i + 1],
                                                       in1=std[:, r, :], op0=ALU.mult, op1=ALU.mult)\
                            .then_inc(*scaled.inc())
                    else:
                        nc.vector.scalar_tensor_tensor(out=y[:, i, 0:n], in0=x[:, i, 0:n], scalar=g[:, i:i + 1],
                                                       in1=std[:, r, :], op0=ALU.mult, op1=ALU.mult)\
                            .then_inc(*out_ready.inc())

        @block.gpsimd
        def _(pool):
            for g in ahead:
                lo_of_slab(k, pool, g % 2, g // 2, slab_size(g))
            if add is not None:
                for i in range(kt):
                    pool.wait_ge(*scaled.at(i + 1))
                    nc.gpsimd.tensor_tensor(add[:, i, :], add[:, i, :], tmp[:, i % 2, :], ALU.add).then_inc(*added.inc())


def product_phase(k, g0, slabs, sources, beside=None, zero=()):
    nc = k.nc
    k.phase()
    drained = [k.sem("drained_act"), k.sem("drained_dve")]
    x_hi, x_lo = k.sem("x_hi"), k.sem("x_lo")
    n = len(slabs)
    todo = split_ahead(k, g0 + n - k.split_done)
    with ExitStack() as ctx:
        parts = [[ctx.enter_context(nc.sbuf_tensor(k.unique("x_part"), [P, kt, nt], F32R)) for _ in range(2)] for _, kt, nt in sources]
        tiles = [(s, q) for s, (_, kt, _) in enumerate(sources) for q in range(kt)]
        block = ctx.enter_context(nc.Block())

        def empty(eng, e, i):
            s, g = slabs[i], g0 + i
            width, nt = s.get("width", 256), sources[s.get("source", 0)][2]
            j = g % 2
            eng.wait_ge(k.slab_done[j], g // 2 + 1)
            if s["kind"] == "features":
                pairs = [(s["to"](c), k.pl[:, 2 * j + c, 0:nt]) for c in range(2)]
            else:
                pairs = [(s["to"][:, b, :], k.pl[:, 2 * j + b // 2, 256 * (b % 2):256 * (b % 2) + width]) for b in range(nt // P)]
            for dst, src in [h for pair in pairs for h in halves(*pair)]:
                m = nc.scalar.activation(dst, src, ACT.Copy) if e == 0 else nc.vector.tensor_copy(dst, src)
            m.then_inc(*drained[e].inc())

        @block.vector
        def _(dve):
            for t, (s, q) in enumerate(tiles):
                dve.wait_ge(*x_hi.at(t + 1))
                nc.vector.tensor_tensor(parts[s][1][:, q, :], sources[s][0][:, q, :], parts[s][0][:, q, :].bitcast(F32), ALU.subtract)\
                    .then_inc(*x_lo.inc())
            for z in zero:
                nc.vector.memset(z, 0.0).then_inc(*k.sem("halves_zeroed").inc())
            if beside:
                beside.vector(dve)
            for i in range(n):
                if (g0 + i) % 2 and not beside:
                    empty(dve, 1, i)

        @block.sync
        def _(sp):
            if beside:
                beside.sync(sp)
            for g in range(g0 + 2, g0 + n + 2):
                issue_slab(k, sp, g)

        @block.tensor
        def _(pe):
            seen, have = [0, 0], 0
            for i, s in enumerate(slabs):
                g = g0 + i
                j = g % 2
                src, width, kt = parts[s.get("source", 0)], s.get("width", 256), s.get("kt", KD)
                nt = sources[s.get("source", 0)][2]
                at = sum(q for _, q, _ in sources[:s.get("source", 0)])
                w = [slab_view(k, j, a, width, kt) for a in range(2)]
                use_slab(k, pe, j, g // 2)
                if seen[j]:
                    pe.wait_ge(*(drained[0].at(i - 1) if beside else drained[j].at(seen[j])))
                seen[j] += 1
                groups = [(k.pl[:, 2 * j + c, 0:nt], c) for c in range(2)] if s["kind"] == "features" else \
                    [(k.pl[:, 2 * j + b // 2, 256 * (b % 2):256 * (b % 2) + width], b) for b in range(nt // P)]
                for out, c in groups:
                    for q in range(kt):
                        if at + q >= have:
                            have = at + q + 1
                            pe.wait_ge(*x_lo.at(have))
                        cols = slice(P * c, P * c + P)
                        if s["kind"] == "features":
                            a, b = [w[e][:, q, cols] for e in range(2)], [src[e][:, q, 0:nt] for e in range(2)]
                        else:
                            a, b = [src[e][:, q, cols] for e in range(2)], [w[e][:, q, 0:width] for e in range(2)]
                        m = product(nc, out, [(a, b)], first=q == 0, last=q == kt - 1)
                m.then_inc(k.slab_done[j], 1)
                if beside:
                    beside.tensor(pe, i)

        @block.scalar
        def _(act):
            for s, q in tiles:
                nc.scalar.activation(parts[s][0][:, q, :], sources[s][0][:, q, :], ACT.Copy).then_inc(*x_hi.inc())
            for i in range(n + 2):
                if g0 + i in todo:
                    hi_of_slab(k, act, (g0 + i) % 2, (g0 + i) // 2, loaded_value(g0 + i), slab_size(g0 + i))
                if i >= 2 and (beside or (g0 + i - 2) % 2 == 0):
                    empty(act, 0, i - 2)
                if beside:
                    beside.scalar(act, i)

        @block.gpsimd
        def _(pool):
            for g in todo:
                lo_of_slab(k, pool, g % 2, g // 2, slab_size(g))


def split_x(k, act, dve, x, parts, x_hi, x_lo):
    nc = k.nc
    for q in range(KD):
        if act is not None:
            nc.scalar.activation(parts[0][:, q, :], x[:, q, :], ACT.Copy).then_inc(*x_hi.inc())
        else:
            dve.wait_ge(*x_hi.at(q + 1))
            nc.vector.tensor_tensor(parts[1][:, q, :], x[:, q, :], parts[0][:, q, :].bitcast(F32), ALU.subtract).then_inc(*x_lo.inc())


def ffn1_phase(k, g0, x, y):
    nc = k.nc
    k.phase()
    assert k.split_done == g0 + 2
    k.split_done = g0 + 4 * TURNS1
    loops = TURNS1 - 1
    w_up, w_down = k.io["w_up"][0], k.io["w_down"][0]
    x_hi, x_lo = k.sem("x_hi"), k.sem("x_lo")
    relu_ready = [k.sem("relu_a"), k.sem("relu_b")]
    squared = [k.sem("squared_a"), k.sem("squared_b")]
    f_hi, f_lo = [k.sem("f_hi_a"), k.sem("f_hi_b")], [k.sem("f_lo_a"), k.sem("f_lo_b")]
    tile_made, tile_added, y_zeroed = k.sem("down_tile_made"), k.sem("down_tile_added"), k.sem("y_zeroed")
    with ExitStack() as ctx:
        def sb(name, shape, dt=F32):
            return ctx.enter_context(nc.sbuf_tensor(k.unique(name), shape, dt))
        parts = [sb("x_part", [P, KD, S], F32R) for _ in range(2)]
        relu, f = sb("relu", [P, 2, 2, S]), sb("f", [P, 2, 2, S])
        fp = [sb("f_part", [P, 2, 2, S], F32R) for _ in range(2)]
        block = ctx.enter_context(nc.Block())
        n0 = g0 // 2

        @block.sync
        def _(sp):
            with sp.Fori(0, loops) as i:
                for o in range(4):
                    j, e = o % 2, o // 2
                    sp.wait_ge(k.slab_lo[j], n0 + 1 + e + 2 * i)
                    if j == 0:
                        src = w_up[:, bass.ds(512 * i + 512 + 256 * e, 256)].rearrange("(k p) n -> p k n", p=P)
                        dst = k.ring[:, j, :].rearrange("p (k n) -> p k n", n=256)
                    else:
                        src = w_down[bass.ds(512 * i + 256 * e, 256), :].rearrange("(k p) n -> p k n", p=P)
                        dst = k.ring[:, j, :].rearrange("p (k n) -> p k n", n=D)
                    sp.dma_start(dst, src).then_inc(k.slab_loaded[j], 16)
            for g in range(g0 + 4 * TURNS1 - 2, g0 + 4 * TURNS1 + 2):
                issue_slab(k, sp, g)

        @block.tensor
        def _(pe):
            def up(e, j, n, t, first=False):
                use_slab(k, pe, j, n0 + n)
                if not first:
                    pe.wait_ge(*squared[e].at(t))
                w = [slab_view(k, j, a) for a in range(2)]
                for c in range(2):
                    for q in range(KD):
                        if first and e == 0 and c == 0:
                            pe.wait_ge(*x_lo.at(q + 1))
                        m = product(nc, k.pl[:, 2 * e + c, :], [([w[a][:, q, P * c:P * c + P] for a in range(2)],
                                                                 [parts[a][:, q, :] for a in range(2)])], q == 0, q == KD - 1)
                m.then_inc(k.slab_done[j], 1)

            def down(e, j, n, t, made, times):
                use_slab(k, pe, j, n0 + n)
                pe.wait_ge(*f_lo[e].at(t + 1))
                w = [slab_view(k, j, a, D, 2) for a in range(2)]
                for c in range(KD):
                    pe.wait_ge(*tile_added.at(made + c + 1))
                    m = product(nc, k.pm[:, c % 4, :], [([w[a][:, q, P * c:P * c + P] for a in range(2)],
                                                         [fp[a][:, e, q, :] for a in range(2)]) for q in range(2)])
                    if c < KD - 1:
                        m.then_inc(*tile_made.inc(times))
                m.then_inc(k.slab_done[j], 1)

            up(0, 0, 0, 0, True)
            up(1, 1, 0, 0, True)
            with pe.Fori(0, loops) as i:
                up(0, 0, 1 + 2 * i, i + 1)
                down(0, 1, 1 + 2 * i, i, 16 * i, loops)
                up(1, 0, 2 + 2 * i, i + 1)
                down(1, 1, 2 + 2 * i, i, 16 * i + 8, loops)
            down(0, 0, 2 * TURNS1 - 1, TURNS1 - 1, 16 * loops, 1)
            down(1, 1, 2 * TURNS1 - 1, TURNS1 - 1, 16 * loops + 8, 1)

        @block.scalar
        def _(act):
            def hi(j, n):
                hi_of_slab(k, act, j, n0 + n, loaded_value(g0 + j) + 16 * n)

            def relu_tiles(e, t, j, n, first=False):
                act.wait_ge(k.slab_done[j], n0 + n + 1)
                if not first:
                    act.wait_ge(*squared[e].at(t))
                nc.scalar.activation(relu[:, e], k.pl[:, 2 * e:2 * e + 2, :], ACT.Relu).then_inc(*relu_ready[e].inc(1 if first else loops))

            def hidden_hi(e, t, first=False):
                act.wait_ge(*squared[e].at(t + 1))
                if not first:
                    act.wait_ge(k.slab_done[1], n0 + e + 2 * t)
                nc.scalar.activation(fp[0][:, e], f[:, e], ACT.Copy).then_inc(*f_hi[e].inc(1 if first else loops))

            split_x(k, act, None, x, parts, x_hi, x_lo)
            for e in range(2):
                hi(e, 1)
                relu_tiles(e, 0, e, 0, True)
            for e in range(2):
                hidden_hi(e, 0, True)
            with act.Fori(0, loops) as i:
                for e in range(2):
                    hi(0, 2 + e + 2 * i)
                    relu_tiles(e, i + 1, 0, 1 + e + 2 * i)
                    hi(1, 2 + e + 2 * i)
                    hidden_hi(e, i + 1)

        @block.gpsimd
        def _(pool):
            for c in range(KD):
                nc.gpsimd.memset(y[:, c, :], 0.0).then_inc(*y_zeroed.inc())
            for e in range(2):
                lo_of_slab(k, pool, e, n0 + 1)
            with pool.Fori(0, loops) as i:
                for e in range(2):
                    lo_of_slab(k, pool, 0, n0 + 2 + e + 2 * i)
                    lo_of_slab(k, pool, 1, n0 + 2 + e + 2 * i)

        @block.vector
        def _(dve):
            def square(e, t, first=False):
                dve.wait_ge(*relu_ready[e].at(t + 1))
                if not first:
                    dve.wait_ge(*f_hi[e].at(t))
                    dve.wait_ge(*f_lo[e].at(t))
                nc.vector.tensor_tensor(f[:, e], relu[:, e], k.pl[:, 2 * e:2 * e + 2, :], ALU.mult)\
                    .then_inc(*squared[e].inc(1 if first else loops))

            def hidden_lo(e, t, first=False):
                dve.wait_ge(*f_hi[e].at(t + 1))
                nc.vector.tensor_tensor(fp[1][:, e], f[:, e], fp[0][:, e].bitcast(F32), ALU.subtract)\
                    .then_inc(*f_lo[e].inc(1 if first else loops))

            split_x(k, None, dve, x, parts, x_hi, x_lo)
            dve.sem_inc(tile_added.sem, 4)
            tile_added.total += 4
            dve.wait_ge(*y_zeroed.at(KD))
            for e in range(2):
                square(e, 0, True)
            for e in range(2):
                hidden_lo(e, 0, True)
            with dve.Fori(0, loops) as i:
                for e in range(2):
                    square(e, i + 1)
                    add_tiles(k, dve, y, 1, n0 + 2 + e + 2 * i, 2 * i + e, tile_made, tile_added, loops)
                    hidden_lo(e, i + 1)
            for e in range(2):
                add_tiles(k, dve, y, e, n0 + 2 * TURNS1, 2 * loops + e, tile_made, tile_added, 1)


def add_tiles(k, dve, y, j, done, before, tile_made, tile_added, times):
    for c in range(KD):
        if c < KD - 1:
            dve.wait_ge(*tile_made.at((KD - 1) * before + c + 1))
        else:
            dve.wait_ge(k.slab_done[j], done)
        dve.wait_ge(*tile_added.at(KD * before + c + 4))
        k.nc.vector.tensor_tensor(y[:, c, :], y[:, c, :], k.pm[:, c % 4, :], ALU.add).then_inc(*tile_added.inc(times))


def ffn2_phase(k, g0, x, y):
    nc = k.nc
    k.phase()
    assert k.split_done == g0 + 2 and g0 % 2 == 0
    k.split_done = g0 + 3 * TURNS2 + 1
    bodies = (TURNS2 - 1) // 2
    w_up, w_down = k.io["w_up_2"][0], k.io["w_down_2"][0]
    cw, cb = k.vec("conv_w_2").rearrange("p (t n) -> p t n", t=3), k.vec("conv_b_2")
    x_hi, x_lo = k.sem("x_hi"), k.sem("x_lo")
    tap2, tap1 = [k.sem("tap2_gate"), k.sem("tap2_up")], [k.sem("tap1_gate"), k.sem("tap1_up")]
    conv = [k.sem("conv_gate"), k.sem("conv_up")]
    gelu_ready, f_ready, f_hi, f_lo = k.sem("gelu_ready"), k.sem("f_ready"), k.sem("f_hi_a"), k.sem("f_lo_a")
    tile_made, tile_added, y_zeroed = k.sem("down_tile_made"), k.sem("down_tile_added"), k.sem("y_zeroed")
    n0 = g0 // 2
    with ExitStack() as ctx:
        def sb(name, shape, dt=F32):
            return ctx.enter_context(nc.sbuf_tensor(k.unique(name), shape, dt))
        parts = [sb("x_part", [P, KD, S], F32R) for _ in range(2)]
        cv, ge, f = sb("conv", [P, 2, 2, S]), sb("gelu", [P, 2, S]), sb("f", [P, 2, S])
        fp = [sb("f_part", [P, 2, S], F32R) for _ in range(2)]
        block = ctx.enter_context(nc.Block())

        def turns(eng, do):
            do(0, 0, 0, 1)
            with eng.Fori(0, bodies) as b:
                for h in range(2):
                    do(2 * b + (1 + h), h, 3 * b + (1 + h), bodies)

        def place(slot, n, o):
            return (slot + o) % 2, n + (slot + o) // 2

        @block.sync
        def _(sp):
            with sp.Fori(0, bodies) as b:
                for h in range(2):
                    for o, (kind, w) in enumerate((("up", 0), ("up", FF2), ("down", 0))):
                        j, n = place(h, 3 * b + (1 + h), o)
                        sp.wait_ge(k.slab_lo[j], n0 + n)
                        if kind == "up":
                            src = w_up[:, bass.ds(512 * b + (256 * (1 + h) + w), 256)].rearrange("(k p) n -> p k n", p=P)
                            dst = k.ring[:, j, :].rearrange("p (k n) -> p k n", n=256)
                        else:
                            src = w_down[bass.ds(512 * b + 256 * h, 256), :].rearrange("(k p) n -> p k n", p=P)
                            dst = k.ring[:, j, :].rearrange("p (k n) -> p k n", n=D)
                        sp.dma_start(dst, src).then_inc(k.slab_loaded[j], 16)
            for g in range(g0 + 3 * TURNS2 - 1, g0 + 3 * TURNS2 + 2):
                issue_slab(k, sp, g)

        @block.tensor
        def _(pe):
            def down(j, n, t, times):
                use_slab(k, pe, j, n0 + n)
                pe.wait_ge(*f_lo.at(t + 1))
                w = [slab_view(k, j, a, D, 2) for a in range(2)]
                for c in range(KD):
                    pe.wait_ge(*tile_added.at(KD * t + c + 1))
                    m = product(nc, k.pm[:, c % 4, :], [([w[a][:, q, P * c:P * c + P] for a in range(2)],
                                                         [fp[a][:, q, :] for a in range(2)]) for q in range(2)])
                    if c < KD - 1:
                        m.then_inc(*tile_made.inc(times))
                m.then_inc(k.slab_done[j], 1)

            def turn(t, slot, n, times):
                for e in range(2):
                    j, m0 = place(slot, n, e)
                    use_slab(k, pe, j, n0 + m0)
                    if times > 1:
                        pe.wait_ge(*conv[e].at(2 * t))
                    w = [slab_view(k, j, a) for a in range(2)]
                    for c in range(2):
                        for q in range(KD):
                            if times == 1 and e == 0 and c == 0:
                                pe.wait_ge(*x_lo.at(q + 1))
                            m = product(nc, k.pl[:, 2 * e + c, :], [([w[a][:, q, P * c:P * c + P] for a in range(2)],
                                                                     [parts[a][:, q, :] for a in range(2)])], q == 0, q == KD - 1)
                    m.then_inc(k.slab_done[j], 1)
                if times > 1:
                    down(*place(slot, n, 2), t - 1, times)
            turns(pe, turn)
            down(0, (3 * TURNS2 - 1) // 2, TURNS2 - 1, 1)

        @block.scalar
        def _(act):
            def hi(slot, n, o):
                j, m = place(slot, n, o)
                hi_of_slab(k, act, j, n0 + m, loaded_value(g0 + j) + 16 * m)

            def turn(t, slot, n, times):
                for e in range(2):
                    j, m = place(slot, n, e)
                    hi(slot, n, e + 2)
                    act.wait_ge(k.slab_done[j], n0 + m + 1)
                    if times > 1:
                        act.wait_ge(*(f_ready.at(2 * t) if e else gelu_ready.at(2 * t)))
                    for c in range(2):
                        at = 2 * t + (NT2 * e + c)
                        nc.scalar.activation(cv[:, e, c, :], k.pl[:, 2 * e + c, :], ACT.Identity, scale=cw[:, 2, bass.ds(at, 1)],
                                             bias=cb[:, bass.ds(at, 1)]).then_inc(*tap2[e].inc(times))
                for c in range(2):
                    act.wait_ge(*conv[0].at(2 * t + c + 1))
                    if times > 1:
                        act.wait_ge(*f_ready.at(2 * t))
                    nc.scalar.activation(ge[:, c, :], cv[:, 0, c, :], ACT.Gelu_apprx_tanh).then_inc(*gelu_ready.inc(times))
                if times > 1:
                    hi(slot, n, 4)
                    j, m = place(slot, n, 2)
                    act.wait_ge(k.slab_done[j], n0 + m + 1)
                act.wait_ge(*f_ready.at(2 * t + 2))
                nc.scalar.activation(fp[0][:], f[:], ACT.Copy).then_inc(*f_hi.inc(times))
            split_x(k, act, None, x, parts, x_hi, x_lo)
            turns(act, turn)

        @block.gpsimd
        def _(pool):
            for c in range(KD):
                nc.gpsimd.memset(y[:, c, :], 0.0).then_inc(*y_zeroed.inc())

            def turn(t, slot, n, times):
                for e in range(2):
                    j, m = place(slot, n, e + 2)
                    lo_of_slab(k, pool, j, n0 + m)
                if times > 1:
                    pool.wait_ge(*f_hi.at(t))
                    pool.wait_ge(*f_lo.at(t))
                for c in range(2):
                    pool.wait_ge(*gelu_ready.at(2 * t + c + 1))
                    pool.wait_ge(*conv[1].at(2 * t + c + 1))
                    nc.gpsimd.tensor_tensor(f[:, c, :], ge[:, c, :], cv[:, 1, c, :], ALU.mult).then_inc(*f_ready.inc(times))
                if times > 1:
                    j, m = place(slot, n, 4)
                    lo_of_slab(k, pool, j, n0 + m)
            turns(pool, turn)

        @block.vector
        def _(dve):
            split_x(k, None, dve, x, parts, x_hi, x_lo)
            dve.sem_inc(tile_added.sem, 4)
            tile_added.total += 4
            dve.wait_ge(*y_zeroed.at(KD))

            def turn(t, slot, n, times):
                for e in range(2):
                    for tap, source, result in ((1, tap2, tap1), (0, tap1, conv)):
                        for c in range(2):
                            at = 2 * t + (NT2 * e + c)
                            dve.wait_ge(*source[e].at(2 * t + c + 1))
                            d = 2 - tap
                            nc.vector.scalar_tensor_tensor(out=cv[:, e, c, d:S], in0=k.pl[:, 2 * e + c, 0:S - d],
                                                           scalar=cw[:, tap, bass.ds(at, 1)], in1=cv[:, e, c, d:S],
                                                           op0=ALU.mult, op1=ALU.add).then_inc(*result[e].inc(times))
                if times > 1:
                    j, m = place(slot, n, 2)
                    add_tiles(k, dve, y, j, n0 + m + 1, t - 1, tile_made, tile_added, times)
                dve.wait_ge(*f_hi.at(t + 1))
                nc.vector.tensor_tensor(fp[1][:], f[:], fp[0][:].bitcast(F32), ALU.subtract).then_inc(*f_lo.inc(times))
            turns(dve, turn)
            add_tiles(k, dve, y, 0, n0 + (3 * TURNS2 - 1) // 2 + 1, TURNS2 - 1, tile_made, tile_added, 1)


def attend(k, groups):
    nc = k.nc
    k.phase()
    units = [dict(u, group=g) for g, (us, _) in enumerate(groups) for u in us]
    n = len(units)
    for s, u in enumerate(units):
        same = [i for i in range(n) if (units[i]["group"], units[i]["half"]) == (u["group"], u["half"])]
        u["first"], u["last"], u["end"] = s == same[0], s == same[-1], s == n - 1 or units[s + 1]["group"] != u["group"]
        u["weighed"] = s + 1 + sum(x.get("gate") is not None for x in units[:s + 1])
    ends = [s for s, u in enumerate(units) if u["end"]]
    scored, masked, p_ready = k.sem("scored"), k.sem("masked"), k.sem("p_ready")
    weight_steps, scaled, turned, copied = k.sem("weight_steps"), [k.sem("p_scaled_pool"), k.sem("p_scaled_dve")], k.sem("p_turned"), [k.sem("p_copied_dve"), k.sem("p_copied_act")]
    mixed, out_ready = k.sem("pv_mixed"), k.sem("out_ready")
    LAG_W, LAG_T, LAG_V = 1, 3, 4
    with nc.sbuf_tensor(k.unique("masked"), [P, 3, S], F32) as sm, nc.sbuf_tensor(k.unique("probs"), [P, 4, S], F32) as pr, \
            nc.sbuf_tensor(k.unique("probsT"), [P, 2, TB, P], F32) as pt, nc.sbuf_tensor(k.unique("rowneg"), [P, n], F32) as rn, \
            nc.sbuf_tensor(k.unique("rowsum"), [P, n], F32) as rs, nc.sbuf_tensor(k.unique("weight"), [P, n], F32) as wt, \
            nc.Block() as block:
        widths = [u["k"].shape[1] for u in units]
        pieces = [[(a, min(P, w - a)) for a in range(0, w, P)] for w in widths]

        @block.tensor
        def _(pe):
            for t in range(n + LAG_V):
                if t < n:
                    u = units[t]
                    if t >= 4:
                        pe.wait_ge(*masked.at(t - 3))
                    nc.tensor.matmul(k.pl[:, t % 4, 0:widths[t]], u["q"], u["k"], start=True, stop=True)\
                        .then_inc(*scored.inc())
                if 0 <= t - LAG_T < n:
                    s = t - LAG_T
                    pe.wait_ge(*scaled[s % 2].at(s // 2 + 1))
                    if s >= 2:
                        pe.wait_ge(*copied[s % 2].at(s // 2))
                    for b, (a, w) in enumerate(pieces[s]):
                        m = nc.tensor.transpose(k.pm[0:w, s % 2, P * b:P * b + P], pr[:, s % 4, a:a + w], k.ident)
                    m.then_inc(*turned.inc())
                if 0 <= t - LAG_V < n:
                    s = t - LAG_V
                    u = units[s]
                    r = slice(HD * u["half"], HD * u["half"] + HD)
                    pe.wait_ge(*copied[s % 2].at(s // 2 + 1))
                    if u["group"] >= 2:
                        pe.wait_ge(*out_ready.at(u["group"] - 1))
                    for b, (a, w) in enumerate(pieces[s]):
                        m = nc.tensor.matmul(k.pm[r, 2 + u["group"] % 2, 0:P], u["v"](b), pt[0:w, s % 2, b, :],
                                             start=u["first"] and b == 0, stop=u["last"] and b == len(pieces[s]) - 1)
                    m.then_inc(*mixed.inc())

        def copy(eng, s, e):
            ps = pieces[s]
            w = ps[-1][1]
            eng.wait_ge(*turned.at(s + 1))
            if s >= 2:
                eng.wait_ge(*mixed.at(s - 1))
            dst, src = pt[0:w, s % 2, 0:len(ps), :], k.pm[0:w, s % 2, 0:P * len(ps)].rearrange("p (b q) -> p b q", q=P)
            if e == 0:
                nc.vector.tensor_copy(dst, src).then_inc(*copied[0].inc())
            else:
                nc.scalar.activation(dst, src, ACT.Copy).then_inc(*copied[1].inc())

        def weigh(eng, s):
            eng.wait_ge(*weight_steps.at(units[s]["weighed"]))
            p = pr[:, s % 4, 0:widths[s]]
            (nc.vector if s % 2 else nc.gpsimd).tensor_scalar(p, p, wt[:, s:s + 1], None, ALU.mult).then_inc(*scaled[s % 2].inc())

        @block.vector
        def _(dve):
            for t in range(n + LAG_V):
                if t < n:
                    u = units[t]
                    dve.wait_ge(*scored.at(t + 1))
                    if t >= 3:
                        dve.wait_ge(*p_ready.at(t - 2))
                    nc.vector.tensor_tensor_reduce(sm[:, t % 3, 0:widths[t]], k.pl[:, t % 4, 0:widths[t]], u["mask"],
                                                   -SCALE, 3e38, ALU.add, ALU.min, rn[:, t:t + 1])\
                        .then_inc(*masked.inc())
                if 0 <= t - LAG_W < n:
                    s = t - LAG_W
                    u = units[s]
                    dve.wait_ge(*p_ready.at(s + 1))
                    nc.vector.reciprocal(wt[:, s:s + 1], rs[:, s:s + 1]).then_inc(*weight_steps.inc())
                    if u.get("gate") is not None:
                        dve.wait_ge(*weight_steps.at(u["weighed"] - 1))
                        nc.vector.tensor_tensor(wt[:, s:s + 1], wt[:, s:s + 1], u["gate"], ALU.mult).then_inc(*weight_steps.inc())
                    if s % 2:
                        weigh(dve, s)
                if 0 <= t - LAG_T < n and (t - LAG_T) % 2 == 0:
                    copy(dve, t - LAG_T, 0)

        @block.gpsimd
        def _(pool):
            for s in range(0, n, 2):
                weigh(pool, s)

        @block.scalar
        def _(act):
            for t in range(n + LAG_V + 1):
                if t < n:
                    act.wait_ge(*masked.at(t + 1))
                    if t >= 4:
                        act.wait_ge(*turned.at(t - 3))
                    nc.scalar.activation(pr[:, t % 4, 0:widths[t]], sm[:, t % 3, 0:widths[t]], ACT.Exp,
                                         bias=rn[:, t:t + 1], scale=-1.0, accum_out=rs[:, t:t + 1])\
                        .then_inc(*p_ready.inc())
                if 0 <= t - LAG_T < n and (t - LAG_T) % 2 == 1:
                    copy(act, t - LAG_T, 1)
                if t - LAG_V - 1 in ends:
                    s = t - LAG_V - 1
                    act.wait_ge(*mixed.at(s + 1))
                    nc.scalar.activation(groups[units[s]["group"]][1], k.pm[:, 2 + units[s]["group"] % 2, 0:P], ACT.Copy)\
                        .then_inc(*out_ready.inc())


def sincos(k, dve, ang, out, tmp, steps):
    nc = k.nc
    C1, C2 = 6.28125, float(np.float32(TWO_PI - 6.28125))
    C3 = float(TWO_PI - 6.28125 - np.float64(np.float32(TWO_PI - 6.28125)))
    MAGIC = 12582912.0
    def step(i):
        i.then_inc(*steps.inc())
        dve.wait_ge(*steps.at(steps.total - steps.base))
    for q in range(2):
        y, t = out[:, q], tmp[:, q]
        step(nc.vector.tensor_scalar(t, ang, 1.0 / TWO_PI, 0.25 * q, ALU.mult, ALU.add))
        step(nc.vector.tensor_scalar(t, t, MAGIC, None, ALU.add))
        step(nc.vector.tensor_scalar(t, t, -MAGIC, None, ALU.add))
        step(nc.vector.scalar_tensor_tensor(out=y, in0=t, scalar=-C1, in1=ang, op0=ALU.mult, op1=ALU.add))
        step(nc.vector.scalar_tensor_tensor(out=y, in0=t, scalar=-C2, in1=y, op0=ALU.mult, op1=ALU.add))
        step(nc.vector.scalar_tensor_tensor(out=y, in0=t, scalar=-C3, in1=y, op0=ALU.mult, op1=ALU.add))
        if q:
            step(nc.vector.tensor_scalar(y, y, TWO_PI / 4, None, ALU.add))
        step(nc.vector.tensor_scalar(y, y, 3.1415925, -3.1415925, ALU.min, ALU.max))


class RopeAndConv:

    def __init__(self, k, ctx, qkv, z, out):
        def sb(name, shape, dt=F32):
            return ctx.enter_context(k.nc.sbuf_tensor(k.unique("rope_" + name), shape, dt))
        self.k, self.qkv, self.z, self.out = k, qkv, z, out
        self.posi, self.posf = sb("posi", [P, TB], I32), sb("posf", [P, TB])
        self.ang, self.angt, self.sc = sb("ang", [P, TB, 32]), sb("angt", [P, 2, TB, 32]), sb("sc", [P, 2, TB, 32])
        self.work = sb("work", [P, 2, S])

    def sync(self, sp):
        sp.dma_start(self.posi[:], self.k.io["positions"][0].rearrange("(b p) -> p b", p=P), allow_slow_non_contiguous=True)\
            .then_inc(*self.k.sem("pos_loaded").dma())

    def vector(self, dve):
        k, posf, ang, sc, steps = self.k, self.posf, self.ang, self.sc, self.k.sem("angle_steps")
        V, M = k.nc.vector, ALU.mult

        def st(i):
            i.then_inc(*steps.inc())
            dve.wait_ge(*steps.at(steps.total - steps.base))

        dve.wait_ge(*k.sem("pos_loaded").dma_at(1))
        st(V.tensor_copy(posf[:], self.posi[:]))
        for b in range(TB):
            st(V.tensor_scalar(ang[:, b, :], k.const("invfreq"), posf[:, b:b + 1], None, M))
        sincos(k, dve, ang[:], sc, self.angt, steps)
        self.angles_stand = steps.total - steps.base
        dve.wait_ge(*k.sem("sines_ready").at(1))
        dve.wait_ge(*k.sem("drained_act").at(4))
        qk = self.qkv[:, :, 0:2 * AW].rearrange("p b (h t c) -> p b h t c", t=2, c=32)
        wa, wb = (self.work[:, n].rearrange("p (h c) -> p h c", c=32) for n in range(2))
        for b in range(TB):
            sn = sc[:, 0, b].unsqueeze(1).broadcast_to([P, 16, 32])
            cs = sc[:, 1, b].unsqueeze(1).broadcast_to([P, 16, 32])
            t1, t2 = qk[:, b, :, 0, :], qk[:, b, :, 1, :]
            V.tensor_tensor(wa, t1, sn, M).then_inc(*steps.inc())
            st(V.tensor_tensor(wb, t2, sn, M))
            V.tensor_tensor(t1, t1, cs, M).then_inc(*steps.inc())
            st(V.tensor_tensor(t2, t2, cs, M))
            V.tensor_tensor(t1, t1, wb, ALU.subtract).then_inc(*steps.inc())
            st(V.tensor_tensor(t2, t2, wa, ALU.add))
        dve.wait_ge(*k.sem("drained_act").at(9))
        cw = k.vec("conv_w").rearrange("p (t n) -> p t n", t=3)
        z, out, cz = self.z, self.out, self.work
        st(V.tensor_tensor(cz[:], z[:, 2:4, :], z[:, 4:6, :], M))
        V.tensor_scalar(out[:, 0, :], cz[:, 0, :], cw[:, 2, 0:1], None, M).then_inc(*steps.inc())
        st(V.tensor_scalar(out[:, 1, :], cz[:, 1, :], cw[:, 2, 1:2], None, M))
        for tap in (1, 0):
            n = S - 2 + tap
            for c in range(2):
                i = V.scalar_tensor_tensor(out=out[:, c, S - n:S], in0=cz[:, c, 0:n], scalar=cw[:, tap, c:c + 1],
                                           in1=out[:, c, S - n:S], op0=M, op1=ALU.add)
                st(i) if c else i.then_inc(*steps.inc())
        st(V.tensor_tensor(out, out, z[:, 0:2, :], M))

    def scalar(self, act, i):
        if i == 2:
            act.wait_ge(*self.k.sem("angle_steps").at(self.angles_stand))
            self.k.nc.scalar.activation(self.sc[:], self.sc[:], ACT.Sin).then_inc(*self.k.sem("sines_ready").inc())

    def tensor(self, pe, i):
        pass


def group_norm_phase(k, x, gain, groups):
    nc = k.nc
    k.phase()
    sq_ready, sum_ready, std_ready, rstd_ready, out = (k.sem("norm_" + s) for s in ("sq", "sum", "std", "rstd", "out"))
    with nc.sbuf_tensor(k.unique("sq"), [P, KD, S], F32) as sq, nc.sbuf_tensor(k.unique("std"), [P, len(groups), S], F32) as std, \
            nc.Block() as block:
        tiles = [i for lo, hi in groups for i in range(lo, hi)]

        @block.scalar
        def _(act):
            for i in tiles:
                nc.scalar.activation(sq[:, i, :], x[:, i, :], ACT.Square).then_inc(*sq_ready.inc())
            for g, (lo, hi) in enumerate(groups):
                act.wait_ge(*sum_ready.at(g + 1))
                nc.scalar.activation(std[:, g, :], k.pm[:, g, :], ACT.Sqrt, bias=k.eps[:, 0:1], scale=1.0 / (P * (hi - lo)))\
                    .then_inc(*std_ready.inc())

        @block.tensor
        def _(pe):
            for g, (lo, hi) in enumerate(groups):
                for i in range(lo, hi):
                    pe.wait_ge(*sq_ready.at(tiles.index(i) + 1))
                    m = nc.tensor.matmul(k.pm[:, g, :], k.ones, sq[:, i, :], start=i == lo, stop=i == hi - 1)
                m.then_inc(*sum_ready.inc())

        @block.vector
        def _(dve):
            for g, (lo, hi) in enumerate(groups):
                dve.wait_ge(*std_ready.at(g + 1))
                nc.vector.reciprocal(std[:, g, :], std[:, g, :]).then_inc(*rstd_ready.inc())
                dve.wait_ge(*rstd_ready.at(g + 1))
                for i in range(lo, hi):
                    nc.vector.scalar_tensor_tensor(out=x[:, i, :], in0=x[:, i, :], scalar=gain[:, i:i + 1], in1=std[:, g, :],
                                                   op0=ALU.mult, op1=ALU.mult).then_inc(*out.inc())


def rwkv_phases(k, z, out, spare):
    nc, io = k.nc, k.io
    ctx = ExitStack()
    with ctx:
        def sb(name, shape):
            return ctx.enter_context(nc.sbuf_tensor(k.unique("rw_" + name), shape, F32))

        kr = sb("kr", [P, 3, 2, S])
        lam = sb("lam", [P, 3, TB, 2])
        tm = sb("tm", [P, TB, 4, RW])
        bonus = sb("bonus", [P, TB, 6])
        gate = sb("gate", [P, TB, RW])
        bh, kh = sb("bh", [P, 3 * S]), sb("kh", [P, 3 * S])
        bhat, khat = (t[:].rearrange("p (i t) -> p i t", t=S) for t in (bh, kh))
        A = z[:].rearrange("p i t -> p (i t)")[:, 0:24 * P].rearrange("p (q t) -> p q t", t=P)
        rwkv_prepare(k, z, kr, bhat, khat, lam, bonus, gate)
        with ExitStack() as products:
            banks = []
            for n, src in enumerate((kr[:, :, 0, :], bhat, khat, z[:, 6:9, 1:S + 1])):
                for i in range(3):
                    banks.append(([src[:, i, P * b:P * b + P] for b in range(TB)], tm[:, :, n, P * i:P * i + P]))
            turn_phase(k, banks)
            AT = products.enter_context(nc.sbuf_tensor(k.unique("rw_AT"), [P, 24, 3, P], F32))
            inverses = ExitStack()
            yx = inverses.enter_context(nc.sbuf_tensor(k.unique("rw_yx"), [P, 24, 2, P], F32))
            k.phase()
            made, masked = k.sem("rw_made"), k.sem("rw_masked")
            with nc.Block() as block:
                @block.tensor
                def _(pe):
                    for q in range(24):
                        h, b = q // 4, q % 4
                        i, p = h // 2, HD * (h % 2)
                        rows, cols = slice(p, p + HD), slice(P * b, P * b + P)
                        if q >= 2:
                            pe.wait_ge(*masked.at(3 * (q - 1)))
                        bank = k.pl[:, 2 * (q % 2), :]
                        nc.tensor.matmul(bank[:, 0:2 * P].rearrange("p (a b) -> p a b", a=2), bhat[rows, i, cols], kr[rows, i, :, cols], start=True, stop=True)
                        nc.tensor.matmul(bank[:, 2 * P:4 * P].rearrange("p (a b) -> p a b", a=2), khat[rows, i, cols], kr[rows, i, :, cols], start=True, stop=True)
                        nc.tensor.matmul(k.pl[:, 2 * (q % 2) + 1, 0:P], kr[rows, i, 0, cols], bhat[rows, i, cols], start=True, stop=True)\
                            .then_inc(*made.inc())

                @block.vector
                def _(dve):
                    for q in range(24):
                        dve.wait_ge(*made.at(q + 1))
                        nc.vector.tensor_tensor(AT[:, q].rearrange("p a b -> p (a b)"), k.pl[:, 2 * (q % 2), P:4 * P], k.const("chunkmask"), ALU.mult)\
                            .then_inc(*masked.inc())
                        nc.vector.tensor_tensor(yx[:, q, 0], k.pl[:, 2 * (q % 2), 0:P], k.const("join1"), ALU.mult).then_inc(*masked.inc())
                        nc.vector.tensor_tensor(A[:, q], k.pl[:, 2 * (q % 2) + 1, 0:P], k.const("below"), ALU.mult).then_inc(*masked.inc())

            invert_phase(k, A, yx, bh[:, 0:8 * P].rearrange("p (a b c) -> p a b c", a=2, b=4))
            wT = z[:].rearrange("p i t -> p (i t)")[:, 24 * P:24 * P + 3 * S].rearrange("p (i t) -> p i t", t=S)
            u = spare.rearrange("p i t -> p (i t)").rearrange("p (b f) -> p b f", f=RW)
            av = bh[:].rearrange("p (b f) -> p b f", f=RW)
            k.phase()
            w_made, w_out, av_made, av_out, u_made, u_out = (k.sem(s) for s in ("rw_w_made", "rw_w_out", "rw_av_made", "rw_av_out", "rw_u_made", "rw_u_out"))
            with nc.Block() as block:
                @block.tensor
                def _(pe):
                    for b in range(TB):
                        if b:
                            pe.wait_ge(*w_out.at(b))
                            pe.wait_ge(*av_out.at(b))
                            pe.wait_ge(*u_out.at(b))
                        for h in range(6):
                            q, i, p = 4 * h + b, h // 2, HD * (h % 2)
                            m = nc.tensor.matmul(k.pl[p:p + HD, 0, P * i:P * i + P], tm[:, b, 0, HD * h:HD * h + HD], yx[:, q, 0, :], start=True, stop=True)
                        m.then_inc(*w_made.inc())
                        for h in range(6):
                            q = 4 * h + b
                            m = nc.tensor.matmul(k.pl[:, 1, HD * h:HD * h + HD], AT[:, q, 1, :], tm[:, b, 3, HD * h:HD * h + HD], start=True, stop=True)
                        m.then_inc(*av_made.inc())
                        pe.wait_ge(*av_out.at(b + 1))
                        for h in range(6):
                            q = 4 * h + b
                            m = nc.tensor.matmul(k.pl[:, 2, HD * h:HD * h + HD], yx[:, q, 0, :], av[:, b, HD * h:HD * h + HD], start=True, stop=True)
                        m.then_inc(*u_made.inc())

                @block.scalar
                def _(act):
                    for b in range(TB):
                        act.wait_ge(*w_made.at(b + 1))
                        nc.scalar.activation(wT[:, :, P * b:P * b + P], k.pl[:, 0, 0:3 * P].rearrange("p (i t) -> p i t", i=3), ACT.Copy).then_inc(*w_out.inc())
                        act.wait_ge(*u_made.at(b + 1))
                        nc.scalar.activation(u[:, b, :], k.pl[:, 2, 0:RW], ACT.Copy).then_inc(*u_out.inc())

                @block.vector
                def _(dve):
                    for b in range(TB):
                        dve.wait_ge(*av_made.at(b + 1))
                        nc.vector.tensor_copy(av[:, b, :], k.pl[:, 1, 0:RW]).then_inc(*av_out.inc())

            inverses.close()
            sa = kh[:, 0:2 * RW].rearrange("p (b f) -> p b f", f=RW)
            st = kh[:, 2 * RW:3 * RW].rearrange("p (b i v) -> p b i v", b=2, v=HD)
            tmp = kh[:, 3 * RW:4 * RW].rearrange("p (b i v) -> p b i v", b=2, v=HD)
            k.phase()
            ws_made, sa_ready, st_made, st_ready, o_made, o_out = (k.sem(s) for s in ("rw_ws_made", "rw_sa_ready", "rw_st_made", "rw_st_ready", "rw_o_made", "rw_o_out"))
            st_sum, zeroed = k.sem("rw_st_sum"), k.sem("rw_zeroed")
            after = HeadNorm(k, products, out, tm, bonus, gate)
            with nc.Block() as block:
                @block.sync
                def _(sp):
                    after.sync(sp)

                @block.tensor
                def _(pe):
                    for b in range(TB):
                        cur = st[:, b % 2]
                        if b == 0:
                            pe.wait_ge(*zeroed.at(1))
                        else:
                            pe.wait_ge(*st_ready.at(b))
                        cols = slice(P * b, P * b + P)
                        for h in (0, 2, 4, 1, 3, 5):
                            i, p = h // 2, HD * (h % 2)
                            m = nc.tensor.matmul(k.pl[:, h % 2, HD * i:HD * i + HD], wT[p:p + HD, i, cols], cur[p:p + HD, i, :], start=True, stop=True)
                        m.then_inc(*ws_made.inc())
                        pe.wait_ge(*sa_ready.at(2 * b + 2))
                        if b < TB - 1:
                            for h in range(6):
                                i, p, hc = h // 2, HD * (h % 2), slice(HD * h, HD * h + HD)
                                nc.tensor.matmul(k.pl[p:p + HD, 2, HD * i:HD * i + HD], tm[:, b, 2, hc], tm[:, b, 3, hc], start=True, stop=False)
                                m = nc.tensor.matmul(k.pl[p:p + HD, 2, HD * i:HD * i + HD], tm[:, b, 1, hc], sa[:, b % 2, hc], start=False, stop=True)
                            m.then_inc(*st_made.inc())
                        if b:
                            pe.wait_ge(*o_out.at(6 * b))
                        for h in (0, 2, 4, 1, 3, 5):
                            i, p, hc, q = h // 2, HD * (h % 2), slice(HD * h, HD * h + HD), 4 * h + b
                            o = k.pm[:, h % 2, HD * i:HD * i + HD]
                            nc.tensor.matmul(o, kr[p:p + HD, i, 1, cols], cur[p:p + HD, i, :], start=True, stop=False)
                            nc.tensor.matmul(o, AT[:, q, 0, :], sa[:, b % 2, hc], start=False, stop=False)
                            m = nc.tensor.matmul(o, AT[:, q, 2, :], tm[:, b, 3, hc], start=False, stop=True)
                        m.then_inc(*o_made.inc())

                @block.gpsimd
                def _(pool):
                    for b in range(TB - 1):
                        after.chunk(pool, nc.gpsimd, b, o_out)

                def parities(t, b):
                    return t[:, b, :].rearrange("p (i e v) -> p e i v", e=2, v=HD)

                @block.vector
                def _(dve):
                    nc.vector.memset(st[:, 0], 0.0).then_inc(*zeroed.inc())
                    dve.wait_ge(*zeroed.at(1))
                    for b in range(TB):
                        dve.wait_ge(*ws_made.at(b + 1))
                        if b >= 2:
                            dve.wait_ge(*o_made.at(b - 1))
                        for e in range(2):
                            nc.vector.scalar_tensor_tensor(out=parities(sa, b % 2)[:, e], in0=k.pl[:, e, 0:3 * HD].rearrange("p (i v) -> p i v", v=HD),
                                                           scalar=-1.0, in1=parities(u, b)[:, e], op0=ALU.mult, op1=ALU.subtract)\
                                .then_inc(*sa_ready.inc())
                        if b < TB - 1:
                            dve.wait_ge(*st_made.at(b + 1))
                            if b:
                                dve.wait_ge(*o_made.at(b))
                            nc.vector.tensor_tensor(tmp[:, 0], st[:, b % 2], k.pl[:, 2, 0:3 * HD].rearrange("p (i v) -> p i v", v=HD), ALU.add).then_inc(*st_sum.inc())
                            dve.wait_ge(*st_sum.at(2 * b + 1))
                            nc.vector.tensor_tensor(tmp[:, 1], tmp[:, 0], lam[:, :, b, 1].unsqueeze(2).broadcast_to([P, 3, HD]), ALU.mult).then_inc(*st_sum.inc())
                            dve.wait_ge(*st_sum.at(2 * b + 2))
                            nc.vector.tensor_tensor(st[:, (b + 1) % 2], tmp[:, 1], lam[:, :, b + 1, 0].unsqueeze(2).broadcast_to([P, 3, HD]), ALU.mult).then_inc(*st_ready.inc())
                        if b:
                            after.invert(dve, b - 1)
                    after.chunk(dve, nc.vector, TB - 1, o_out)

                @block.scalar
                def _(act):
                    for b in range(TB):
                        act.wait_ge(*o_made.at(b + 1))
                        after.scalar(act, b, lambda h: k.pm[:, h % 2, HD * (h // 2):HD * (h // 2) + HD], o_out)


def rwkv_prepare(k, z, kr, bh, kh, lam, bonus, gate):
    nc, io = k.nc, k.io
    ctx = ExitStack()
    with ctx:
        def sb(name, shape):
            return ctx.enter_context(nc.sbuf_tensor(k.unique("rp_" + name), shape, F32))
        w2a2 = sb("w2a2", [P, RW])
        g2 = sb("g2", [P, RW])
        vec = k.vec("rw_w0_2", 15).rearrange("p (n i) -> p n i", i=3)
        la = sb("la", [P, S])
        gl = sb("gl", [P, S])
        ld = sb("ld", [P, 3, S])
        L = sb("L", [P, 3, S])
        a = sb("a", [P, 3, S])
        kk = sb("kk", [P, 3, S])
        e = sb("e", [P, 3, S])
        t1 = sb("t1", [P, 3, S])
        k.phase()
        loaded, lora, gates_made, sig, scan = (k.sem(s) for s in ("rp_loaded", "rp_lora", "rp_made", "rp_sig", "rp_scan"))
        step, astep, pstep = k.sem("rp_step"), k.sem("rp_act_step"), k.sem("rp_pe_step")
        r, kz = z[:, 0:3, 1:S + 1], z[:, 3:6, 1:S + 1]
        with nc.Block() as block:
            @block.sync
            def _(sp):
                sp.dma_start(w2a2[0:64], io["rw_w2_2"][0]).then_inc(*loaded.dma())
                sp.dma_start(w2a2[64:128], io["rw_a2_2"][0]).then_inc(*loaded.dma())
                sp.dma_start(g2[:], io["rw_g2_2"][0]).then_inc(*loaded.dma())

            @block.tensor
            def _(pe):
                pe.wait_ge(*loaded.dma_at(3))
                pe.wait_ge(*lora.at(2))
                for i in range(3):
                    nc.tensor.matmul(k.pl[:, i, :], w2a2[0:64, P * i:P * i + P], la[0:64], start=True, stop=True)
                    m = nc.tensor.matmul(k.pm[:, i, :], w2a2[64:128, P * i:P * i + P], la[64:128], start=True, stop=True)
                m.then_inc(*gates_made.inc())
                pe.wait_ge(*sig.at(6))
                pe.wait_ge(*step.at(4))
                for i in range(3):
                    m = nc.tensor.matmul(k.pl[:, i, :], k.const("headsum"), t1[:, i, :], start=True, stop=True)
                m.then_inc(*pstep.inc())
                pe.wait_ge(*lora.at(3))
                for b in range(TB):
                    m = nc.tensor.matmul(k.pm[:, b, 0:RW], gl[:, P * b:P * b + P], g2[:], start=True, stop=True)
                m.then_inc(*pstep.inc())
                pe.wait_ge(*astep.at(7))
                pe.wait_ge(*step.at(16))
                for i in range(3):
                    for b in range(TB):
                        m = nc.tensor.matmul(k.pm[:, 0, 6 * b + 2 * i:6 * b + 2 * i + 2], t1[:, i, P * b:P * b + P], k.const("headcol"), start=True, stop=True)
                m.then_inc(*pstep.inc())

            @block.scalar
            def _(act):
                nc.scalar.activation(la[0:64], z[0:64, 9, 1:S + 1], ACT.Tanh).then_inc(*lora.inc())
                nc.scalar.activation(la[64:128], z[64:128, 9, 1:S + 1], ACT.Copy).then_inc(*lora.inc())
                nc.scalar.activation(gl[:], z[:, 10, 1:S + 1], ACT.Sigmoid).then_inc(*lora.inc())
                act.wait_ge(*gates_made.at(1))
                for i in range(3):
                    nc.scalar.activation(ld[:, i, :], k.pl[:, i, :], ACT.Sigmoid, bias=vec[:, 0, i:i + 1]).then_inc(*sig.inc())
                for i in range(3):
                    nc.scalar.activation(a[:, i, :], k.pm[:, i, :], ACT.Sigmoid, bias=vec[:, 1, i:i + 1]).then_inc(*sig.inc())
                act.wait_ge(*pstep.at(1))
                act.wait_ge(*step.at(4))
                nc.scalar.activation(t1[:], k.pl[:, 0:3, :], ACT.Sqrt).then_inc(*astep.inc())
                act.wait_ge(*k.sem("rp_L").at(2))
                act.wait_ge(*k.sem("rp_kk").at(1))
                nc.scalar.activation(e[:], L[:], ACT.Exp).then_inc(*astep.inc())
                act.wait_ge(*k.sem("rp_use").at(1))
                nc.scalar.activation(e[:], L[:], ACT.Exp, scale=-1.0).then_inc(*astep.inc())
                act.wait_ge(*k.sem("rp_prev").at(1))
                nc.scalar.activation(t1[:], t1[:], ACT.Exp).then_inc(*astep.inc())
                act.wait_ge(*k.sem("rp_L").at(3))
                nc.scalar.activation(lam[:], lam[:], ACT.Exp).then_inc(*astep.inc())
                act.wait_ge(*pstep.at(2))
                nc.scalar.activation(gate[:, 0:2, :], k.pm[:, 0:2, 0:RW], ACT.Copy).then_inc(*astep.inc())
                nc.scalar.activation(gate[:, 2:4, :], k.pm[:, 2:4, 0:RW], ACT.Copy).then_inc(*astep.inc())
                act.wait_ge(*pstep.at(3))
                nc.scalar.activation(bonus[:].rearrange("p b h -> p (b h)"), k.pm[:, 0, 0:24], ACT.Copy).then_inc(*astep.inc())

            @block.vector
            def _(dve):
                DEC = -float(np.exp(-0.5))
                for i in range(3):
                    nc.vector.tensor_scalar(kk[:, i, :], kz[:, i, :], vec[:, 2, i:i + 1], None, ALU.mult).then_inc(*step.inc())
                dve.wait_ge(*step.at(3))
                nc.vector.tensor_tensor(t1[:], kk[:], kk[:], ALU.mult).then_inc(*step.inc())
                dve.wait_ge(*sig.at(6))
                nc.vector.tensor_scalar(ld[:], ld[:], DEC, None, ALU.mult).then_inc(*scan.inc())
                dve.wait_ge(*scan.at(1))
                for i in range(3):
                    nc.vector.tensor_tensor_scan(L[:, i, :], k.const("first"), ld[:, i, :], 0.0, ALU.mult, ALU.add).then_inc(*scan.inc())
                dve.wait_ge(*scan.at(4))
                Lc = L[:].rearrange("p i (b t) -> p (i b) t", t=P)
                lm = lam[:].rearrange("p i b e -> p (i b) e")
                nc.vector.tensor_copy(lm[:, :, 0], Lc[:, :, P // 2]).then_inc(*k.sem("rp_L").inc())
                dve.wait_ge(*k.sem("rp_L").at(1))
                nc.vector.tensor_tensor(Lc, Lc, lm[:, :, 0:1].broadcast_to([P, 12, P]), ALU.subtract).then_inc(*k.sem("rp_L").inc())
                dve.wait_ge(*astep.at(1))
                nc.vector.tensor_scalar(t1[:], t1[:], 1e-12, None, ALU.max).then_inc(*step.inc())
                dve.wait_ge(*step.at(5))
                nc.vector.reciprocal(t1[:], t1[:]).then_inc(*step.inc())
                dve.wait_ge(*step.at(6))
                nc.vector.tensor_tensor(kk[:], kk[:], t1[:], ALU.mult).then_inc(*k.sem("rp_kk").inc())
                dve.wait_ge(*k.sem("rp_kk").at(1))
                dve.wait_ge(*k.sem("rp_L").at(2))
                nc.vector.tensor_tensor(t1[:], L[:], ld[:], ALU.subtract).then_inc(*k.sem("rp_prev").inc())
                nc.vector.tensor_copy(lm[:, :, 1], Lc[:, :, P - 1]).then_inc(*k.sem("rp_L").inc())
                dve.wait_ge(*k.sem("rp_L").at(3))
                dve.wait_ge(*astep.at(2))
                nc.vector.tensor_tensor(kr[:, :, 1, :], r, e[:], ALU.mult).then_inc(*k.sem("rp_use").inc())
                for i in range(3):
                    nc.vector.tensor_scalar(kh[:, i, :], a[:, i, :], -1.0, vec[:, 3, i:i + 1], ALU.add, ALU.mult).then_inc(*step.inc())
                dve.wait_ge(*step.at(9))
                nc.vector.scalar_tensor_tensor(out=kh[:], in0=kh[:], scalar=1.0, in1=kz, op0=ALU.add, op1=ALU.mult).then_inc(*step.inc())
                nc.vector.tensor_tensor(bh[:], kk[:], a[:], ALU.mult).then_inc(*step.inc())
                dve.wait_ge(*step.at(11))
                dve.wait_ge(*astep.at(4))
                nc.vector.tensor_tensor(kr[:, :, 0, :], kk[:], t1[:], ALU.mult).then_inc(*step.inc())
                nc.vector.tensor_tensor(bh[:], bh[:], e[:], ALU.mult).then_inc(*step.inc())
                dve.wait_ge(*step.at(12))
                for i in range(3):
                    nc.vector.scalar_tensor_tensor(out=t1[:, i, :], in0=r[:, i, :], scalar=vec[:, 4, i:i + 1], in1=kh[:, i, :],
                                                   op0=ALU.mult, op1=ALU.mult).then_inc(*step.inc())
                dve.wait_ge(*step.at(16))
                nc.vector.tensor_tensor(kh[:], kh[:], e[:], ALU.mult).then_inc(*step.inc())


def invert_phase(k, A, yx, tt):
    nc = k.nc
    k.phase()
    first, t_made, t_out, p_made, joined = (k.sem(s) for s in ("inv_first", "inv_t_made", "inv_t_out", "inv_p_made", "inv_joined"))
    with nc.Block() as block:
        sizes = [2, 4, 8, 16, 32, 64]
        rounds = [(b, g) for b in sizes for g in range(6)]

        def batch(t, g):
            return t[:, 4 * g:4 * g + 4]

        @block.vector
        def _(dve):
            j1t = k.const("join1T").unsqueeze(1).broadcast_to([P, 4, P])
            idb = k.ident.unsqueeze(1).broadcast_to([P, 4, P])
            for g in range(6):
                nc.vector.tensor_tensor(batch(yx, g)[:, :, 1], batch(A, g), j1t, ALU.mult).then_inc(*first.inc())
            for g in range(6):
                dve.wait_ge(*first.at(g + 1))
                for e in range(2):
                    nc.vector.tensor_tensor(batch(yx, g)[:, :, e], idb, batch(yx, g)[:, :, e], ALU.subtract).then_inc(*joined.inc())

            def out_t(n):
                b, g = rounds[n]
                dve.wait_ge(*t_made.at(n + 1))
                if n >= 2:
                    dve.wait_ge(*p_made.at(n - 1))
                if b == P // 2:
                    nc.vector.tensor_copy(tt[0:b, n % 2, :, b:P], k.pm[0:b, n % 2, :].rearrange("p (a b) -> p a b", a=4)[:, :, b:P]).then_inc(*t_out.inc())
                    return
                m = k.const(f"join{b}").unsqueeze(1).broadcast_to([P, 4, P])
                nc.vector.tensor_tensor(tt[:, n % 2], k.pm[:, n % 2, :].rearrange("p (a b) -> p a b", a=4), m, ALU.mult).then_inc(*t_out.inc())

            def out_p(n):
                b, g = rounds[n]
                dve.wait_ge(*p_made.at(n + 1))
                if b == P // 2:
                    new = batch(yx, g)[0:b, :, 0, b:P]
                    nc.vector.tensor_tensor(new, new, k.pl[0:b, 2 * (n % 2), 0:4 * b].rearrange("p (a b) -> p a b", a=4), ALU.subtract).then_inc(*joined.inc())
                    return
                nc.vector.tensor_tensor(batch(yx, g), batch(yx, g), k.pl[:, 2 * (n % 2):2 * (n % 2) + 2, :].rearrange("p h (a e b) -> p (h a) e b", e=2, a=2), ALU.subtract).then_inc(*joined.inc())

            for n in range(len(rounds) + 1):
                if n < len(rounds):
                    out_t(n)
                if n:
                    out_p(n - 1)

        @block.tensor
        def _(pe):
            def first_product(n):
                b, g = rounds[n]
                pe.wait_ge(*joined.at(2 * g + 2 if b == 2 else 12 + n - 6 + 1))
                if n >= 2:
                    pe.wait_ge(*t_out.at(n - 1))
                for a in range(4):
                    q = 4 * g + a
                    if b == P // 2:
                        m = nc.tensor.matmul(k.pm[0:b, n % 2, P * a + b:P * a + P], A[:, q, 0:b], yx[:, q, 0, b:P], start=True, stop=True)
                        continue
                    m = nc.tensor.matmul(k.pm[:, n % 2, P * a:P * a + P], A[:, q], yx[:, q, 0], start=True, stop=True)
                m.then_inc(*t_made.inc())

            def second_product(n):
                b, g = rounds[n]
                pe.wait_ge(*t_out.at(n + 1))
                if n >= 2:
                    pe.wait_ge(*joined.at(12 + n - 1))
                for a in range(4):
                    q = 4 * g + a
                    if b == P // 2:
                        m = nc.tensor.matmul(k.pl[0:b, 2 * (n % 2), b * a:b * a + b], yx[0:b, q, 1, 0:b], tt[0:b, n % 2, a, b:P], start=True, stop=True)
                        continue
                    bank = k.pl[:, 2 * (n % 2) + a // 2, :]
                    at = 2 * P * (a % 2)
                    nc.tensor.matmul(bank[:, at:at + P], yx[:, q, 1], tt[:, n % 2, a], start=True, stop=True)
                    m = nc.tensor.matmul(bank[:, at + P:at + 2 * P], tt[:, n % 2, a], yx[:, q, 1], start=True, stop=True)
                m.then_inc(*p_made.inc())

            for n in range(len(rounds) + 1):
                if n < len(rounds):
                    first_product(n)
                if n:
                    second_product(n - 1)


class HeadNorm:

    def __init__(self, k, ctx, o, tm, bonus, gate):
        def sb(name, shape):
            return ctx.enter_context(k.nc.sbuf_tensor(k.unique("hn_" + name), shape, F32))
        self.k, self.o, self.tm, self.bonus, self.gate = k, o, tm, bonus, gate
        self.gw, self.sq, self.mean, self.extra = sb("gw", [P, 2, RW]), sb("sq", [P, 6, HD]), sb("mean", [P, TB, 2, 6]), sb("extra", [P, RW])
        self.loaded, self.step, self.centred, self.var, self.std, self.inv = (k.sem("hn_" + s) for s in ("loaded", "step", "centred", "var", "std", "inv"))

    def sync(self, sp):
        for n, name in enumerate(("rw_gn_w_2", "rw_gn_b_2")):
            sp.dma_start(self.gw[:, n, :], self.k.io[name].broadcast_to([P, RW])).then_inc(*self.loaded.dma())

    def chunk(self, eng, ns, b, o_out):
        step, mean = self.step, self.mean[:, b]
        ob = self.o[:, b, :]
        oh = ob.rearrange("p (h v) -> p h v", v=HD)

        def done(i):
            i.then_inc(*step.inc())
            eng.wait_ge(*step.at(step.total - step.base))

        def per_head(t):
            return t.unsqueeze(2).broadcast_to([P, 6, HD])

        if b == 0:
            eng.wait_ge(*self.loaded.dma_at(2))
        elif b == TB - 1:
            eng.wait_ge(*step.at(step.total - step.base))
        done(ns.tensor_tensor(self.extra[:].rearrange("p (h v) -> p h v", v=HD), self.tm[:, b, 3, :].rearrange("p (h v) -> p h v", v=HD),
                              per_head(self.bonus[:, b, :]), ALU.mult))
        eng.wait_ge(*o_out.at(6 * b + 6))
        done(ns.tensor_scalar(mean[:, 0, :], mean[:, 0, :], 1.0 / HD, None, ALU.mult))
        ns.tensor_tensor(oh, oh, per_head(mean[:, 0, :]), ALU.subtract).then_inc(*self.centred.inc())
        if b == TB - 1:
            self.invert(eng, b)
        eng.wait_ge(*self.inv.at(b + 1))
        done(ns.tensor_tensor(oh, oh, per_head(mean[:, 1, :]), ALU.mult))
        done(ns.tensor_tensor(ob, ob, self.gw[:, 0, :], ALU.mult))
        done(ns.tensor_tensor(ob, ob, self.gw[:, 1, :], ALU.add))
        done(ns.tensor_tensor(ob, ob, self.extra[:], ALU.add))
        done(ns.tensor_tensor(ob, ob, self.gate[:, b, :], ALU.mult))

    def scalar(self, act, b, source, o_out):
        nc, mean = self.k.nc, self.mean[:, b]
        oh = self.o[:, b, :].rearrange("p (h v) -> p h v", v=HD)
        for h in range(6):
            nc.scalar.activation(oh[:, h], source(h), ACT.Copy, accum_out=mean[:, 0, h:h + 1]).then_inc(*o_out.inc())
        act.wait_ge(*self.centred.at(b + 1))
        for h in range(6):
            nc.scalar.activation(self.sq[:, h], oh[:, h], ACT.Square, accum_out=mean[:, 1, h:h + 1]).then_inc(*self.var.inc())
        act.wait_ge(*self.var.at(6 * b + 6))
        nc.scalar.activation(mean[:, 1, :], mean[:, 1, :], ACT.Sqrt, bias=self.k.eps[:, 1:2], scale=1.0 / HD).then_inc(*self.std.inc())

    def invert(self, dve, b):
        dve.wait_ge(*self.std.at(b + 1))
        v = self.mean[:, b, 1, :]
        self.k.nc.vector.reciprocal(v, v).then_inc(*self.inv.inc())


def compress_buffers(k, ctx):
    def sb(name, shape):
        return ctx.enter_context(k.nc.sbuf_tensor(k.unique("cp_" + name), shape, F32))
    return {name: dict(raw=sb("raw", [CMP_LEN // 2, P]), w1=sb("w1", [P, CMP_LEN // 2, P]), w2=sb("w2", [P, HD])) for name in "kv"}


def load_compress(k, sp, buffers):
    loaded = k.sem("cp_loaded")
    for name, b in buffers.items():
        sp.dma_start(b["raw"][:], k.io[f"cmp_pe_{name}_2"][0].rearrange("(l e) d -> l (e d)", e=2)).then_inc(*loaded.dma())
        w1 = k.io[f"cmp_w1_{name}_2"][0].rearrange("(l p) n -> p l n", p=P)
        for l in (0, CMP_LEN // 4):
            sp.dma_start(b["w1"][:, l:l + CMP_LEN // 4, :], w1[:, l:l + CMP_LEN // 4, :]).then_inc(*loaded.dma())
        sp.dma_start(b["w2"][:], k.io[f"cmp_w2_{name}_2"][0]).then_inc(*loaded.dma())


def compress_phase(k, buffers, kc, vc, kcmp, vcmp):
    nc = k.nc
    k.phase()
    pe_turned, pe_out, doubled, windows, hid_made, hid_out, out_made, out = (k.sem("cp_" + s) for s in (
        "pe_turned", "pe_out", "doubled", "windows", "hid_made", "hid_out", "out_made", "out"))
    L2 = CMP_LEN // 2
    with nc.sbuf_tensor(k.unique("cp_pe"), [P, 2, L2], F32) as pe_t, nc.sbuf_tensor(k.unique("cp_win"), [P, 2, L2, 2, NC], F32) as win, \
            nc.sbuf_tensor(k.unique("cp_hid"), [P, 2, 2, NC], F32) as hid, nc.Block() as block:
        @block.tensor
        def _(pe):
            pe.wait_ge(*k.sem("cp_loaded").at(0))
            for n, b in enumerate(buffers.values()):
                nc.tensor.transpose(k.pm[:, n, 0:L2], b["raw"][:], k.ident[0:L2, 0:L2]).then_inc(*pe_turned.inc())
            for n, x in enumerate((kc, vc)):
                for g in range(2):
                    m = nc.tensor.matmul(k.pl[:, 2 * n + g, :], k.const(f"twice{g}"), x, start=True, stop=True)
                m.then_inc(*doubled.inc())
            for n, b in enumerate(buffers.values()):
                pe.wait_ge(*windows.at(4 * n + 4))
                for l in range(L2):
                    m = nc.tensor.matmul(k.pm[:, 2 + n, 0:2 * NC], b["w1"][:, l, :], win[:, n, l].rearrange("p g n -> p (g n)"), start=l == 0, stop=l == L2 - 1)
                m.then_inc(*hid_made.inc())
            for n, b in enumerate(buffers.values()):
                pe.wait_ge(*hid_out.at(n + 1))
                for g in range(2):
                    if n:
                        m = nc.tensor.matmul(k.pm[0:NC, 1, HD * g:HD * g + HD], hid[:, n, g, :], b["w2"][:], start=True, stop=True)
                    else:
                        m = nc.tensor.matmul(k.pm[HD * g:HD * g + HD, 0, 0:NC], b["w2"][:], hid[:, n, g, :], start=True, stop=True)
                m.then_inc(*out_made.inc())

        @block.scalar
        def _(act):
            for n in range(2):
                act.wait_ge(*hid_made.at(n + 1))
                nc.scalar.activation(hid[:, n], k.pm[:, 2 + n, 0:2 * NC].rearrange("p (g n) -> p g n", g=2), ACT.Gelu_apprx_tanh).then_inc(*hid_out.inc())

        @block.vector
        def _(dve):
            for n in range(2):
                dve.wait_ge(*pe_turned.at(n + 1))
                nc.vector.tensor_copy(pe_t[:, n], k.pm[:, n, 0:L2]).then_inc(*pe_out.inc())
            dve.wait_ge(*pe_out.at(2))
            for n in range(2):
                dve.wait_ge(*doubled.at(n + 1))
                for odd in range(2):
                    r = slice(HD * odd, HD * odd + HD)
                    x = k.pl[r, 2 * n:2 * n + 2, :].rearrange("p g (n l e) -> p e l g n", e=2, l=CMP_STRIDE // 2)[:, odd]
                    for half in range(2):
                        lo = CMP_STRIDE // 2 * half
                        code = pe_t[r, n, lo:lo + CMP_STRIDE // 2].unsqueeze(2).unsqueeze(3).broadcast_to([HD, CMP_STRIDE // 2, 2, NC])
                        nc.vector.tensor_tensor(win[r, n, lo:lo + CMP_STRIDE // 2], x[:, :, :, half:half + NC], code, ALU.add).then_inc(*windows.inc())
            dve.wait_ge(*out_made.at(1))
            nc.vector.tensor_copy(kcmp, k.pm[:, 0, 0:NC]).then_inc(*out.inc())
            dve.wait_ge(*out_made.at(2))
            nc.vector.tensor_copy(vcmp[0:NC].rearrange("p g d -> p (g d)"), k.pm[0:NC, 1, 0:P]).then_inc(*out.inc())


class S5:

    def __init__(self, k, ctx, spare):
        self.k = k

        def sb(name, shape):
            return ctx.enter_context(k.nc.sbuf_tensor(k.unique("s5_" + name), shape, F32))
        self.par = sb("par", [P, 16, 8])
        self.bt = sb("bt", [P, 2, 2, P])
        self.ct = sb("ct", [P, 2, 2, P])
        self.rot = [sb("rot", [P, 8, S]), spare]

    def work_buffers(self, ctx):
        def sb(name, shape):
            return ctx.enter_context(self.k.nc.sbuf_tensor(self.k.unique("s5_" + name), shape, F32))
        self.scs, self.tmp = sb("sincos", [P, 2, 8]), sb("tmp", [P, 2, 8])
        self.braw, self.bx = sb("braw", [P, 2, 8, 16]), sb("bx", [P, 2, 8, 2, 16])
        self.craw, self.btmp = sb("craw", [P, 2, 2, 2, HD]), sb("btmp", [P, 2, 8, 16])
        self.rt, self.pw = sb("rt", [P, 4, P]), sb("pw", [P, 2, 2, 8])
        self.marks = {}

    def sync(self, sp):
        k, io = self.k, self.k.io
        loaded = k.sem("s5_loaded")
        for g in range(2):
            row = io["s5_log_dt_2"].rearrange("o (i g) -> g o i", g=2)[g]
            sp.dma_start(self.par[HD * g:HD * g + HD, 2, :], row.broadcast_to([HD, 8]), allow_slow_non_contiguous=True)\
                .then_inc(*loaded.dma())
        for n, name in enumerate(("s5_b_re_2", "s5_b_im_2")):
            for g in range(2):
                sp.dma_start(self.braw[HD * g:HD * g + HD, n], io[name][0].rearrange("(i g) p c -> g p i c", g=2)[g]).then_inc(*loaded.dma())
        for n, name in enumerate(("s5_c_re_2", "s5_c_im_2")):
            for g in range(2):
                sp.dma_start(self.craw[:, n, :, g, :], io[name][0].rearrange("(h q) c p -> (q c) h p", h=2)).then_inc(*loaded.dma())

    LOADS = 10

    def vector(self, dve):
        k, par, scs, rot, rt, pw = self.k, self.par, self.scs, self.rot, self.rt, self.pw
        braw, bx, craw, btmp, marks = self.braw, self.bx, self.craw, self.btmp, self.marks
        nc, step, loaded, sines, exps = k.nc, k.sem("s5_step"), k.sem("s5_loaded"), k.sem("s5_sines"), k.sem("s5_exps")
        turned, emptied = k.sem("s5_turned"), k.sem("s5_emptied")

        def st(i):
            i.then_inc(*step.inc())
            dve.wait_ge(*step.at(step.total - step.base))
        V = nc.vector
        M, Ad, Su = ALU.mult, ALU.add, ALU.subtract
        def q(n):
            return (k.vec("s5_lam_re_2"), k.vec("s5_lam_im_2"))[n] if n < 2 else par[:, n, :]
        dve.wait_ge(*loaded.dma_at(self.LOADS))
        dve.wait_ge(*exps.at(1))
        st(V.tensor_tensor(q(4), q(1), q(2), M))
        st(V.tensor_tensor(q(3), q(0), q(2), M))
        marks["exp"] = step.total - step.base
        sincos(k, dve, q(4), scs, self.tmp, step)
        marks["sine"] = step.total - step.base
        dve.wait_ge(*sines.at(2))
        sn, cs = scs[:, 0], scs[:, 1]
        st(V.tensor_tensor(q(5), q(3), cs, M))
        st(V.tensor_tensor(q(6), q(3), sn, M))
        st(V.tensor_tensor(q(7), q(0), q(0), M))
        st(V.tensor_tensor(q(8), q(1), q(1), M))
        st(V.tensor_tensor(q(7), q(7), q(8), Ad))
        st(V.reciprocal(q(7), q(7)))
        st(V.tensor_scalar(q(8), q(5), -1.0, None, Ad))
        st(V.tensor_tensor(q(9), q(8), q(0), M))
        st(V.tensor_tensor(q(10), q(6), q(1), M))
        st(V.tensor_tensor(q(9), q(9), q(10), Ad))
        st(V.tensor_tensor(q(9), q(9), q(7), M))
        st(V.tensor_tensor(q(10), q(6), q(0), M))
        st(V.tensor_tensor(q(11), q(8), q(1), M))
        st(V.tensor_tensor(q(10), q(10), q(11), Su))
        st(V.tensor_tensor(q(10), q(10), q(7), M))
        def over_c(n):
            return q(n).unsqueeze(2).broadcast_to([P, 8, 16])
        st(V.memset(bx[:], 0.0))
        for part in range(2):
            st(V.tensor_tensor(btmp[:, 0], braw[:, part], over_c(9), M))
            st(V.tensor_tensor(btmp[:, 1], braw[:, 1 - part], over_c(10), M))
            for g in range(2):
                r = slice(HD * g, HD * g + HD)
                st(V.tensor_tensor(bx[r, part, :, g, :], btmp[r, 0], btmp[r, 1], Ad if part else Su))
        for part in range(2):
            for g in range(2):
                st(V.tensor_scalar(craw[:, part, :, g, :], craw[:, part, :, g, :], k.const("pairsel")[:, g:g + 1],
                                   -1.0 if part else 1.0, M, M))
        marks["bc"] = step.total - step.base
        dve.wait_ge(*turned.at(1))
        V.tensor_copy(self.bt[:], k.pm[:, 0, :].rearrange("p (a h s) -> p a h s", a=2, h=2)).then_inc(*emptied.inc())
        V.tensor_copy(self.ct[:], k.pm[:, 1, :].rearrange("p (a h s) -> p a h s", a=2, h=2)).then_inc(*emptied.inc())
        st(V.memset(rot[0][:, :, 0:1], 1.0))
        st(V.memset(rot[1][:, :, 0:1], 0.0))
        st(V.tensor_copy(pw[:, 0, 0], cs))
        st(V.tensor_copy(pw[:, 0, 1], sn))
        n, cur = 1, 0
        while n < S:
            size, cols = max(1, min(8, P // n)), min(n, P)
            for i, a in [(i, a) for i in range(0, 8, size) for a in range(0, n, cols)]:
                t = slice(i, i + size)
                ra = [rt[:, x, 0:size * cols].rearrange("p (i n) -> p i n", n=cols) for x in range(4)]
                pr = pw[:, cur, 0, t].unsqueeze(2).broadcast_to([P, size, cols])
                pi = pw[:, cur, 1, t].unsqueeze(2).broadcast_to([P, size, cols])
                c0, s0 = rot[0][:, t, a:a + cols], rot[1][:, t, a:a + cols]
                V.tensor_tensor(ra[0], c0, pr, M).then_inc(*step.inc())
                V.tensor_tensor(ra[1], s0, pi, M).then_inc(*step.inc())
                V.tensor_tensor(ra[2], c0, pi, M).then_inc(*step.inc())
                st(V.tensor_tensor(ra[3], s0, pr, M))
                V.tensor_tensor(rot[0][:, t, n + a:n + a + cols], ra[0], ra[1], Su).then_inc(*step.inc())
                st(V.tensor_tensor(rot[1][:, t, n + a:n + a + cols], ra[2], ra[3], Ad))
            n *= 2
            if n < S:
                o = pw[:, cur]
                V.tensor_tensor(rt[:, 0, 0:8], o[:, 0], o[:, 0], M).then_inc(*step.inc())
                V.tensor_tensor(rt[:, 1, 0:8], o[:, 1], o[:, 1], M).then_inc(*step.inc())
                st(V.scalar_tensor_tensor(out=pw[:, 1 - cur, 1], in0=o[:, 0], scalar=2.0, in1=o[:, 1], op0=M, op1=M))
                st(V.tensor_tensor(pw[:, 1 - cur, 0], rt[:, 0, 0:8], rt[:, 1, 0:8], Su))
                cur = 1 - cur

    def scalar(self, act, i):
        k, par, scs = self.k, self.par, self.scs
        step, sines, exps = k.sem("s5_step"), k.sem("s5_sines"), k.sem("s5_exps")
        if i == 1:
            act.wait_ge(*k.sem("s5_loaded").dma_at(self.LOADS))
            k.nc.scalar.activation(par[:, 2, :], par[:, 2, :], ACT.Exp).then_inc(*exps.inc())
        elif i == 2:
            act.wait_ge(*step.at(self.marks["exp"]))
            k.nc.scalar.activation(par[:, 3, :], par[:, 3, :], ACT.Exp).then_inc(*sines.inc())
        elif i == 3:
            act.wait_ge(*step.at(self.marks["sine"]))
            k.nc.scalar.activation(scs[:], scs[:], ACT.Sin).then_inc(*sines.inc())

    def tensor(self, pe, i):
        if i != 5:
            return
        k = self.k
        pe.wait_ge(*k.sem("s5_step").at(self.marks["bc"]))
        for part in range(2):
            for h in range(2):
                at = P * (2 * part + h)
                k.nc.tensor.transpose(k.pm[:, 0, at:at + P], self.bx[:, part, 4 * h:4 * h + 4].rearrange("p i g c -> p (i g c)"), k.ident)
                m = k.nc.tensor.transpose(k.pm[:, 1, at:at + P], self.craw[:, part, h].rearrange("p g s -> p (g s)"), k.ident)
        m.then_inc(*k.sem("s5_turned").inc())


def s5_phase(k, s5, u, out, z, mu, compress):
    nc = k.nc
    par, bt, ct, rot, dsk = s5.par, s5.bt, s5.ct, s5.rot, k.vec("s5_d_2")
    with ExitStack() as ctx:
        def sb(name, shape):
            return ctx.enter_context(nc.sbuf_tensor(k.unique("s5_" + name), shape, F32))
        bu = sb("bu", [P, 4, S])
        wg = sb("wglu", [P, 2, 2 * CW])
        before, keep = sb("before", [P, 2, S]), sb("keep", [P, 11])
        w = sb("w", [P, 2, 2, S])
        sc = sb("scan", [P, 2, 2, S])
        back, yg = sb("back", [P, 4, S]), sb("y", [P, 2, S])
        k.phase()
        glu_loaded, kept, before_ready, shifted = k.sem("s5_glu_loaded"), k.sem("shift_kept"), k.sem("shift_before"), k.sem("shifted")
        made, prod, scanned, back_re, back_im, read = (k.sem("s5_" + s) for s in ("made", "prod", "scanned", "back_re", "back_im", "read"))
        in_re, in_im, state_re, state_im = (k.sem("s5_" + s) for s in ("in_re", "in_im", "state_re", "state_im"))
        ysum, ygelu, glu_made, gate_ready, out_done = (k.sem("s5_" + s) for s in ("ysum", "ygelu", "glu_made", "gate_ready", "out_done"))
        with nc.Block() as block:
            @block.sync
            def _(sp):
                sp.dma_start(wg[:], k.io["s5_w_glu_2"][0].rearrange("(h p) n -> p h n", p=P)).then_inc(*glu_loaded.dma())
                load_compress(k, sp, compress)

            @block.tensor
            def _(pe):
                def project(i):
                    h, r = i // 4, slice(32 * (i % 4), 32 * (i % 4) + 32)
                    if i >= 2:
                        pe.wait_ge(*prod.at(4 * (i - 1)))
                    for part in range(2):
                        m = nc.tensor.matmul(k.pl[:, 2 * (i % 2) + part, :], bt[r, part, h, :], u[r, h, :], start=True, stop=True)
                    m.then_inc(*made.inc())

                def mix(i):
                    h, r = i // 4, slice(32 * (i % 4), 32 * (i % 4) + 32)
                    pe.wait_ge(*state_re.at(i + 1))
                    pe.wait_ge(*state_im.at(i + 1))
                    for part in range(2):
                        m = nc.tensor.matmul(k.pm[r, h, :], ct[:, part, h, r], w[:, i % 2, part, :], start=part == 0, stop=part == 1)
                    m.then_inc(*read.inc())
                project(0)
                project(1)
                for i in range(8):
                    if i < 6:
                        project(i + 2)
                    mix(i)
                pe.wait_ge(*glu_loaded.dma_at(1))
                pe.wait_ge(*ygelu.at(2))
                for c in range(4):
                    for h in range(2):
                        m = nc.tensor.matmul(k.pl[:, c, :], wg[:, h, P * c:P * c + P], yg[:, h, :], start=h == 0, stop=h == 1)
                m.then_inc(*glu_made.inc())

            @block.vector
            def _(dve):
                V, M, Ad, Su = nc.vector, ALU.mult, ALU.add, ALU.subtract

                def shift(i):
                    dve.wait_ge(*before_ready.at(i + 1))
                    V.scalar_tensor_tensor(out=z[:, i, 1:S + 1], in0=z[:, i, 1:S + 1], scalar=keep[:, i:i + 1],
                                           in1=before[:, i % 2, :], op0=M, op1=Ad).then_inc(*shifted.inc())

                V.tensor_scalar(keep[:], mu, -1.0, 1.0, M, Ad).then_inc(*kept.inc())
                dve.wait_ge(*kept.at(1))
                for i in range(3):
                    shift(i)
                for i in range(9):
                    if i:
                        shift(i + 2)
                    if i < 8:
                        c, s = rot[0][:, i, :], rot[1][:, i, :]
                        dve.wait_ge(*made.at(i + 1))
                        re, im = k.pl[:, 2 * (i % 2), :], k.pl[:, 2 * (i % 2) + 1, :]
                        if i:
                            dve.wait_ge(*in_re.at(i))
                            dve.wait_ge(*in_im.at(i))
                        V.tensor_tensor(bu[:, 2], im, c, M).then_inc(*prod.inc())
                        V.tensor_tensor(bu[:, 3], re, s, M).then_inc(*prod.inc())
                        V.tensor_tensor(bu[:, 0], re, c, M).then_inc(*prod.inc())
                        V.tensor_tensor(bu[:, 1], im, s, M).then_inc(*prod.inc())
                    if i:
                        c, s, e = rot[0][:, i - 1, :], rot[1][:, i - 1, :], (i - 1) % 2
                        dve.wait_ge(*scanned.at(2 * i))
                        V.tensor_tensor(back[:, 0], sc[:, e, 0], c, M).then_inc(*back_re.inc())
                        V.tensor_tensor(back[:, 1], sc[:, e, 1], s, M).then_inc(*back_re.inc())
                        dve.wait_ge(*back_re.at(2 * i))
                        V.tensor_tensor(w[:, e, 0], back[:, 0], back[:, 1], Su).then_inc(*state_re.inc())
                    if i < 8:
                        dve.wait_ge(*prod.at(4 * i + 4))
                        if i >= 2:
                            dve.wait_ge(*read.at(i - 1))
                        V.tensor_tensor(w[:, i % 2, 0], bu[:, 0], bu[:, 1], Ad).then_inc(*in_re.inc())
                        dve.wait_ge(*in_re.at(i + 1))
                        if i >= 2:
                            dve.wait_ge(*back_im.at(2 * (i - 1)))
                            dve.wait_ge(*back_re.at(2 * (i - 1)))
                        mag = par[:, 3, i:i + 1].broadcast_to([P, S])
                        V.tensor_tensor_scan(sc[:, i % 2, 0], mag, w[:, i % 2, 0], 0.0, M, Ad).then_inc(*scanned.inc())
                        dve.wait_ge(*in_im.at(i + 1))
                        V.tensor_tensor_scan(sc[:, i % 2, 1], mag, w[:, i % 2, 1], 0.0, M, Ad).then_inc(*scanned.inc())
                dve.wait_ge(*read.at(8))
                for h in range(2):
                    V.scalar_tensor_tensor(out=yg[:, h], in0=u[:, h, :], scalar=dsk[:, h:h + 1], in1=k.pm[:, h, :], op0=M, op1=Ad).then_inc(*ysum.inc())
                dve.wait_ge(*gate_ready.at(2))
                for h in range(2):
                    V.tensor_tensor(out[:, h, :], k.pl[:, h, :], bu[:, h], M).then_inc(*out_done.inc())

            @block.gpsimd
            def _(pool):
                V, M, Ad, Su = nc.gpsimd, ALU.mult, ALU.add, ALU.subtract
                for i in range(9):
                    if i < 8:
                        pool.wait_ge(*prod.at(4 * i + 2))
                        if i >= 2:
                            pool.wait_ge(*read.at(i - 1))
                        V.tensor_tensor(w[:, i % 2, 1], bu[:, 2], bu[:, 3], Su).then_inc(*in_im.inc())
                    if i:
                        c, s, e = rot[0][:, i - 1, :], rot[1][:, i - 1, :], (i - 1) % 2
                        pool.wait_ge(*scanned.at(2 * i))
                        if i > 1:
                            pool.wait_ge(*state_im.at(i - 1))
                        V.tensor_tensor(back[:, 2], sc[:, e, 0], s, M).then_inc(*back_im.inc())
                        V.tensor_tensor(back[:, 3], sc[:, e, 1], c, M).then_inc(*back_im.inc())
                        pool.wait_ge(*back_im.at(2 * i))
                        V.tensor_tensor(w[:, e, 1], back[:, 2], back[:, 3], Ad).then_inc(*state_im.inc())

            @block.scalar
            def _(act):
                for i in range(11):
                    if i >= 2:
                        act.wait_ge(*shifted.at(i - 1))
                    nc.scalar.activation(before[:, i % 2, :], z[:, i, 0:S], ACT.Copy, scale=mu[:, i:i + 1]).then_inc(*before_ready.inc())
                for h in range(2):
                    act.wait_ge(*ysum.at(h + 1))
                    nc.scalar.activation(yg[:, h], yg[:, h], ACT.Gelu_apprx_tanh).then_inc(*ygelu.inc())
                act.wait_ge(*glu_made.at(1))
                act.wait_ge(*in_im.at(8))
                act.wait_ge(*in_re.at(8))
                for h in range(2):
                    nc.scalar.activation(bu[:, h], k.pl[:, 2 + h, :], ACT.Sigmoid).then_inc(*gate_ready.inc())


def gate_phase(k, g0, x, out, e):
    nc = k.nc
    k.phase()
    todo = split_ahead(k, NSLABS)
    x_hi, x_lo = k.sem("x_hi"), k.sem("x_lo")
    gate_ready, prod_ready, added = k.sem("plg_gate"), k.sem("plg_prod"), k.sem("plg_added")
    with nc.sbuf_tensor(k.unique("plg"), [P, 2, 2, S], F32) as ga, nc.sbuf_tensor(k.unique("x_hi"), [P, KD, S], F32R) as xh, \
            nc.sbuf_tensor(k.unique("x_lo"), [P, KD, S], F32R) as xl, nc.Block() as block:
        parts = (xh, xl)

        @block.sync
        def _(sp):
            for g in range(g0 + 2, g0 + 4):
                issue_slab(k, sp, g)

        @block.tensor
        def _(pe):
            for i in range(4):
                g = g0 + i
                j = g % 2
                use_slab(k, pe, j, g // 2)
                if i >= 2:
                    pe.wait_ge(*gate_ready.at(i - 1))
                w = [slab_view(k, j, a) for a in range(2)]
                for c in range(2):
                    for q in range(KD):
                        if i == 0 and c == 0:
                            pe.wait_ge(*x_lo.at(q + 1))
                        m = product(nc, k.pl[:, 2 * j + c, :], [([w[a][:, q, P * c:P * c + P] for a in range(2)],
                                                                 [parts[a][:, q, :] for a in range(2)])], q == 0, q == KD - 1)
                m.then_inc(k.slab_done[j], 1)

        @block.scalar
        def _(act):
            split_x(k, act, None, x, parts, x_hi, x_lo)
            for i in range(-2, 4):
                g = g0 + i
                j = g % 2
                if g + 2 in todo:
                    hi_of_slab(k, act, j, g // 2 + 1, loaded_value(g + 2))
                if i >= 0:
                    act.wait_ge(k.slab_done[j], g // 2 + 1)
                    if i >= 2:
                        act.wait_ge(*prod_ready.at(i - 1))
                    nc.scalar.activation(ga[:, j], k.pl[:, 2 * j:2 * j + 2, :], ACT.Sigmoid).then_inc(*gate_ready.inc())

        @block.vector
        def _(dve):
            split_x(k, None, dve, x, parts, x_hi, x_lo)
            for i in range(4):
                t = slice(2 * i, 2 * i + 2)
                dve.wait_ge(*gate_ready.at(i + 1))
                nc.vector.tensor_tensor(e[:, t, :], e[:, t, :], ga[:, (g0 + i) % 2], ALU.mult).then_inc(*prod_ready.inc())
                dve.wait_ge(*prod_ready.at(i + 1))
                nc.vector.tensor_tensor(out[:, t, :], e[:, t, :], x[:, t, :], ALU.add).then_inc(*added.inc())

        @block.gpsimd
        def _(pool):
            for g in todo:
                lo_of_slab(k, pool, g % 2, g // 2)


def two_blocks(nc, io, out, probe=None):
    def see(name, ap):
        if probe:
            probe(name, ap)
    ctx = ExitStack()
    with ctx:
        k = Kit(nc, ctx, io)

        def sb(name, shape, dt=F32):
            return ctx.enter_context(nc.sbuf_tensor(name, shape, dt))

        k.tables[0] = sb("table", [P, k.widths[0]])
        k.ring = sb("ring", [P, 2, SLAB])
        xT, hT = sb("xT", [P, KD, S]), sb("hT", [P, KD, S])
        k.eps = sb("eps", [P, 2])
        k.vecs = sb("vecs", [P, 3 * P])
        k.pl = ctx.enter_context(nc.psum_tensor("pl", [P, 4, 512], F32))
        k.pm = ctx.enter_context(nc.psum_tensor("pm", [P, 4, 512], F32))
        k.slab_loaded = [ctx.enter_context(nc.semaphore(f"slab_loaded{j}")) for j in range(2)]
        k.slab_done = [ctx.enter_context(nc.semaphore(f"slab_done{j}")) for j in range(2)]
        k.slab_hi = [ctx.enter_context(nc.semaphore(f"slab_hi{j}")) for j in range(2)]
        k.slab_lo = [ctx.enter_context(nc.semaphore(f"slab_lo{j}")) for j in range(2)]
        k.split_done = 0
        k.ones, k.ident = k.const("ones"), k.const("ident")
        G = {n: k.vec(n) for n in ("g_pre_mix", "g_mem", "g_post_mix", "g_pre_mlp", "g_post_mlp", "pre_mix_norm_2",
                                   "post_mix_norm_2", "pre_ffn_norm_2", "post_ffn_norm_2")}
        G["mix"] = k.vec("g_attn_out", KD)
        gple, mu = k.vec("ple_norm_2"), k.vec("shift_mu_2")

        k.phase()
        eps_set, consts_loaded, rows_turned, rows_out = (k.sem(s) for s in ("eps_set", "consts_loaded", "rows_turned", "rows_out"))
        with nc.sbuf_tensor(k.unique("rows"), [P, 3, P], F32) as rows, nc.Block() as block:
            @block.gpsimd
            def _(pool):
                nc.gpsimd.memset(k.eps[:, 0:1], EPS).then_inc(*eps_set.inc())
                nc.gpsimd.memset(k.eps[:, 1:2], GN_EPS).then_inc(*eps_set.inc())
                nc.gpsimd.memset(rows[:], 0.0).then_inc(*eps_set.inc())

            @block.sync
            def _(sp):
                sp.dma_start(k.tables[0][:], io["table"]).then_inc(*consts_loaded.dma())
                sp.wait_ge(*eps_set.at(3))
                for name, n in VECTORS:
                    at, flat = k.vec_at[name], io[name]
                    while len(flat.shape) > 1:
                        flat = flat.rearrange("a b -> (a b)") if len(flat.shape) == 2 else flat.rearrange("a b c -> (a b) c")
                    flat = flat.rearrange("(n p) -> n p", p=P)
                    done = 0
                    while done < n:
                        r, c = (at + done) % P, (at + done) // P
                        m = min(n - done, P - r)
                        sp.dma_start(rows[r:r + m, c, :], flat[done:done + m]).then_inc(*consts_loaded.dma())
                        done += m

            @block.tensor
            def _(pe):
                pe.wait_ge(*consts_loaded.at(consts_loaded.total - consts_loaded.base))
                for r in range(3):
                    m = nc.tensor.transpose(k.pm[:, 0, P * r:P * r + P], rows[:, r, :], k.ident)
                m.then_inc(*rows_turned.inc())

            @block.vector
            def _(dve):
                dve.wait_ge(*rows_turned.at(1))
                nc.vector.tensor_copy(k.vecs[:], k.pm[:, 0, 0:3 * P]).then_inc(*rows_out.inc())

        splitting = ExitStack()
        splitting.enter_context(k.splitting())
        with nc.sbuf_tensor(k.unique("qkv"), [P, TB, 3 * AW], F32) as qkv, nc.sbuf_tensor(k.unique("cz6"), [P, 6, S], F32) as cz6, \
                nc.sbuf_tensor(k.unique("qx"), [P, 2, 2, S], F32) as qx, nc.sbuf_tensor(k.unique("kx"), [P, 2, NM], F32) as kx, \
                nc.sbuf_tensor(k.unique("vx"), [P, 2, XW], F32) as vx:
            def padded(q, i):
                return q[0:HD, 0, i, :], q[HD:P, 1, i, :]

            def other_halves(q):
                return q[HD:P, 0], q[0:HD, 1]

            with nc.sbuf_tensor(k.unique("memT"), [P, KD, NM], F32) as memT:
                with nc.sbuf_tensor(k.unique("xin"), [P, TB, D], F32) as xin, nc.sbuf_tensor(k.unique("memin"), [P, 2, D], F32) as memin:
                    banks = [([xin[:, b, P * f:P * f + P] for b in range(TB)], xT[:, f, :]) for f in range(KD)]
                    banks += [([memin[:, b, P * f:P * f + P] for b in range(2)], memT[:, f, :]) for f in range(KD)]
                    turn_phase(k, banks, load=[(xin[:], io["x"][0].rearrange("(b p) d -> p b d", p=P)),
                                               (memin[:], io["mem"][0].rearrange("(b p) d -> p b d", p=P))], stream=(0, 1))
                norm_phase(k, xT, hT, G["g_pre_mix"], ahead=2)
                norm_phase(k, memT, memT, G["g_mem"], n=NM)
                slabs = [dict(kind="tokens", to=qkv[:, :, 256 * i:256 * i + 256]) for i in range(6)]
                slabs += [dict(kind="features", to=lambda c, i=i: cz6[:, 2 * i + c, :]) for i in range(3)]
                slabs += [dict(kind="features", to=lambda c: padded(qx, c))]
                slabs += [dict(kind="features", to=lambda c: kx[:, c, :], source=1)]
                slabs += [dict(kind="tokens", to=vx, source=1)]
                with ExitStack() as work:
                    beside = RopeAndConv(k, work, qkv, cz6, hT[:, 4:6, :])
                    product_phase(k, IN1, slabs, [(hT, KD, S), (memT, KD, NM)], beside=beside, zero=other_halves(qx))
            see("qkv", qkv[:].rearrange("p b f -> p (b f)"))
            with nc.sbuf_tensor(k.unique("qT"), [P, 2, 4, S], F32) as qT, nc.sbuf_tensor(k.unique("kT"), [P, 4, S], F32) as kT:
                turn_phase(k, [([qkv[:, b, P * f:P * f + P] for b in range(TB)], padded(qT, f) if f < 4 else kT[:, f - 4, :]) for f in range(8)],
                           zero=other_halves(qT))
                groups = []
                for i in range(4):
                    for b in range(TB):
                        w = P * (b + 1)
                        units = [dict(q=qT[:, e, i, P * b:P * b + P], k=kT[:, i, 0:w], mask=k.const("band")[:, S - w:S], half=e,
                                      v=lambda a, h=2 * i + e: qkv[:, a, 2 * AW + HD * h:2 * AW + HD * h + HD]) for e in range(2)]
                        groups.append((units, hT[:, i, P * b:P * b + P]))
                for i in range(2):
                    for b in range(TB):
                        units = [dict(q=qx[:, e, i, P * b:P * b + P], k=kx[:, i, :], mask=k.const("nomask"), half=e,
                                      v=lambda a, h=2 * i + e: vx[:, a, HD * h:HD * h + HD]) for e in range(2)]
                        groups.append((units, hT[:, 6 + i, P * b:P * b + P]))
                attend(k, groups)
            group_norm_phase(k, hT, G["mix"], [(0, 4), (4, 6), (6, 8)])
        see("mix", hT[:].rearrange("p b f -> p (b f)"))
        with nc.sbuf_tensor(k.unique("yT"), [P, KD, S], F32) as yT:
            product_phase(k, WO1, [dict(kind="features", to=lambda c, i=i: yT[:, 2 * i + c, :]) for i in range(4)], [(hT, KD, S)])
            norm_phase(k, yT, None, G["g_post_mix"], add=xT, then=(hT, G["g_pre_mlp"]), ahead=2)
            see("x_mix", xT[:].rearrange("p b f -> p (b f)"))
            ffn1_phase(k, FFN1, hT, yT)
            norm_phase(k, yT, None, G["g_post_mlp"], add=xT, then=(hT, G["pre_mix_norm_2"]))
            see("x_1", xT[:].rearrange("p b f -> p (b f)"))

        splitting.close()

        with nc.sbuf_tensor(k.unique("z"), [P, 11, S + 1], F32) as z:
            with nc.sbuf_tensor(k.unique("q2"), [P, 2, 3, S], F32) as q2, nc.sbuf_tensor(k.unique("kv2"), [P, 4, S], F32) as kv2, \
                    nc.sbuf_tensor(k.unique("v2"), [P, TB, 256], F32) as v2, nc.sbuf_tensor(k.unique("u5"), [P, 2, S], F32) as u5, \
                    nc.sbuf_tensor(k.unique("gl2"), [P, TB, 18], F32) as gl2:
                tiles = [z[:, n, 1:S + 1] for n in range(11)] + [padded(q2, n) for n in range(3)] + [kv2[:, n, :] for n in range(4)]
                slabs = [dict(kind="features", to=lambda c, i=i: tiles[2 * i + c]) for i in range(9)]
                slabs += [dict(kind="tokens", to=v2)]
                slabs += [dict(kind="features", to=lambda c: u5[:, c, :])]
                slabs += [dict(kind="tokens", to=gl2, width=18)]
                k.phase()
                zeroed = k.sem("z_zeroed")
                with nc.Block() as block:
                    @block.gpsimd
                    def _(pool):
                        nc.gpsimd.memset(z[:, :, 0:1], 0.0).then_inc(*zeroed.inc())
                with nc.sbuf_tensor(k.unique("kcmp"), [P, NC], F32) as kcmp, nc.sbuf_tensor(k.unique("vcmp"), [NC, 2, HD], F32) as vcmp:
                    with ExitStack() as early:
                        s5 = S5(k, early, hT)
                        with k.splitting(), ExitStack() as work:
                            s5.work_buffers(work)
                            product_phase(k, IN2, slabs, [(hT, KD, S)], beside=s5, zero=other_halves(q2))
                        compress = compress_buffers(k, early)
                        s5_phase(k, s5, u5, hT[:, 6:8, :], z, mu, compress)
                        see("z", z[:].rearrange("p b f -> p (b f)"))
                        see("s5", hT[:, 6:8, :].rearrange("p b f -> p (b f)"))
                        compress_phase(k, compress, kv2[:, 0, :], kv2[:, 1, :], kcmp[:], vcmp)
                    with nc.sbuf_tensor(k.unique("nsa_table"), [P, k.widths[1]], F32) as k.tables[1]:
                        k.phase()
                        sig, cut, table_loaded = k.sem("nsa_gate"), k.sem("nsa_gate_cut"), k.sem("nsa_table_loaded")
                        with nc.Block() as block:
                            @block.sync
                            def _(sp):
                                sp.dma_start(k.tables[1][:], io["nsa_table"]).then_inc(*table_loaded.dma())
                                sp.wait_ge(*table_loaded.dma_at(1))

                            @block.scalar
                            def _(act):
                                nc.scalar.activation(gl2[:], gl2[:], ACT.Sigmoid).then_inc(*sig.inc())

                            @block.vector
                            def _(dve):
                                dve.wait_ge(*sig.at(1))
                                c = gl2[:, 0, :].rearrange("p (h n) -> p h n", n=3)[:, :, 0]
                                nc.vector.tensor_scalar(c, c, k.const("anycmp"), None, ALU.mult).then_inc(*cut.inc())
                        groups = []
                        for j in range(3):
                            for b in range(TB):
                                units, w = [], P * (b + 1)
                                for branch in range(3):
                                    for half in range(2):
                                        h = 2 * j + half
                                        e = h // 3
                                        un = dict(q=q2[:, e, h % 3, P * b:P * b + P], half=half, gate=gl2[:, b, 3 * h + branch:3 * h + branch + 1])
                                        if branch == 0:
                                            at = NC * (6 * b + h)
                                            un.update(k=kcmp[:], mask=k.const("cmp")[:, at:at + NC], v=lambda a, e=e: vcmp[:, e, :])
                                        else:
                                            un.update(k=kv2[:, 1 + branch, 0:w], mask=k.const(f"causal{h}")[:, S - w:S],
                                                      v=lambda a, e=e, n=branch - 1: v2[:, a, P * n + HD * e:P * n + HD * e + HD])
                                        units.append(un)
                                groups.append((units, hT[:, 3 + j, P * b:P * b + P]))
                        attend(k, groups)
                        see("nsa", hT[:, 3:6, :].rearrange("p b f -> p (b f)"))
            with nc.sbuf_tensor(k.unique("y3"), [P, TB, RW], F32) as y3:
                rwkv_phases(k, z, y3, hT[:, 0:3, :])
                turn_phase(k, [([y3[:, b, P * f:P * f + P] for b in range(TB)], hT[:, f, :]) for f in range(3)])
        see("mix2", hT[:].rearrange("p b f -> p (b f)"))
        with k.splitting(), nc.sbuf_tensor(k.unique("yT2"), [P, KD, S], F32) as yT:
            product_phase(k, WO2, [dict(kind="features", to=lambda c, i=i: yT[:, 2 * i + c, :]) for i in range(4)], [(hT, KD, S)])
            norm_phase(k, yT, None, G["post_mix_norm_2"], add=xT, then=(hT, G["pre_ffn_norm_2"]), ahead=2)
            see("h_mix", xT[:].rearrange("p b f -> p (b f)"))
            ffn2_phase(k, FFN2, hT, yT)
            with nc.sbuf_tensor(k.unique("eT"), [P, KD, S], F32) as eT:
                with nc.sbuf_tensor(k.unique("pin"), [P, TB, PLE], F32) as pin, nc.sbuf_tensor(k.unique("pT"), [P, 2, S], F32) as pT:
                    turn_phase(k, [([pin[:, b, P * f:P * f + P] for b in range(TB)], pT[:, f, :]) for f in range(2)],
                               load=[(pin[:], io["p_2"][0, 0].rearrange("(b p) d -> p b d", p=P))])
                    ple_phase(k, pT, eT)
                norm_phase(k, eT, eT, gple)
                norm_phase(k, yT, None, G["post_ffn_norm_2"], add=xT)
                see("h_ffn", xT[:].rearrange("p b f -> p (b f)"))
                gate_phase(k, GATEW, xT, hT, eT)
        with nc.sbuf_tensor(k.unique("xout"), [P, TB, D], F32) as xout:
            banks = []
            for b in range(TB):
                for half in range(2):
                    banks.append(([hT[:, 4 * half + f, P * b:P * b + P] for f in range(4)], xout[:, b, 512 * half:512 * half + 512]))
            turn_phase(k, banks)
            k.phase()
            stored = k.sem("stored")
            with nc.Block() as block:
                @block.sync
                def _(sp):
                    sp.dma_start(out[0].rearrange("(b p) d -> p b d", p=P), xout[:]).then_inc(*stored.dma())
                    sp.wait_ge(*stored.dma_at(1))


def ple_phase(k, pT, eT):
    nc = k.nc
    k.phase()
    made, out = k.sem("ple_made"), [k.sem("ple_out_act"), k.sem("ple_out_dve")]
    x_hi, x_lo = k.sem("x_hi"), k.sem("x_lo")
    with nc.sbuf_tensor(k.unique("p_hi"), [P, 2, S], F32R) as ph, nc.sbuf_tensor(k.unique("p_lo"), [P, 2, S], F32R) as pl, \
            nc.Block() as block:
        parts = (ph, pl)
        @block.sync
        def _(sp):
            issue_slab(k, sp, PLEW + 2)

        @block.tensor
        def _(pe):
            w = [slab_view(k, PLEW % 2, a, D, 2) for a in range(2)]
            use_slab(k, pe, PLEW % 2, PLEW // 2)
            pe.wait_ge(*x_lo.at(1))
            for n in range(KD):
                if n >= 4:
                    pe.wait_ge(*out[n % 2].at((n - 4) // 2 + 1))
                m = product(nc, k.pl[:, n % 4, :], [([w[a][:, q, P * n:P * n + P] for a in range(2)],
                                                     [parts[a][:, q, :] for a in range(2)]) for q in range(2)])
                if n < KD - 1:
                    m.then_inc(*made.inc())
            m.then_inc(k.slab_done[PLEW % 2], 1)

        def empty(eng, e):
            for n in range(e, KD, 2):
                if n < KD - 1:
                    eng.wait_ge(*made.at(n + 1))
                else:
                    eng.wait_ge(k.slab_done[PLEW % 2], PLEW // 2 + 1)
                if e == 0:
                    nc.scalar.activation(eT[:, n, :], k.pl[:, n % 4, :], ACT.Copy).then_inc(*out[0].inc())
                else:
                    nc.vector.tensor_copy(eT[:, n, :], k.pl[:, n % 4, :]).then_inc(*out[1].inc())

        @block.scalar
        def _(act):
            nc.scalar.activation(ph[:], pT[:], ACT.Copy).then_inc(*x_hi.inc())
            empty(act, 0)

        @block.vector
        def _(dve):
            dve.wait_ge(*x_hi.at(1))
            nc.vector.tensor_tensor(pl[:], pT[:], ph[:].bitcast(F32), ALU.subtract).then_inc(*x_lo.inc())
            empty(dve, 1)



_INS = ["x", "mem", "positions", "g_pre_mix", "g_mem", "w_in", "w_mem_kv", "conv_w", "g_attn_out", "g_conv_out", "g_xattn_out",
        "w_out", "g_post_mix", "g_pre_mlp", "w_up", "w_down", "g_post_mlp", "p_2", "pre_mix_norm_2", "post_mix_norm_2",
        "pre_ffn_norm_2", "post_ffn_norm_2", "w_in_2", "w_out_2", "shift_mu_2", "rw_w0_2", "rw_w2_2", "rw_a0_2", "rw_a2_2",
        "rw_g2_2", "rw_k_k_2", "rw_k_a_2", "rw_r_k_2", "rw_gn_w_2", "rw_gn_b_2", "cmp_pe_k_2", "cmp_pe_v_2", "cmp_w1_k_2",
        "cmp_w2_k_2", "cmp_w1_v_2", "cmp_w2_v_2", "s5_lam_re_2", "s5_lam_im_2", "s5_log_dt_2", "s5_b_re_2", "s5_b_im_2",
        "s5_c_re_2", "s5_c_im_2", "s5_d_2", "s5_w_glu_2", "w_up_2", "conv_w_2", "conv_b_2", "w_down_2", "w_ple_2",
        "ple_norm_2", "w_ple_gate_2"]


def kernel(**inputs):
    import numpy as _np
    import concourse.bacc as _bacc
    from concourse import mybir as _mybir
    from concourse.bass_utils import run_bass_kernel_spmd as _run

    nc = _bacc.Bacc("TRN2", target_bir_lowering=False, num_devices=1)
    arrays, io = {}, {}
    given = {name: _np.ascontiguousarray(inputs[name]) for name in _INS}
    given["table"], given["nsa_table"] = constants()[1]
    for name, a in given.items():
        arrays[f"in_{name}"] = a
        io[name] = nc.dram_tensor(f"in_{name}", a.shape, _mybir.dt.from_np(a.dtype), kind="ExternalInput").ap()
    out = nc.dram_tensor("out_0", (1, S, D), F32, kind="ExternalOutput").ap()
    two_blocks(nc, io, out)
    r = _run(nc, [arrays], core_ids=[0])
    return r.results[0]["out_0"]
```

```python
from contextlib import ExitStack, contextmanager

import numpy as np

import concourse.bass as bass
from concourse import mybir

F32 = mybir.dt.float32
F32R = mybir.dt.float32r
I32 = mybir.dt.int32
ALU = mybir.AluOpType
ACT = mybir.ActivationFunctionType
AX_X = mybir.AxisListType.X

P = 128
S = 512
TB = S // P
D = 1024
KD = D // P
NM = 256
HD = 64
EPS = 1e-6
GN_EPS = 64e-5
NEG = -1e30
SCALE = HD ** -0.5
AW, CW, XW = 512, 256, 256
FF1 = 4096
FF2 = 2816
NT2 = FF2 // P
RW = 384
PLE = 256
CMP_LEN, CMP_STRIDE = 32, 16
NC = (S - CMP_LEN) // CMP_STRIDE + 1
SLAB = 2048
TWO_PI = 2.0 * np.pi


def alibi(n):
    def pow2(m):
        return [2.0 ** (-8.0 / m * (i + 1)) for i in range(m)]
    c = 2 ** int(np.floor(np.log2(n)))
    return pow2(n) if c == n else pow2(c) + pow2(2 * c)[0::2][: n - c]


def constants():
    p = np.arange(P)[:, None]
    c = {}
    c["ident"] = np.eye(P)
    c["ones"] = np.ones((P, P))
    c["headsum"] = (p // HD == np.arange(P)[None] // HD) * 1.0
    rel = p + 384 - np.arange(S)[None]
    mult = ((rel >= 0) & (rel <= 128)) * 1 + ((rel >= 0) & (rel % 4 == 0)) * 1 + ((rel >= 0) & (rel % 16 == 0)) * 1
    c["band"] = np.where(mult > 0, np.log(np.maximum(mult, 1)) / SCALE, NEG / SCALE)
    c["nomask"] = np.zeros((P, NM))
    for h, sl in enumerate(alibi(6)):
        c[f"causal{h}"] = np.where(rel >= 0, -np.float32(sl) * np.maximum(rel, 0) / SCALE, NEG / SCALE)
    t = p[:, :, None] + P * np.arange(TB)[None, :, None]
    dist = t - (np.arange(NC) * CMP_STRIDE + CMP_LEN - 1)[None, None, :]
    c["cmp"] = np.stack([np.where(dist >= 0, -np.float32(sl) * np.abs(dist) / SCALE, NEG / SCALE) for sl in alibi(6)], 2).reshape(P, -1)
    c["anycmp"] = (p >= CMP_LEN - 1) * 1.0
    inv = (1e4 ** (-(np.arange(32) * 2.0 / HD)))[None, :].repeat(P, 0)
    c["invfreq"] = inv
    t = np.arange(P)[None]
    lt, le = (p < t) * 1.0, (p <= t) * 1.0
    c["chunkmask"] = np.concatenate([le, lt, le], 1)
    c["below"] = (p > t) * 1.0
    b = 1
    while b < P:
        c[f"join{b}"] = ((p // (2 * b) == t // (2 * b)) & (p % (2 * b) < b) & (t % (2 * b) >= b)) * 1.0
        b *= 2
    c["join1T"] = c["join1"].T
    for g in range(2):
        c[f"twice{g}"] = (p == HD * g + np.arange(P)[None] % HD) * 1.0
    c["headcol"] = (p // HD == np.arange(2)[None]) * 1.0
    c["pairsel"] = ((p // 16) % 2 == np.arange(2)[None]) * 1.0
    c["first"] = (np.arange(S)[None] % P != 0) * np.ones((P, 1))
    nsa = [name for name in c if name.startswith(("causal", "cmp"))]
    names, tables = {}, []
    for which, group in enumerate(([name for name in c if name not in nsa], nsa)):
        at = 0
        for name in group:
            names[name] = (which, at, c[name].shape[1])
            at += c[name].shape[1]
        tables.append(np.ascontiguousarray(np.concatenate([c[name].astype(np.float32) for name in group], 1)))
    return names, tables


class Tally:

    def __init__(self, sem):
        self.sem, self.base, self.total = sem, 0, 0

    def inc(self, times=1):
        self.total += times
        return self.sem, 1

    def dma(self, times=1):
        self.total += 16 * times
        return self.sem, 16

    def at(self, n):
        return self.sem, self.base + n

    def dma_at(self, n):
        return self.sem, self.base + 16 * n


VECTORS = [("g_pre_mix", 8), ("g_mem", 8), ("g_attn_out", 4), ("g_conv_out", 2), ("g_xattn_out", 2), ("g_post_mix", 8),
           ("g_pre_mlp", 8), ("g_post_mlp", 8), ("pre_mix_norm_2", 8), ("post_mix_norm_2", 8), ("pre_ffn_norm_2", 8),
           ("post_ffn_norm_2", 8), ("ple_norm_2", 8), ("shift_mu_2", 11), ("rw_w0_2", 3), ("rw_a0_2", 3), ("rw_k_k_2", 3),
           ("rw_k_a_2", 3), ("rw_r_k_2", 3), ("s5_d_2", 2), ("conv_w", 6), ("conv_b_2", 44), ("s5_lam_re_2", 8),
           ("s5_lam_im_2", 8), ("conv_w_2", 132)]


class Kit:

    def __init__(self, nc, ctx, io):
        self.nc, self.ctx, self.io, self.tallies = nc, ctx, io, {}
        self.names, tables = constants()
        self.widths = [t.shape[1] for t in tables]
        self.tables = [None, None]
        self.buffers = 0
        self.vec_at, at = {}, 0
        for name, n in VECTORS:
            if n < P and at // P != (at + n - 1) // P:
                at = -(-at // P) * P
            self.vec_at[name] = at
            at += n

    def phase(self):
        for t in self.tallies.values():
            t.base = t.total

    @contextmanager
    def splitting(self):
        with ExitStack() as ctx:
            self.split = [[ctx.enter_context(self.nc.sbuf_tensor(self.unique("slab_part"), [P, SLAB], F32R)) for _ in range(2)]
                          for _ in range(2)]
            yield

    def sem(self, name):
        if name not in self.tallies:
            self.tallies[name] = Tally(self.ctx.enter_context(self.nc.semaphore(name)))
        return self.tallies[name]

    def unique(self, name):
        self.buffers += 1
        return f"{name}_{self.buffers}"

    def vec(self, name, n=None):
        return self.vecs[:, self.vec_at[name]:self.vec_at[name] + (n or dict(VECTORS)[name])]

    def const(self, name):
        which, a, n = self.names[name]
        return self.tables[which][:, a:a + n]



IN1, WO1, FFN1, IN2, WO2, FFN2, PLEW, GATEW, NSLABS = 0, 12, 16, 48, 60, 64, 97, 98, 102
Q2, KC2, KS2, GL2, S52 = 1408, 1792, 2048, 2560, 2578
TURNS1, TURNS2 = FF1 // 512, FF2 // 256


def slab_parts(k, g):
    io = k.io
    slot = k.ring[:, g % 2, :]

    def cols(w, lo, n=256, rows=slice(0, D), at=0, width=256):
        kt = (rows.stop - rows.start) // P
        dst = slot[:, 0:kt * width].rearrange("p (k n) -> p k n", n=width)[:, :, at:at + n]
        return dst, w[rows, lo:lo + n].rearrange("(k p) n -> p k n", p=P)

    def rows_of(w, lo):
        return slot.rearrange("p (k n) -> p k n", n=D), w[lo:lo + 256, :].rearrange("(k p) n -> p k n", p=P)

    if g < 10:
        return [cols(io["w_in"][0], 256 * g)]
    if g < WO1:
        return [cols(io["w_mem_kv"][0], 256 * (g - 10))]
    if g < FFN1:
        return [cols(io["w_out"][0], 256 * (g - WO1))]
    if g < IN2:
        n = g - FFN1
        if n < 2:
            return [cols(io["w_up"][0], 256 * n)]
        return [rows_of(io["w_down"][0], 512 * (TURNS1 - 1) + 256 * (n - 4 * TURNS1 + 2))]
    w = io["w_in_2"][0]
    if g < WO2:
        n = g - IN2
        if n < 5:
            return [cols(w, 256 * n)]
        if n < 7:
            if n == 5:
                return [cols(w, 1280, 128)] + [cols(w, Q2 + HD * h, HD, at=128 + HD * j) for j, h in enumerate((0, 3))]
            return [cols(w, Q2 + HD * h, HD, at=HD * j) for j, h in enumerate((1, 4, 2, 5))]
        if n == 7:
            return [cols(w, KC2)]
        if n == 8:
            return [cols(w, KS2, 128), cols(w, KS2 + 256, 128, at=128)]
        if n == 9:
            return [cols(w, KS2 + 128, 128), cols(w, KS2 + 384, 128, at=128)]
        if n == 10:
            return [cols(w, S52)]
        return [cols(w, GL2, 18, width=18)]
    if g < FFN2:
        return [cols(io["w_out_2"][0], 256 * (g - WO2))]
    if g < PLEW:
        n = g - FFN2
        if n < 2:
            return [cols(io["w_up_2"][0], FF2 * n)]
        return [rows_of(io["w_down_2"][0], 256 * (TURNS2 - 1))]
    if g == PLEW:
        return [cols(io["w_ple_2"][0], 0, D, rows=slice(0, PLE), width=D)]
    return [cols(io["w_ple_gate_2"][0], 256 * (g - GATEW))]


PARTS = {IN2 + 5: 3, IN2 + 6: 4, IN2 + 8: 2, IN2 + 9: 2}


def loaded_value(g):
    return 16 * sum(PARTS.get(q, 1) for q in range(g % 2, g + 1, 2))


def issue_slab(k, sp, g):
    if g >= NSLABS:
        return
    if g >= 2:
        sp.wait_ge(k.slab_lo[g % 2], g // 2)
    for dst, src in slab_parts(k, g):
        sp.dma_start(dst, src).then_inc(k.slab_loaded[g % 2], 16)


def slab_size(g):
    return KD * 18 if g == WO2 - 1 else SLAB


def hi_of_slab(k, act, j, n, loaded, size=SLAB):
    act.wait_ge(k.slab_loaded[j], loaded)
    if not isinstance(n, int) or n > 0:
        act.wait_ge(k.slab_done[j], n)
    k.nc.scalar.activation(k.split[j][0][:, 0:size], k.ring[:, j, 0:size], ACT.Copy).then_inc(k.slab_hi[j], 1)


def lo_of_slab(k, eng, j, n, size=SLAB, ns=None):
    eng.wait_ge(k.slab_hi[j], n + 1)
    (ns or k.nc.gpsimd).tensor_tensor(k.split[j][1][:, 0:size], k.ring[:, j, 0:size], k.split[j][0][:, 0:size].bitcast(F32),
                                      ALU.subtract).then_inc(k.slab_lo[j], 1)


def split_ahead(k, n):
    first = k.split_done
    k.split_done = min(first + n, NSLABS)
    return range(first, k.split_done)


def use_slab(k, pe, j, n):
    pe.wait_ge(k.slab_lo[j], n + 1)


def slab_view(k, j, part, width=256, kt=KD):
    return k.split[j][part][:, 0:kt * width].rearrange("p (k n) -> p k n", n=width)


def product(nc, out, pairs, first=True, last=True):
    for i, (a, b) in enumerate(pairs):
        for n, (x, y) in enumerate(((0, 0), (0, 1), (1, 0))):
            m = nc.tensor.matmul(out, a[x], b[y], start=first and i == 0 and n == 0,
                                 stop=last and i == len(pairs) - 1 and n == 2)
    return m



def halves(dst, src):
    if isinstance(dst, tuple):
        return [(dst[0], src[0:HD]), (dst[1], src[HD:P])]
    return [(dst, src)]


def turn_phase(k, banks, after=None, zero=(), store=None):
    nc = k.nc
    k.phase()
    turned, stored = k.sem("turned"), k.sem("stored")
    emptied = [k.sem("turn_emptied_dve"), k.sem("turn_emptied_act")]
    with nc.Block() as block:
        @block.sync
        def _(sp):
            for n in range(len(banks) // 2 if store else 0):
                for e in range(2):
                    sp.wait_ge(*emptied[e].at(n + 1))
                sp.dma_start(*store(n)).then_inc(*stored.dma())
            if store:
                sp.wait_ge(*stored.dma_at(len(banks) // 2))

        @block.tensor
        def _(pe):
            if after:
                pe.wait_ge(*after.at(0))
            for b, (srcs, dst) in enumerate(banks):
                if b >= 4:
                    pe.wait_ge(*emptied[b % 2].at(b // 2 - 1))
                for j, s in enumerate(srcs):
                    rows, cols = s.shape
                    t = nc.tensor.transpose(k.pm[0:cols, b % 4, j * rows:(j + 1) * rows], s, k.ident[0:rows, 0:rows])
                t.then_inc(*turned.inc())

        def empty(eng, e):
            for b, (srcs, dst) in enumerate(banks):
                if b % 2 != e:
                    continue
                rows, cols = srcs[0].shape
                src = k.pm[0:cols, b % 4, 0:rows * len(srcs)]
                if not isinstance(dst, tuple) and len(dst.shape) == 3:
                    src = src.rearrange("p (a b) -> p a b", a=dst.shape[1])
                eng.wait_ge(*turned.at(b + 1))
                for to, part in halves(dst, src):
                    if e == 0:
                        i = nc.vector.tensor_copy(to, part)
                    else:
                        i = nc.scalar.activation(to, part, ACT.Copy)
                i.then_inc(*emptied[e].inc())

        @block.gpsimd
        def _(pool):
            zeroed = k.sem("halves_zeroed")
            for n, z in enumerate(zero):
                if n:
                    pool.wait_ge(*zeroed.at(n))
                nc.gpsimd.memset(z, 0.0).then_inc(*zeroed.inc())

        @block.vector
        def _(dve):
            empty(dve, 0)

        @block.scalar
        def _(act):
            empty(act, 1)


def norm_phase(k, jobs, ahead=0):
    nc = k.nc
    k.phase()
    sq_ready, pair_ready, sum_ready, std_ready, rstd_ready, scaled, out_ready = (
        k.sem("norm_" + s) for s in ("sq", "pair", "sum", "std", "rstd", "scaled", "out"))
    added = [k.sem("norm_added_pool"), k.sem("norm_added_dve")]
    ahead = split_ahead(k, ahead)
    jobs = [dict(dict(kt=KD, n=S, after=False, out=None, add=None), **j) for j in jobs]
    squares = pairs = scales = adds = 0
    for j in jobs:
        j.update(squares=squares, pairs=pairs, scales=scales, adds=adds)
        squares += j["kt"]
        pairs += 0 if j["after"] else j["kt"] // 2
        if j["add"] is not None:
            scales, adds = scales + j["kt"], adds + j["kt"] // 2
    with ExitStack() as ctx:
        def sb(name, shape):
            return ctx.enter_context(nc.sbuf_tensor(k.unique(name), shape, F32))
        sq = [sb("sq", [P, j["kt"], j["n"]]) for j in jobs]
        std, tmp = sb("std", [P, len(jobs), S]), sb("scaled", [P, 4, S])
        block = ctx.enter_context(nc.Block())

        @block.scalar
        def _(act):
            def root(r):
                j = jobs[r]
                act.wait_ge(*sum_ready.at(r + 1))
                nc.scalar.activation(std[:, r, 0:j["n"]], k.pm[:, r, 0:j["n"]], ACT.Sqrt, bias=k.eps[:, 0:1], scale=1.0 / (P * j["kt"]))\
                    .then_inc(*std_ready.inc())

            for g in ahead:
                hi_of_slab(k, act, g % 2, g // 2, loaded_value(g), slab_size(g))
            for r, j in enumerate(jobs):
                if j["after"]:
                    root(r - 1)
                for i in range(j["kt"]):
                    if j["after"]:
                        act.wait_ge(*added[i % 2].at(jobs[r - 1]["adds"] + i // 2 + 1))
                    nc.scalar.activation(sq[r][:, i, :], j["x"][:, i, :], ACT.Square).then_inc(*sq_ready.inc())
                if r and not j["after"]:
                    root(r - 1)
            root(len(jobs) - 1)

        @block.tensor
        def _(pe):
            for r, j in enumerate(jobs):
                tiles = range(j["kt"]) if j["after"] else range(0, j["kt"], 2)
                for i in tiles:
                    if j["after"]:
                        pe.wait_ge(*sq_ready.at(j["squares"] + i + 1))
                    else:
                        pe.wait_ge(*pair_ready.at(j["pairs"] + i // 2 + 1))
                    m = nc.tensor.matmul(k.pm[:, r, 0:j["n"]], k.ones, sq[r][:, i, :], start=i == 0, stop=i == tiles[-1])
                m.then_inc(*sum_ready.inc())

        @block.vector
        def _(dve):
            def add_pairs(r):
                j = jobs[r]
                for i in range(0, j["kt"], 2):
                    dve.wait_ge(*sq_ready.at(j["squares"] + i + 2))
                    nc.vector.tensor_tensor(sq[r][:, i, :], sq[r][:, i, :], sq[r][:, i + 1, :], ALU.add).then_inc(*pair_ready.inc())

            def scale(r):
                j = jobs[r]
                x, g, rstd = j["x"], j["gain"], std[:, r, 0:j["n"]]
                dve.wait_ge(*std_ready.at(r + 1))
                nc.vector.reciprocal(rstd, rstd).then_inc(*rstd_ready.inc())
                dve.wait_ge(*rstd_ready.at(r + 1))
                for i in range(j["kt"]):
                    to, sem = (j["out"], out_ready) if j["add"] is None else (tmp, scaled)
                    if j["add"] is not None and i >= 4:
                        dve.wait_ge(*added[i % 2].at(j["adds"] + i // 2 - 1))
                    nc.vector.scalar_tensor_tensor(out=to[:, i if j["add"] is None else i % 4, :], in0=x[:, i, :], scalar=g[:, i:i + 1], in1=rstd,
                                                   op0=ALU.mult, op1=ALU.mult).then_inc(*sem.inc())
                    if j["add"] is not None and i % 2:
                        dve.wait_ge(*scaled.at(j["scales"] + i + 1))
                        nc.vector.tensor_tensor(j["add"][:, i, :], j["add"][:, i, :], tmp[:, i % 4, :], ALU.add).then_inc(*added[1].inc())

            for r, j in enumerate(jobs):
                if not j["after"]:
                    add_pairs(r)
            for r in range(len(jobs)):
                scale(r)

        @block.gpsimd
        def _(pool):
            for g in ahead:
                lo_of_slab(k, pool, g % 2, g // 2, slab_size(g))
            for j in jobs:
                if j["add"] is not None:
                    for i in range(0, j["kt"], 2):
                        pool.wait_ge(*scaled.at(j["scales"] + i + 1))
                        nc.gpsimd.tensor_tensor(j["add"][:, i, :], j["add"][:, i, :], tmp[:, i % 4, :], ALU.add).then_inc(*added[0].inc())


def product_phase(k, g0, slabs, sources, beside=None, zero=()):
    nc = k.nc
    k.phase()
    drained = [k.sem("drained_act"), k.sem("drained_dve")]
    x_hi, x_lo = k.sem("x_hi"), k.sem("x_lo")
    n = len(slabs)
    todo = split_ahead(k, g0 + n - k.split_done)
    first = todo[0] == g0
    with ExitStack() as ctx:
        parts = [[ctx.enter_context(nc.sbuf_tensor(k.unique("x_part"), [P, kt, nt], F32R)) for _ in range(2)] for _, kt, nt in sources]
        tiles = [(s, q) for s, (_, kt, _) in enumerate(sources) for q in range(kt)]
        block = ctx.enter_context(nc.Block())

        def empty(eng, e, i):
            s, g = slabs[i], g0 + i
            width, nt = s.get("width", 256), sources[s.get("source", 0)][2]
            j = g % 2
            eng.wait_ge(k.slab_done[j], g // 2 + 1)
            if s["kind"] == "features":
                pairs = [(s["to"](c), k.pl[:, 2 * j + c, 0:nt]) for c in range(2)]
            else:
                pairs = [(s["to"][:, b, :], k.pl[:, 2 * j + b // 2, 256 * (b % 2):256 * (b % 2) + width]) for b in range(nt // P)]
            for dst, src in [h for pair in pairs for h in halves(*pair)]:
                m = nc.scalar.activation(dst, src, ACT.Copy) if e == 0 else nc.vector.tensor_copy(dst, src)
            m.then_inc(*drained[e].inc())

        @block.vector
        def _(dve):
            if first:
                lo_of_slab(k, dve, g0 % 2, g0 // 2, slab_size(g0), nc.vector)
            for t, (s, q) in enumerate(tiles):
                dve.wait_ge(*x_hi.at(t + 1))
                nc.vector.tensor_tensor(parts[s][1][:, q, :], sources[s][0][:, q, :], parts[s][0][:, q, :].bitcast(F32), ALU.subtract)\
                    .then_inc(*x_lo.inc())
            for z in zero:
                nc.vector.memset(z, 0.0).then_inc(*k.sem("halves_zeroed").inc())
            if beside:
                beside.vector(dve)
            for i in range(n):
                if (g0 + i) % 2 and not beside:
                    empty(dve, 1, i)

        @block.sync
        def _(sp):
            if beside:
                beside.sync(sp)
            for g in range(g0 + 2, g0 + n + 2):
                issue_slab(k, sp, g)

        @block.tensor
        def _(pe):
            seen, have = [0, 0], 0
            for i, s in enumerate(slabs):
                g = g0 + i
                j = g % 2
                src, width, kt = parts[s.get("source", 0)], s.get("width", 256), s.get("kt", KD)
                nt = sources[s.get("source", 0)][2]
                at = sum(q for _, q, _ in sources[:s.get("source", 0)])
                w = [slab_view(k, j, a, width, kt) for a in range(2)]
                use_slab(k, pe, j, g // 2)
                if seen[j]:
                    pe.wait_ge(*(drained[0].at(i - 1) if beside else drained[j].at(seen[j])))
                seen[j] += 1
                groups = [(k.pl[:, 2 * j + c, 0:nt], c) for c in range(2)] if s["kind"] == "features" else \
                    [(k.pl[:, 2 * j + b // 2, 256 * (b % 2):256 * (b % 2) + width], b) for b in range(nt // P)]
                for out, c in groups:
                    for q in range(kt):
                        if at + q >= have:
                            have = at + q + 1
                            pe.wait_ge(*x_lo.at(have))
                        cols = slice(P * c, P * c + P)
                        if s["kind"] == "features":
                            a, b = [w[e][:, q, cols] for e in range(2)], [src[e][:, q, 0:nt] for e in range(2)]
                        else:
                            a, b = [src[e][:, q, cols] for e in range(2)], [w[e][:, q, 0:width] for e in range(2)]
                        m = product(nc, out, [(a, b)], first=q == 0, last=q == kt - 1)
                m.then_inc(k.slab_done[j], 1)
                if beside:
                    beside.tensor(pe, i)

        @block.scalar
        def _(act):
            if first:
                hi_of_slab(k, act, g0 % 2, g0 // 2, loaded_value(g0), slab_size(g0))
            for s, q in tiles:
                nc.scalar.activation(parts[s][0][:, q, :], sources[s][0][:, q, :], ACT.Copy).then_inc(*x_hi.inc())
            for i in range(n + 2):
                if g0 + i in todo and (i or not first):
                    hi_of_slab(k, act, (g0 + i) % 2, (g0 + i) // 2, loaded_value(g0 + i), slab_size(g0 + i))
                if i >= 2 and (beside or (g0 + i - 2) % 2 == 0):
                    empty(act, 0, i - 2)
                if beside:
                    beside.scalar(act, i)

        @block.gpsimd
        def _(pool):
            for g in todo[1 if first else 0:]:
                lo_of_slab(k, pool, g % 2, g // 2, slab_size(g))


def split_x(k, act, dve, x, parts, x_hi, x_lo):
    nc = k.nc
    for q in range(KD):
        if act is not None:
            nc.scalar.activation(parts[0][:, q, :], x[:, q, :], ACT.Copy).then_inc(*x_hi.inc())
        else:
            dve.wait_ge(*x_hi.at(q + 1))
            nc.vector.tensor_tensor(parts[1][:, q, :], x[:, q, :], parts[0][:, q, :].bitcast(F32), ALU.subtract).then_inc(*x_lo.inc())


def ffn1_phase(k, g0, x, y):
    nc = k.nc
    k.phase()
    assert k.split_done == g0 + 2
    k.split_done = g0 + 4 * TURNS1
    loops = TURNS1 - 1
    w_up, w_down = k.io["w_up"][0], k.io["w_down"][0]
    x_hi, x_lo = k.sem("x_hi"), k.sem("x_lo")
    relu_ready = [k.sem("relu_a"), k.sem("relu_b")]
    squared = [k.sem("squared_a"), k.sem("squared_b")]
    f_hi, f_lo = [k.sem("f_hi_a"), k.sem("f_hi_b")], [k.sem("f_lo_a"), k.sem("f_lo_b")]
    tile_made, tile_added, y_zeroed = k.sem("down_tile_made"), k.sem("down_tile_added"), k.sem("zeroed")
    with ExitStack() as ctx:
        def sb(name, shape, dt=F32):
            return ctx.enter_context(nc.sbuf_tensor(k.unique(name), shape, dt))
        parts = [sb("x_part", [P, KD, S], F32R) for _ in range(2)]
        relu, f = sb("relu", [P, 2, 2, S]), sb("f", [P, 2, 2, S])
        fp = [sb("f_part", [P, 2, 2, S], F32R) for _ in range(2)]
        block = ctx.enter_context(nc.Block())
        n0 = g0 // 2

        @block.sync
        def _(sp):
            with sp.Fori(0, loops) as i:
                for o in range(4):
                    j, e = o % 2, o // 2
                    sp.wait_ge(k.slab_lo[j], n0 + 1 + e + 2 * i)
                    if j == 0:
                        src = w_up[:, bass.ds(512 * i + 512 + 256 * e, 256)].rearrange("(k p) n -> p k n", p=P)
                        dst = k.ring[:, j, :].rearrange("p (k n) -> p k n", n=256)
                    else:
                        src = w_down[bass.ds(512 * i + 256 * e, 256), :].rearrange("(k p) n -> p k n", p=P)
                        dst = k.ring[:, j, :].rearrange("p (k n) -> p k n", n=D)
                    sp.dma_start(dst, src).then_inc(k.slab_loaded[j], 16)
            for g in range(g0 + 4 * TURNS1 - 2, g0 + 4 * TURNS1 + 2):
                issue_slab(k, sp, g)

        @block.tensor
        def _(pe):
            def up(e, j, n, t, first=False):
                use_slab(k, pe, j, n0 + n)
                if not first:
                    pe.wait_ge(*squared[e].at(t))
                w = [slab_view(k, j, a) for a in range(2)]
                for c in range(2):
                    for q in range(KD):
                        if first and e == 0 and c == 0:
                            pe.wait_ge(*x_lo.at(q + 1))
                        m = product(nc, k.pl[:, 2 * e + c, :], [([w[a][:, q, P * c:P * c + P] for a in range(2)],
                                                                 [parts[a][:, q, :] for a in range(2)])], q == 0, q == KD - 1)
                m.then_inc(k.slab_done[j], 1)

            def down(e, j, n, t, made, times):
                use_slab(k, pe, j, n0 + n)
                pe.wait_ge(*f_lo[e].at(t + 1))
                w = [slab_view(k, j, a, D, 2) for a in range(2)]
                for c in range(KD):
                    pe.wait_ge(*tile_added.at(made + c + 1))
                    m = product(nc, k.pm[:, c % 4, :], [([w[a][:, q, P * c:P * c + P] for a in range(2)],
                                                         [fp[a][:, e, q, :] for a in range(2)]) for q in range(2)])
                    if c < KD - 1:
                        m.then_inc(*tile_made.inc(times))
                m.then_inc(k.slab_done[j], 1)

            up(0, 0, 0, 0, True)
            up(1, 1, 0, 0, True)
            with pe.Fori(0, loops) as i:
                up(0, 0, 1 + 2 * i, i + 1)
                down(0, 1, 1 + 2 * i, i, 16 * i, loops)
                up(1, 0, 2 + 2 * i, i + 1)
                down(1, 1, 2 + 2 * i, i, 16 * i + 8, loops)
            down(0, 0, 2 * TURNS1 - 1, TURNS1 - 1, 16 * loops, 1)
            down(1, 1, 2 * TURNS1 - 1, TURNS1 - 1, 16 * loops + 8, 1)

        @block.scalar
        def _(act):
            def hi(j, n):
                hi_of_slab(k, act, j, n0 + n, loaded_value(g0 + j) + 16 * n)

            def relu_tiles(e, t, j, n, first=False):
                act.wait_ge(k.slab_done[j], n0 + n + 1)
                if not first:
                    act.wait_ge(*squared[e].at(t))
                nc.scalar.activation(relu[:, e], k.pl[:, 2 * e:2 * e + 2, :], ACT.Relu).then_inc(*relu_ready[e].inc(1 if first else loops))

            def hidden_hi(e, t, first=False):
                act.wait_ge(*squared[e].at(t + 1))
                if not first:
                    act.wait_ge(k.slab_done[1], n0 + e + 2 * t)
                nc.scalar.activation(fp[0][:, e], f[:, e], ACT.Copy).then_inc(*f_hi[e].inc(1 if first else loops))

            split_x(k, act, None, x, parts, x_hi, x_lo)
            for e in range(2):
                hi(e, 1)
                relu_tiles(e, 0, e, 0, True)
            for e in range(2):
                hidden_hi(e, 0, True)
            with act.Fori(0, loops) as i:
                for e in range(2):
                    hi(0, 2 + e + 2 * i)
                    relu_tiles(e, i + 1, 0, 1 + e + 2 * i)
                    hi(1, 2 + e + 2 * i)
                    hidden_hi(e, i + 1)

        @block.gpsimd
        def _(pool):
            for c in range(KD):
                nc.gpsimd.memset(y[:, c, :], 0.0).then_inc(*y_zeroed.inc())
            for e in range(2):
                lo_of_slab(k, pool, e, n0 + 1)
            with pool.Fori(0, loops) as i:
                for e in range(2):
                    lo_of_slab(k, pool, 0, n0 + 2 + e + 2 * i)
                    lo_of_slab(k, pool, 1, n0 + 2 + e + 2 * i)

        @block.vector
        def _(dve):
            def square(e, t, first=False):
                dve.wait_ge(*relu_ready[e].at(t + 1))
                if not first:
                    dve.wait_ge(*f_hi[e].at(t))
                    dve.wait_ge(*f_lo[e].at(t))
                nc.vector.tensor_tensor(f[:, e], relu[:, e], k.pl[:, 2 * e:2 * e + 2, :], ALU.mult)\
                    .then_inc(*squared[e].inc(1 if first else loops))

            def hidden_lo(e, t, first=False):
                dve.wait_ge(*f_hi[e].at(t + 1))
                nc.vector.tensor_tensor(fp[1][:, e], f[:, e], fp[0][:, e].bitcast(F32), ALU.subtract)\
                    .then_inc(*f_lo[e].inc(1 if first else loops))

            split_x(k, None, dve, x, parts, x_hi, x_lo)
            dve.sem_inc(tile_added.sem, 4)
            tile_added.total += 4
            dve.wait_ge(*y_zeroed.at(KD))
            for e in range(2):
                square(e, 0, True)
            for e in range(2):
                hidden_lo(e, 0, True)
            with dve.Fori(0, loops) as i:
                for e in range(2):
                    square(e, i + 1)
                    add_tiles(k, dve, y, 1, n0 + 2 + e + 2 * i, 2 * i + e, tile_made, tile_added, loops)
                    hidden_lo(e, i + 1)
            for e in range(2):
                add_tiles(k, dve, y, e, n0 + 2 * TURNS1, 2 * loops + e, tile_made, tile_added, 1)


def add_tiles(k, dve, y, j, done, before, tile_made, tile_added, times):
    for c in range(KD):
        if c < KD - 1:
            dve.wait_ge(*tile_made.at((KD - 1) * before + c + 1))
        else:
            dve.wait_ge(k.slab_done[j], done)
        dve.wait_ge(*tile_added.at(KD * before + c + 4))
        k.nc.vector.tensor_tensor(y[:, c, :], y[:, c, :], k.pm[:, c % 4, :], ALU.add).then_inc(*tile_added.inc(times))


def ffn2_phase(k, g0, x, y, load):
    nc = k.nc
    k.phase()
    assert k.split_done == g0 + 2 and g0 % 2 == 0
    k.split_done = g0 + 3 * TURNS2 + 1
    bodies = (TURNS2 - 1) // 2
    w_up, w_down = k.io["w_up_2"][0], k.io["w_down_2"][0]
    cw, cb = k.vec("conv_w_2").rearrange("p (t n) -> p t n", t=3), k.vec("conv_b_2")
    x_hi, x_lo = k.sem("x_hi"), k.sem("x_lo")
    tap2, tap1 = [k.sem("tap2_gate"), k.sem("tap2_up")], [k.sem("tap1_gate"), k.sem("tap1_up")]
    conv = [k.sem("conv_gate"), k.sem("conv_up")]
    gelu_ready, f_ready, f_hi, f_lo = k.sem("gelu_ready"), k.sem("f_ready"), k.sem("f_hi_a"), k.sem("f_lo_a")
    tile_made, tile_added, y_zeroed = k.sem("down_tile_made"), k.sem("down_tile_added"), k.sem("zeroed")
    n0 = g0 // 2
    with ExitStack() as ctx:
        def sb(name, shape, dt=F32):
            return ctx.enter_context(nc.sbuf_tensor(k.unique(name), shape, dt))
        parts = [sb("x_part", [P, KD, S], F32R) for _ in range(2)]
        cv, ge, f = sb("conv", [P, 2, 2, S]), sb("gelu", [P, 2, S]), sb("f", [P, 2, S])
        fp = [sb("f_part", [P, 2, S], F32R) for _ in range(2)]
        block = ctx.enter_context(nc.Block())

        def turns(eng, do):
            do(0, 0, 0, 1)
            with eng.Fori(0, bodies) as b:
                for h in range(2):
                    do(2 * b + (1 + h), h, 3 * b + (1 + h), bodies)

        def place(slot, n, o):
            return (slot + o) % 2, n + (slot + o) // 2

        @block.sync
        def _(sp):
            sp.dma_start(*load).then_inc(*k.sem("p_loaded").dma())
            with sp.Fori(0, bodies) as b:
                for h in range(2):
                    for o, (kind, w) in enumerate((("up", 0), ("up", FF2), ("down", 0))):
                        j, n = place(h, 3 * b + (1 + h), o)
                        sp.wait_ge(k.slab_lo[j], n0 + n)
                        if kind == "up":
                            src = w_up[:, bass.ds(512 * b + (256 * (1 + h) + w), 256)].rearrange("(k p) n -> p k n", p=P)
                            dst = k.ring[:, j, :].rearrange("p (k n) -> p k n", n=256)
                        else:
                            src = w_down[bass.ds(512 * b + 256 * h, 256), :].rearrange("(k p) n -> p k n", p=P)
                            dst = k.ring[:, j, :].rearrange("p (k n) -> p k n", n=D)
                        sp.dma_start(dst, src).then_inc(k.slab_loaded[j], 16)
            for g in range(g0 + 3 * TURNS2 - 1, g0 + 3 * TURNS2 + 2):
                issue_slab(k, sp, g)

        @block.tensor
        def _(pe):
            def down(j, n, t, times):
                use_slab(k, pe, j, n0 + n)
                pe.wait_ge(*f_lo.at(t + 1))
                w = [slab_view(k, j, a, D, 2) for a in range(2)]
                for c in range(KD):
                    pe.wait_ge(*tile_added.at(KD * t + c + 1))
                    m = product(nc, k.pm[:, c % 4, :], [([w[a][:, q, P * c:P * c + P] for a in range(2)],
                                                         [fp[a][:, q, :] for a in range(2)]) for q in range(2)])
                    if c < KD - 1:
                        m.then_inc(*tile_made.inc(times))
                m.then_inc(k.slab_done[j], 1)

            def turn(t, slot, n, times):
                for e in range(2):
                    j, m0 = place(slot, n, e)
                    use_slab(k, pe, j, n0 + m0)
                    if times > 1:
                        pe.wait_ge(*conv[e].at(2 * t))
                    w = [slab_view(k, j, a) for a in range(2)]
                    for c in range(2):
                        for q in range(KD):
                            if times == 1 and e == 0 and c == 0:
                                pe.wait_ge(*x_lo.at(q + 1))
                            m = product(nc, k.pl[:, 2 * e + c, :], [([w[a][:, q, P * c:P * c + P] for a in range(2)],
                                                                     [parts[a][:, q, :] for a in range(2)])], q == 0, q == KD - 1)
                    m.then_inc(k.slab_done[j], 1)
                if times > 1:
                    down(*place(slot, n, 2), t - 1, times)
            turns(pe, turn)
            down(0, (3 * TURNS2 - 1) // 2, TURNS2 - 1, 1)

        @block.scalar
        def _(act):
            def hi(slot, n, o):
                j, m = place(slot, n, o)
                hi_of_slab(k, act, j, n0 + m, loaded_value(g0 + j) + 16 * m)

            def turn(t, slot, n, times):
                for e in range(2):
                    j, m = place(slot, n, e)
                    hi(slot, n, e + 2)
                    act.wait_ge(k.slab_done[j], n0 + m + 1)
                    if times > 1:
                        act.wait_ge(*(f_ready.at(2 * t) if e else gelu_ready.at(2 * t)))
                    for c in range(2):
                        at = 2 * t + (NT2 * e + c)
                        nc.scalar.activation(cv[:, e, c, :], k.pl[:, 2 * e + c, :], ACT.Identity, scale=cw[:, 2, bass.ds(at, 1)],
                                             bias=cb[:, bass.ds(at, 1)]).then_inc(*tap2[e].inc(times))
                for c in range(2):
                    act.wait_ge(*conv[0].at(2 * t + c + 1))
                    if times > 1:
                        act.wait_ge(*f_ready.at(2 * t))
                    nc.scalar.activation(ge[:, c, :], cv[:, 0, c, :], ACT.Gelu_apprx_tanh).then_inc(*gelu_ready.inc(times))
                if times > 1:
                    hi(slot, n, 4)
                    j, m = place(slot, n, 2)
                    act.wait_ge(k.slab_done[j], n0 + m + 1)
                act.wait_ge(*f_ready.at(2 * t + 2))
                nc.scalar.activation(fp[0][:], f[:], ACT.Copy).then_inc(*f_hi.inc(times))
            split_x(k, act, None, x, parts, x_hi, x_lo)
            turns(act, turn)

        @block.gpsimd
        def _(pool):
            for c in range(KD):
                nc.gpsimd.memset(y[:, c, :], 0.0).then_inc(*y_zeroed.inc())

            def turn(t, slot, n, times):
                for e in range(2):
                    j, m = place(slot, n, e + 2)
                    lo_of_slab(k, pool, j, n0 + m)
                if times > 1:
                    pool.wait_ge(*f_hi.at(t))
                    pool.wait_ge(*f_lo.at(t))
                for c in range(2):
                    pool.wait_ge(*gelu_ready.at(2 * t + c + 1))
                    pool.wait_ge(*conv[1].at(2 * t + c + 1))
                    nc.gpsimd.tensor_tensor(f[:, c, :], ge[:, c, :], cv[:, 1, c, :], ALU.mult).then_inc(*f_ready.inc(times))
                if times > 1:
                    j, m = place(slot, n, 4)
                    lo_of_slab(k, pool, j, n0 + m)
            turns(pool, turn)

        @block.vector
        def _(dve):
            split_x(k, None, dve, x, parts, x_hi, x_lo)
            dve.sem_inc(tile_added.sem, 4)
            tile_added.total += 4
            dve.wait_ge(*y_zeroed.at(KD))

            def turn(t, slot, n, times):
                for e in range(2):
                    for tap, source, result in ((1, tap2, tap1), (0, tap1, conv)):
                        for c in range(2):
                            at = 2 * t + (NT2 * e + c)
                            dve.wait_ge(*source[e].at(2 * t + c + 1))
                            d = 2 - tap
                            nc.vector.scalar_tensor_tensor(out=cv[:, e, c, d:S], in0=k.pl[:, 2 * e + c, 0:S - d],
                                                           scalar=cw[:, tap, bass.ds(at, 1)], in1=cv[:, e, c, d:S],
                                                           op0=ALU.mult, op1=ALU.add).then_inc(*result[e].inc(times))
                if times > 1:
                    j, m = place(slot, n, 2)
                    add_tiles(k, dve, y, j, n0 + m + 1, t - 1, tile_made, tile_added, times)
                dve.wait_ge(*f_hi.at(t + 1))
                nc.vector.tensor_tensor(fp[1][:], f[:], fp[0][:].bitcast(F32), ALU.subtract).then_inc(*f_lo.inc(times))
            turns(dve, turn)
            add_tiles(k, dve, y, 0, n0 + (3 * TURNS2 - 1) // 2 + 1, TURNS2 - 1, tile_made, tile_added, 1)


def attend(k, groups):
    nc = k.nc
    k.phase()
    units = [dict(u, group=g) for g, (us, _) in enumerate(groups) for u in us]
    n = len(units)
    for s, u in enumerate(units):
        same = [i for i in range(n) if (units[i]["group"], units[i]["half"]) == (u["group"], u["half"])]
        u["first"], u["last"], u["end"] = s == same[0], s == same[-1], s == n - 1 or units[s + 1]["group"] != u["group"]
        u["weighed"] = s + 1 + sum(x.get("gate") is not None for x in units[:s + 1])
    ends = [s for s, u in enumerate(units) if u["end"]]
    scored, masked, p_ready = k.sem("scored"), k.sem("masked"), k.sem("p_ready")
    weight_steps, scaled, turned, copied = k.sem("weight_steps"), [k.sem("p_scaled_pool"), k.sem("p_scaled_dve")], k.sem("p_turned"), [k.sem("p_copied_dve"), k.sem("p_copied_act")]
    mixed, out_ready = k.sem("pv_mixed"), k.sem("out_ready")
    LAG_W, LAG_T, LAG_V = 1, 4, 6
    SLOTS = LAG_T + 1
    with nc.sbuf_tensor(k.unique("masked"), [P, 3, S], F32) as sm, nc.sbuf_tensor(k.unique("probs"), [P, SLOTS, S], F32) as pr, \
            nc.sbuf_tensor(k.unique("probsT"), [P, 3, TB, P], F32) as pt, nc.sbuf_tensor(k.unique("rowneg"), [P, n], F32) as rn, \
            nc.sbuf_tensor(k.unique("rowsum"), [P, n], F32) as rs, nc.sbuf_tensor(k.unique("weight"), [P, n], F32) as wt, \
            nc.Block() as block:
        widths = [u["k"].shape[1] for u in units]
        pieces = [[(a, min(P, w - a)) for a in range(0, w, P)] for w in widths]

        @block.tensor
        def _(pe):
            for t in range(n + LAG_V):
                if t < n:
                    u = units[t]
                    if t >= 4:
                        pe.wait_ge(*masked.at(t - 3))
                    nc.tensor.matmul(k.pl[:, t % 4, 0:widths[t]], u["q"], u["k"], start=True, stop=True)\
                        .then_inc(*scored.inc())
                if 0 <= t - LAG_T < n:
                    s = t - LAG_T
                    pe.wait_ge(*scaled[s % 2].at(s // 2 + 1))
                    if s >= 2:
                        pe.wait_ge(*copied[s % 2].at(s // 2))
                    for b, (a, w) in enumerate(pieces[s]):
                        m = nc.tensor.transpose(k.pm[0:w, s % 2, P * b:P * b + P], pr[:, s % SLOTS, a:a + w], k.ident)
                    m.then_inc(*turned.inc())
                if 0 <= t - LAG_V < n:
                    s = t - LAG_V
                    u = units[s]
                    r = slice(HD * u["half"], HD * u["half"] + HD)
                    pe.wait_ge(*copied[s % 2].at(s // 2 + 1))
                    if u["group"] >= 2:
                        pe.wait_ge(*out_ready.at(u["group"] - 1))
                    for b, (a, w) in enumerate(pieces[s]):
                        m = nc.tensor.matmul(k.pm[r, 2 + u["group"] % 2, 0:P], u["v"](b), pt[0:w, s % 3, b, :],
                                             start=u["first"] and b == 0, stop=u["last"] and b == len(pieces[s]) - 1)
                    m.then_inc(*mixed.inc())

        def copy(eng, s, e):
            ps = pieces[s]
            w = ps[-1][1]
            eng.wait_ge(*turned.at(s + 1))
            if s >= 3:
                eng.wait_ge(*mixed.at(s - 2))
            dst, src = pt[0:w, s % 3, 0:len(ps), :], k.pm[0:w, s % 2, 0:P * len(ps)].rearrange("p (b q) -> p b q", q=P)
            if e == 0:
                nc.vector.tensor_copy(dst, src).then_inc(*copied[0].inc())
            else:
                nc.scalar.activation(dst, src, ACT.Copy).then_inc(*copied[1].inc())

        def weigh(eng, s):
            eng.wait_ge(*weight_steps.at(units[s]["weighed"]))
            p = pr[:, s % SLOTS, 0:widths[s]]
            (nc.vector if s % 2 else nc.gpsimd).tensor_scalar(p, p, wt[:, s:s + 1], None, ALU.mult).then_inc(*scaled[s % 2].inc())

        @block.vector
        def _(dve):
            for t in range(n + LAG_V):
                if t < n:
                    u = units[t]
                    dve.wait_ge(*scored.at(t + 1))
                    if t >= 3:
                        dve.wait_ge(*p_ready.at(t - 2))
                    nc.vector.tensor_tensor_reduce(sm[:, t % 3, 0:widths[t]], k.pl[:, t % 4, 0:widths[t]], u["mask"],
                                                   -SCALE, 3e38, ALU.add, ALU.min, rn[:, t:t + 1])\
                        .then_inc(*masked.inc())
                if 0 <= t - LAG_W < n:
                    s = t - LAG_W
                    u = units[s]
                    dve.wait_ge(*p_ready.at(s + 1))
                    nc.vector.reciprocal(wt[:, s:s + 1], rs[:, s:s + 1]).then_inc(*weight_steps.inc())
                    if u.get("gate") is not None:
                        dve.wait_ge(*weight_steps.at(u["weighed"] - 1))
                        nc.vector.tensor_tensor(wt[:, s:s + 1], wt[:, s:s + 1], u["gate"], ALU.mult).then_inc(*weight_steps.inc())
                    if s % 2:
                        weigh(dve, s)
                if 0 <= t - LAG_T < n and (t - LAG_T) % 2 == 0:
                    copy(dve, t - LAG_T, 0)

        @block.gpsimd
        def _(pool):
            for s in range(0, n, 2):
                weigh(pool, s)

        @block.scalar
        def _(act):
            for t in range(n + LAG_V + 1):
                if t < n:
                    act.wait_ge(*masked.at(t + 1))
                    if t >= SLOTS:
                        act.wait_ge(*turned.at(t - SLOTS + 1))
                    nc.scalar.activation(pr[:, t % SLOTS, 0:widths[t]], sm[:, t % 3, 0:widths[t]], ACT.Exp,
                                         bias=rn[:, t:t + 1], scale=-1.0, accum_out=rs[:, t:t + 1])\
                        .then_inc(*p_ready.inc())
                if 0 <= t - LAG_T < n and (t - LAG_T) % 2 == 1:
                    copy(act, t - LAG_T, 1)
                if t - LAG_V - 1 in ends:
                    s = t - LAG_V - 1
                    act.wait_ge(*mixed.at(s + 1))
                    nc.scalar.activation(groups[units[s]["group"]][1], k.pm[:, 2 + units[s]["group"] % 2, 0:P], ACT.Copy)\
                        .then_inc(*out_ready.inc())


def sincos(k, dve, ang, out, tmp, steps):
    nc = k.nc
    C1, C2 = 6.28125, float(np.float32(TWO_PI - 6.28125))
    C3 = float(TWO_PI - 6.28125 - np.float64(np.float32(TWO_PI - 6.28125)))
    MAGIC = 12582912.0
    def step(i):
        i.then_inc(*steps.inc())
        dve.wait_ge(*steps.at(steps.total - steps.base))
    for q in range(2):
        y, t = out[:, q], tmp[:, q]
        step(nc.vector.tensor_scalar(t, ang, 1.0 / TWO_PI, 0.25 * q, ALU.mult, ALU.add))
        step(nc.vector.tensor_scalar(t, t, MAGIC, None, ALU.add))
        step(nc.vector.tensor_scalar(t, t, -MAGIC, None, ALU.add))
        step(nc.vector.scalar_tensor_tensor(out=y, in0=t, scalar=-C1, in1=ang, op0=ALU.mult, op1=ALU.add))
        step(nc.vector.scalar_tensor_tensor(out=y, in0=t, scalar=-C2, in1=y, op0=ALU.mult, op1=ALU.add))
        step(nc.vector.scalar_tensor_tensor(out=y, in0=t, scalar=-C3, in1=y, op0=ALU.mult, op1=ALU.add))
        if q:
            step(nc.vector.tensor_scalar(y, y, TWO_PI / 4, None, ALU.add))
        step(nc.vector.tensor_scalar(y, y, 3.1415925, -3.1415925, ALU.min, ALU.max))


class RopeAndConv:

    def __init__(self, k, ctx, qkv, z, out):
        def sb(name, shape, dt=F32):
            return ctx.enter_context(k.nc.sbuf_tensor(k.unique("rope_" + name), shape, dt))
        self.k, self.qkv, self.z, self.out = k, qkv, z, out
        self.posi, self.posf = sb("posi", [P, TB], I32), sb("posf", [P, TB])
        self.ang, self.angt, self.sc = sb("ang", [P, TB, 32]), sb("angt", [P, 2, TB, 32]), sb("sc", [P, 2, TB, 32])
        self.work = sb("work", [P, 2, S])

    def sync(self, sp):
        sp.dma_start(self.posi[:], self.k.io["positions"][0].rearrange("(b p) -> p b", p=P), allow_slow_non_contiguous=True)\
            .then_inc(*self.k.sem("pos_loaded").dma())

    def vector(self, dve):
        k, posf, ang, sc, steps = self.k, self.posf, self.ang, self.sc, self.k.sem("angle_steps")
        V, M = k.nc.vector, ALU.mult

        def st(i):
            i.then_inc(*steps.inc())
            dve.wait_ge(*steps.at(steps.total - steps.base))

        dve.wait_ge(*k.sem("pos_loaded").dma_at(1))
        st(V.tensor_copy(posf[:], self.posi[:]))
        for b in range(TB):
            st(V.tensor_scalar(ang[:, b, :], k.const("invfreq"), posf[:, b:b + 1], None, M))
        sincos(k, dve, ang[:], sc, self.angt, steps)
        self.angles_stand = steps.total - steps.base
        dve.wait_ge(*k.sem("sines_ready").at(1))
        dve.wait_ge(*k.sem("drained_act").at(4))
        qk = self.qkv[:, :, 0:2 * AW].rearrange("p b (h t c) -> p b h t c", t=2, c=32)
        wa, wb = (self.work[:, n].rearrange("p (h c) -> p h c", c=32) for n in range(2))
        for b in range(TB):
            sn = sc[:, 0, b].unsqueeze(1).broadcast_to([P, 16, 32])
            cs = sc[:, 1, b].unsqueeze(1).broadcast_to([P, 16, 32])
            t1, t2 = qk[:, b, :, 0, :], qk[:, b, :, 1, :]
            V.tensor_tensor(wa, t1, sn, M).then_inc(*steps.inc())
            st(V.tensor_tensor(wb, t2, sn, M))
            V.tensor_tensor(t1, t1, cs, M).then_inc(*steps.inc())
            st(V.tensor_tensor(t2, t2, cs, M))
            V.tensor_tensor(t1, t1, wb, ALU.subtract).then_inc(*steps.inc())
            st(V.tensor_tensor(t2, t2, wa, ALU.add))
        dve.wait_ge(*k.sem("drained_act").at(9))
        cw = k.vec("conv_w").rearrange("p (t n) -> p t n", t=3)
        z, out, cz = self.z, self.out, self.work
        st(V.tensor_tensor(cz[:], z[:, 2:4, :], z[:, 4:6, :], M))
        V.tensor_scalar(out[:, 0, :], cz[:, 0, :], cw[:, 2, 0:1], None, M).then_inc(*steps.inc())
        st(V.tensor_scalar(out[:, 1, :], cz[:, 1, :], cw[:, 2, 1:2], None, M))
        for tap in (1, 0):
            n = S - 2 + tap
            for c in range(2):
                i = V.scalar_tensor_tensor(out=out[:, c, S - n:S], in0=cz[:, c, 0:n], scalar=cw[:, tap, c:c + 1],
                                           in1=out[:, c, S - n:S], op0=M, op1=ALU.add)
                st(i) if c else i.then_inc(*steps.inc())
        st(V.tensor_tensor(out, out, z[:, 0:2, :], M))

    def scalar(self, act, i):
        if i == 2:
            act.wait_ge(*self.k.sem("angle_steps").at(self.angles_stand))
            self.k.nc.scalar.activation(self.sc[:], self.sc[:], ACT.Sin).then_inc(*self.k.sem("sines_ready").inc())

    def tensor(self, pe, i):
        pass


def group_norm_phase(k, x, gain, groups, ahead=0):
    nc = k.nc
    k.phase()
    ahead = split_ahead(k, ahead)
    sq_ready, sum_ready, std_ready, rstd_ready, out = (k.sem("norm_" + s) for s in ("sq", "sum", "std", "rstd", "out"))
    with nc.sbuf_tensor(k.unique("sq"), [P, KD, S], F32) as sq, nc.sbuf_tensor(k.unique("std"), [P, len(groups), S], F32) as std, \
            nc.Block() as block:
        tiles = [i for lo, hi in groups for i in range(lo, hi)]

        @block.scalar
        def _(act):
            for i in tiles:
                nc.scalar.activation(sq[:, i, :], x[:, i, :], ACT.Square).then_inc(*sq_ready.inc())
            for g in ahead:
                hi_of_slab(k, act, g % 2, g // 2, loaded_value(g), slab_size(g))
            for g, (lo, hi) in enumerate(groups):
                act.wait_ge(*sum_ready.at(g + 1))
                nc.scalar.activation(std[:, g, :], k.pm[:, g, :], ACT.Sqrt, bias=k.eps[:, 0:1], scale=1.0 / (P * (hi - lo)))\
                    .then_inc(*std_ready.inc())

        @block.gpsimd
        def _(pool):
            for g in ahead:
                lo_of_slab(k, pool, g % 2, g // 2, slab_size(g))

        @block.tensor
        def _(pe):
            for g, (lo, hi) in enumerate(groups):
                for i in range(lo, hi):
                    pe.wait_ge(*sq_ready.at(tiles.index(i) + 1))
                    m = nc.tensor.matmul(k.pm[:, g, :], k.ones, sq[:, i, :], start=i == lo, stop=i == hi - 1)
                m.then_inc(*sum_ready.inc())

        @block.vector
        def _(dve):
            for g, (lo, hi) in enumerate(groups):
                dve.wait_ge(*std_ready.at(g + 1))
                nc.vector.reciprocal(std[:, g, :], std[:, g, :]).then_inc(*rstd_ready.inc())
                dve.wait_ge(*rstd_ready.at(g + 1))
                for i in range(lo, hi):
                    nc.vector.scalar_tensor_tensor(out=x[:, i, :], in0=x[:, i, :], scalar=gain[:, i:i + 1], in1=std[:, g, :],
                                                   op0=ALU.mult, op1=ALU.mult).then_inc(*out.inc())


def rwkv_phases(k, z, out, spare):
    nc = k.nc
    ctx = ExitStack()
    with ctx:
        def sb(name, shape):
            return ctx.enter_context(nc.sbuf_tensor(k.unique("rw_" + name), shape, F32))

        kr = sb("kr", [P, 3, 2, S])
        lam = sb("lam", [P, 3, TB, 2])
        tm = sb("tm", [P, TB, 4, RW])
        bonus = sb("bonus", [P, TB, 6])
        gate = sb("gate", [P, TB, RW])
        bh, kh = sb("bh", [P, 3 * S]), sb("kh", [P, 3 * S])
        bhat, khat = (t[:].rearrange("p (i t) -> p i t", t=S) for t in (bh, kh))
        A = z[:].rearrange("p i t -> p (i t)")[:, 0:24 * P].rearrange("p (q t) -> p q t", t=P)
        rwkv_prepare(k, z, kr, bhat, khat, lam, bonus, gate)
        with ExitStack() as products:
            banks = []
            for n, src in enumerate((kr[:, :, 0, :], bhat, khat, z[:, 6:9, 1:S + 1])):
                for i in range(3):
                    banks.append(([src[:, i, P * b:P * b + P] for b in range(TB)], tm[:, :, n, P * i:P * i + P]))
            turn_phase(k, banks)
            AT = products.enter_context(nc.sbuf_tensor(k.unique("rw_AT"), [P, 24, 3, P], F32))
            inverses = ExitStack()
            yx = inverses.enter_context(nc.sbuf_tensor(k.unique("rw_yx"), [P, 24, 2, P], F32))
            k.phase()
            made, masked, zeroed, padded = k.sem("rw_made"), k.sem("rw_masked"), k.sem("zeroed"), k.sem("rw_padded")
            with nc.sbuf_tensor(k.unique("rw_khat1"), [P, S], F32) as last, nc.Block() as block:
                alone = [[spare[:, 0, :], spare[:, 1, :]], [spare[:, 2, :], last[:]]]

                @block.tensor
                def _(pe):
                    for q in range(24):
                        h, b = q // 4, q % 4
                        i, e = h // 2, h % 2
                        cols = slice(P * b, P * b + P)
                        bz, kz = alone[0][e][:, cols], alone[1][e][:, cols]
                        if b == 0:
                            pe.wait_ge(*padded.at(4 * i + 2 * e + 2))
                        if q >= 2:
                            pe.wait_ge(*masked.at(3 * (q - 1)))
                        bank = k.pl[:, 2 * (q % 2), :]
                        nc.tensor.matmul(bank[:, 0:2 * P].rearrange("p (a b) -> p a b", a=2), bz, kr[:, i, :, cols], start=True, stop=True)
                        nc.tensor.matmul(bank[:, 2 * P:4 * P].rearrange("p (a b) -> p a b", a=2), kz, kr[:, i, :, cols], start=True, stop=True)
                        nc.tensor.matmul(k.pl[:, 2 * (q % 2) + 1, 0:P], kr[:, i, 0, cols], bz, start=True, stop=True)\
                            .then_inc(*made.inc())

                @block.scalar
                def _(act):
                    act.wait_ge(*zeroed.at(4))
                    for i in range(3):
                        for e in range(2):
                            rows = slice(HD * e, HD * e + HD)
                            if i:
                                act.wait_ge(*made.at(8 * (i - 1) + 4 * e + 4))
                            for to, src in ((alone[0][e], bhat), (alone[1][e], khat)):
                                nc.scalar.activation(to[rows], src[rows, i, :], ACT.Copy).then_inc(*padded.inc())

                @block.vector
                def _(dve):
                    for t in alone:
                        for e in range(2):
                            nc.vector.memset(t[e][HD * (1 - e):HD * (1 - e) + HD], 0.0).then_inc(*zeroed.inc())
                    for q in range(24):
                        dve.wait_ge(*made.at(q + 1))
                        nc.vector.tensor_tensor(AT[:, q].rearrange("p a b -> p (a b)"), k.pl[:, 2 * (q % 2), P:4 * P], k.const("chunkmask"), ALU.mult)\
                            .then_inc(*masked.inc())
                        nc.vector.tensor_tensor(yx[:, q, 0], k.pl[:, 2 * (q % 2), 0:P], k.const("join1"), ALU.mult).then_inc(*masked.inc())
                        nc.vector.tensor_tensor(A[:, q], k.pl[:, 2 * (q % 2) + 1, 0:P], k.const("below"), ALU.mult).then_inc(*masked.inc())

            invert_phase(k, A, yx, bh[:, 0:8 * P].rearrange("p (a b c) -> p a b c", a=2, b=4))
            wT = z[:].rearrange("p i t -> p (i t)")[:, 24 * P:24 * P + 3 * S].rearrange("p (i t) -> p i t", t=S)
            u = spare.rearrange("p i t -> p (i t)").rearrange("p (b f) -> p b f", f=RW)
            av = bh[:].rearrange("p (b f) -> p b f", f=RW)
            k.phase()
            w_made, w_out, av_made, av_out, u_made, u_out = (k.sem(s) for s in ("rw_w_made", "rw_w_out", "rw_av_made", "rw_av_out", "rw_u_made", "rw_u_out"))
            with nc.Block() as block:
                @block.tensor
                def _(pe):
                    for b in range(TB):
                        if b:
                            pe.wait_ge(*w_out.at(b))
                            pe.wait_ge(*av_out.at(b))
                            pe.wait_ge(*u_out.at(b))
                        for h in range(6):
                            q, i, p = 4 * h + b, h // 2, HD * (h % 2)
                            m = nc.tensor.matmul(k.pl[p:p + HD, 0, P * i:P * i + P], tm[:, b, 0, HD * h:HD * h + HD], yx[:, q, 0, :], start=True, stop=True)
                        m.then_inc(*w_made.inc())
                        for h in range(6):
                            q = 4 * h + b
                            m = nc.tensor.matmul(k.pl[:, 1, HD * h:HD * h + HD], AT[:, q, 1, :], tm[:, b, 3, HD * h:HD * h + HD], start=True, stop=True)
                        m.then_inc(*av_made.inc())
                        pe.wait_ge(*av_out.at(b + 1))
                        for h in range(6):
                            q = 4 * h + b
                            m = nc.tensor.matmul(k.pl[:, 2, HD * h:HD * h + HD], yx[:, q, 0, :], av[:, b, HD * h:HD * h + HD], start=True, stop=True)
                        m.then_inc(*u_made.inc())

                @block.scalar
                def _(act):
                    for b in range(TB):
                        act.wait_ge(*w_made.at(b + 1))
                        nc.scalar.activation(wT[:, :, P * b:P * b + P], k.pl[:, 0, 0:3 * P].rearrange("p (i t) -> p i t", i=3), ACT.Copy).then_inc(*w_out.inc())
                        act.wait_ge(*u_made.at(b + 1))
                        nc.scalar.activation(u[:, b, :], k.pl[:, 2, 0:RW], ACT.Copy).then_inc(*u_out.inc())

                @block.vector
                def _(dve):
                    for b in range(TB):
                        dve.wait_ge(*av_made.at(b + 1))
                        nc.vector.tensor_copy(av[:, b, :], k.pl[:, 1, 0:RW]).then_inc(*av_out.inc())

            inverses.close()
            sa = kh[:, 0:2 * RW].rearrange("p (b f) -> p b f", f=RW)
            st = kh[:, 2 * RW:3 * RW].rearrange("p (b i v) -> p b i v", b=2, v=HD)
            tmp = kh[:, 3 * RW:4 * RW].rearrange("p (b i v) -> p b i v", b=2, v=HD)
            k.phase()
            ws_made, sa_ready, st_made, st_ready, o_made, o_out = (k.sem(s) for s in ("rw_ws_made", "rw_sa_ready", "rw_st_made", "rw_st_ready", "rw_o_made", "rw_o_out"))
            st_sum, zeroed = k.sem("rw_st_sum"), k.sem("zeroed")
            after = HeadNorm(k, products, out, tm, bonus, gate)
            with nc.Block() as block:
                @block.sync
                def _(sp):
                    after.sync(sp)

                @block.tensor
                def _(pe):
                    for b in range(TB):
                        cur = st[:, b % 2]
                        if b == 0:
                            pe.wait_ge(*zeroed.at(1))
                        else:
                            pe.wait_ge(*st_ready.at(b))
                        cols = slice(P * b, P * b + P)
                        for h in (0, 2, 4, 1, 3, 5):
                            i, p = h // 2, HD * (h % 2)
                            m = nc.tensor.matmul(k.pl[:, h % 2, HD * i:HD * i + HD], wT[p:p + HD, i, cols], cur[p:p + HD, i, :], start=True, stop=True)
                        m.then_inc(*ws_made.inc())
                        pe.wait_ge(*sa_ready.at(2 * b + 2))
                        if b < TB - 1:
                            for h in range(6):
                                i, p, hc = h // 2, HD * (h % 2), slice(HD * h, HD * h + HD)
                                nc.tensor.matmul(k.pl[p:p + HD, 2, HD * i:HD * i + HD], tm[:, b, 2, hc], tm[:, b, 3, hc], start=True, stop=False)
                                m = nc.tensor.matmul(k.pl[p:p + HD, 2, HD * i:HD * i + HD], tm[:, b, 1, hc], sa[:, b % 2, hc], start=False, stop=True)
                            m.then_inc(*st_made.inc())
                        if b:
                            pe.wait_ge(*o_out.at(6 * b))
                        for h in (0, 2, 4, 1, 3, 5):
                            i, p, hc, q = h // 2, HD * (h % 2), slice(HD * h, HD * h + HD), 4 * h + b
                            o = k.pm[:, h % 2, HD * i:HD * i + HD]
                            nc.tensor.matmul(o, kr[p:p + HD, i, 1, cols], cur[p:p + HD, i, :], start=True, stop=False)
                            nc.tensor.matmul(o, AT[:, q, 0, :], sa[:, b % 2, hc], start=False, stop=False)
                            m = nc.tensor.matmul(o, AT[:, q, 2, :], tm[:, b, 3, hc], start=False, stop=True)
                        m.then_inc(*o_made.inc())

                @block.gpsimd
                def _(pool):
                    for b in range(TB - 1):
                        after.chunk(pool, nc.gpsimd, b, o_out)

                def parities(t, b):
                    return t[:, b, :].rearrange("p (i e v) -> p e i v", e=2, v=HD)

                @block.vector
                def _(dve):
                    nc.vector.memset(st[:, 0], 0.0).then_inc(*zeroed.inc())
                    dve.wait_ge(*zeroed.at(1))
                    for b in range(TB):
                        dve.wait_ge(*ws_made.at(b + 1))
                        if b >= 2:
                            dve.wait_ge(*o_made.at(b - 1))
                        for e in range(2):
                            nc.vector.scalar_tensor_tensor(out=parities(sa, b % 2)[:, e], in0=k.pl[:, e, 0:3 * HD].rearrange("p (i v) -> p i v", v=HD),
                                                           scalar=-1.0, in1=parities(u, b)[:, e], op0=ALU.mult, op1=ALU.subtract)\
                                .then_inc(*sa_ready.inc())
                        if b < TB - 1:
                            dve.wait_ge(*st_made.at(b + 1))
                            if b:
                                dve.wait_ge(*o_made.at(b))
                            nc.vector.tensor_tensor(tmp[:, 0], st[:, b % 2], k.pl[:, 2, 0:3 * HD].rearrange("p (i v) -> p i v", v=HD), ALU.add).then_inc(*st_sum.inc())
                            dve.wait_ge(*st_sum.at(2 * b + 1))
                            nc.vector.tensor_tensor(tmp[:, 1], tmp[:, 0], lam[:, :, b, 1].unsqueeze(2).broadcast_to([P, 3, HD]), ALU.mult).then_inc(*st_sum.inc())
                            dve.wait_ge(*st_sum.at(2 * b + 2))
                            nc.vector.tensor_tensor(st[:, (b + 1) % 2], tmp[:, 1], lam[:, :, b + 1, 0].unsqueeze(2).broadcast_to([P, 3, HD]), ALU.mult).then_inc(*st_ready.inc())
                        if b:
                            after.invert(dve, b - 1)
                    after.chunk(dve, nc.vector, TB - 1, o_out)

                @block.scalar
                def _(act):
                    for b in range(TB):
                        act.wait_ge(*o_made.at(b + 1))
                        after.scalar(act, b, lambda h: k.pm[:, h % 2, HD * (h // 2):HD * (h // 2) + HD], o_out)


def rwkv_prepare(k, z, kr, bh, kh, lam, bonus, gate):
    nc, io = k.nc, k.io
    with ExitStack() as ctx:
        def sb(name, shape):
            return ctx.enter_context(nc.sbuf_tensor(k.unique("rp_" + name), shape, F32))
        w2a2 = sb("w2a2", [P, 2, RW])
        g2 = sb("g2", [P, RW])
        vec = k.vec("rw_w0_2", 15).rearrange("p (n i) -> p n i", i=3)
        la = sb("la", [P, S])
        gl = sb("gl", [P, S])
        sg = sb("sg", [P, 3, S])
        L = sb("L", [P, 3, S])
        a, kk, t1 = sb("a", [P, 3, S]), sb("kk", [P, 3, S]), sb("t1", [P, 3, S])
        up, down = sb("up", [P, 3, S]), sb("down", [P, 3, S])
        DEC = -float(np.exp(-0.5))
        k.phase()
        def sem(name):
            return k.sem("rp_" + name)
        loaded, padded, lora, gates_made, sig = (sem(x) for x in ("loaded", "padded", "lora", "gates_made", "sig"))
        scaled_k, squared, norms_made, rooted, norm_steps, unit_k = (sem(x) for x in ("scaled_k", "squared", "norms_made", "rooted", "norm_steps", "unit_k"))
        scanned, middle, centred, ends, before = (sem(x) for x in ("scanned", "middle", "centred", "ends", "before"))
        exps, k2, ka, out, rk, gate_made, gate_out, bonus_made = (sem(x) for x in ("exps", "k2", "ka", "out", "rk", "gate_made", "gate_out", "bonus_made"))
        r, kz = z[:, 0:3, 1:S + 1], z[:, 3:6, 1:S + 1]
        spare_banks = [k.pl[:, 3, :], k.pm[:, 3, :], k.pm[:, 2, :]]
        with nc.Block() as block:
            @block.sync
            def _(sp):
                sp.dma_start(w2a2[0:HD, 0], io["rw_w2_2"][0]).then_inc(*loaded.dma())
                sp.dma_start(w2a2[HD:P, 1], io["rw_a2_2"][0]).then_inc(*loaded.dma())
                sp.dma_start(g2[:], io["rw_g2_2"][0]).then_inc(*loaded.dma())

            @block.tensor
            def _(pe):
                for i in range(3):
                    pe.wait_ge(*squared.at(i + 1))
                    nc.tensor.matmul(spare_banks[i], k.const("headsum"), t1[:, i, :], start=True, stop=True).then_inc(*norms_made.inc())
                pe.wait_ge(*loaded.dma_at(3))
                pe.wait_ge(*padded.at(2))
                pe.wait_ge(*lora.at(2))
                for n, banks in enumerate((k.pl, k.pm)):
                    for i in range(3):
                        if n and i == 2:
                            pe.wait_ge(*rooted.at(3))
                        nc.tensor.matmul(banks[:, i, :], w2a2[:, n, P * i:P * i + P], la[:], start=True, stop=True).then_inc(*gates_made.inc())
                pe.wait_ge(*lora.at(3))
                pe.wait_ge(*sig.at(6))
                for b in range(TB):
                    m = nc.tensor.matmul(k.pm[:, b, 0:RW], gl[:, P * b:P * b + P], g2[:], start=True, stop=True)
                m.then_inc(*gate_made.inc())
                pe.wait_ge(*gate_out.at(2))
                pe.wait_ge(*rk.at(3))
                for i in range(3):
                    for b in range(TB):
                        m = nc.tensor.matmul(k.pm[:, 0, 6 * b + 2 * i:6 * b + 2 * i + 2], t1[:, i, P * b:P * b + P], k.const("headcol"), start=True, stop=True)
                m.then_inc(*bonus_made.inc())

            @block.scalar
            def _(act):
                nc.scalar.activation(la[0:HD], z[0:HD, 9, 1:S + 1], ACT.Tanh).then_inc(*lora.inc())
                nc.scalar.activation(la[HD:P], z[HD:P, 9, 1:S + 1], ACT.Copy).then_inc(*lora.inc())
                for i in range(3):
                    act.wait_ge(*norms_made.at(i + 1))
                    nc.scalar.activation(t1[:, i, :], spare_banks[i], ACT.Sqrt).then_inc(*rooted.inc())
                nc.scalar.activation(gl[:], z[:, 10, 1:S + 1], ACT.Sigmoid).then_inc(*lora.inc())
                for n, (banks, to) in enumerate(((k.pl, sg), (k.pm, a))):
                    for i in range(3):
                        act.wait_ge(*gates_made.at(3 * n + i + 1))
                        nc.scalar.activation(to[:, i, :], banks[:, i, :], ACT.Sigmoid, bias=vec[:, n, i:i + 1]).then_inc(*sig.inc())
                act.wait_ge(*centred.at(1))
                nc.scalar.activation(up[:], L[:], ACT.Exp, scale=DEC).then_inc(*exps.inc())
                nc.scalar.activation(down[:], L[:], ACT.Exp, scale=-DEC).then_inc(*exps.inc())
                act.wait_ge(*before.at(1))
                nc.scalar.activation(t1[:], t1[:], ACT.Exp, scale=DEC).then_inc(*exps.inc())
                act.wait_ge(*ends.at(1))
                nc.scalar.activation(lam[:], lam[:], ACT.Exp, scale=DEC).then_inc(*exps.inc())
                act.wait_ge(*gate_made.at(1))
                for b in (0, 2):
                    nc.scalar.activation(gate[:, b:b + 2, :], k.pm[:, b:b + 2, 0:RW], ACT.Copy).then_inc(*gate_out.inc())
                act.wait_ge(*bonus_made.at(1))
                nc.scalar.activation(bonus[:].rearrange("p b h -> p (b h)"), k.pm[:, 0, 0:24], ACT.Copy).then_inc(*gate_out.inc())

            @block.gpsimd
            def _(pool):
                for i in range(3):
                    pool.wait_ge(*sig.at(4 + i))
                    nc.gpsimd.tensor_scalar(kh[:, i, :], a[:, i, :], -1.0, vec[:, 3, i:i + 1], ALU.add, ALU.mult).then_inc(*k2.inc())
                for i in range(3):
                    pool.wait_ge(*k2.at(3 + 2 * i))
                    nc.gpsimd.tensor_tensor(kh[:, i, :], kh[:, i, :], kz[:, i, :], ALU.mult).then_inc(*k2.inc())
                    pool.wait_ge(*k2.at(4 + 2 * i))
                    nc.gpsimd.tensor_tensor(kh[:, i, :], kh[:, i, :], kz[:, i, :], ALU.add).then_inc(*k2.inc())
                for i in range(3):
                    pool.wait_ge(*unit_k.at(i + 1))
                    nc.gpsimd.tensor_tensor(bh[:, i, :], kk[:, i, :], a[:, i, :], ALU.mult).then_inc(*ka.inc())

            @block.vector
            def _(dve):
                V = nc.vector

                def unit(i):
                    dve.wait_ge(*rooted.at(i + 1))
                    V.tensor_scalar(t1[:, i, :], t1[:, i, :], 1e-12, None, ALU.max).then_inc(*norm_steps.inc())
                    dve.wait_ge(*norm_steps.at(2 * i + 1))
                    V.reciprocal(t1[:, i, :], t1[:, i, :]).then_inc(*norm_steps.inc())
                    dve.wait_ge(*norm_steps.at(2 * i + 2))
                    V.tensor_tensor(kk[:, i, :], kk[:, i, :], t1[:, i, :], ALU.mult).then_inc(*unit_k.inc())

                for i in range(3):
                    V.tensor_scalar(kk[:, i, :], kz[:, i, :], vec[:, 2, i:i + 1], None, ALU.mult).then_inc(*scaled_k.inc())
                    dve.wait_ge(*scaled_k.at(i + 1))
                    V.tensor_tensor(t1[:, i, :], kk[:, i, :], kk[:, i, :], ALU.mult).then_inc(*squared.inc())
                V.memset(w2a2[HD:P, 0], 0.0).then_inc(*padded.inc())
                V.memset(w2a2[0:HD, 1], 0.0).then_inc(*padded.inc())
                unit(0)
                unit(1)
                for i in range(3):
                    dve.wait_ge(*sig.at(i + 1))
                    V.tensor_tensor_scan(L[:, i, :], k.const("first"), sg[:, i, :], 0.0, ALU.mult, ALU.add).then_inc(*scanned.inc())
                dve.wait_ge(*scanned.at(3))
                Lc = L[:].rearrange("p i (b t) -> p (i b) t", t=P)
                lm = lam[:].rearrange("p i b e -> p (i b) e")
                V.tensor_copy(lm[:, :, 0], Lc[:, :, P // 2]).then_inc(*middle.inc())
                dve.wait_ge(*middle.at(1))
                V.tensor_tensor(Lc, Lc, lm[:, :, 0:1].broadcast_to([P, 12, P]), ALU.subtract).then_inc(*centred.inc())
                unit(2)
                dve.wait_ge(*centred.at(1))
                V.tensor_copy(lm[:, :, 1], Lc[:, :, P - 1]).then_inc(*ends.inc())
                dve.wait_ge(*unit_k.at(3))
                V.tensor_tensor(t1[:], L[:], sg[:], ALU.subtract).then_inc(*before.inc())
                dve.wait_ge(*exps.at(1))
                V.tensor_tensor(kr[:, :, 1, :], r, up[:], ALU.mult).then_inc(*out.inc())
                dve.wait_ge(*exps.at(3))
                V.tensor_tensor(kr[:, :, 0, :], kk[:], t1[:], ALU.mult).then_inc(*out.inc())
                dve.wait_ge(*out.at(2))
                dve.wait_ge(*k2.at(9))
                for i in range(3):
                    V.scalar_tensor_tensor(out=t1[:, i, :], in0=r[:, i, :], scalar=vec[:, 4, i:i + 1], in1=kh[:, i, :],
                                           op0=ALU.mult, op1=ALU.mult).then_inc(*rk.inc())
                dve.wait_ge(*rk.at(3))
                V.tensor_tensor(kh[:], kh[:], down[:], ALU.mult).then_inc(*out.inc())
                dve.wait_ge(*ka.at(3))
                V.tensor_tensor(bh[:], bh[:], down[:], ALU.mult).then_inc(*out.inc())


def invert_phase(k, A, yx, tt):
    nc = k.nc
    k.phase()
    first, t_made, t_out, p_made, joined = (k.sem(s) for s in ("inv_first", "inv_t_made", "inv_t_out", "inv_p_made", "inv_joined"))
    with nc.Block() as block:
        sizes = [2, 4, 8, 16, 32, 64]
        rounds = [(b, g) for b in sizes for g in range(6)]

        def batch(t, g):
            return t[:, 4 * g:4 * g + 4]

        @block.vector
        def _(dve):
            j1t = k.const("join1T").unsqueeze(1).broadcast_to([P, 4, P])
            idb = k.ident.unsqueeze(1).broadcast_to([P, 4, P])
            for g in range(6):
                nc.vector.tensor_tensor(batch(yx, g)[:, :, 1], batch(A, g), j1t, ALU.mult).then_inc(*first.inc())
            for g in range(6):
                dve.wait_ge(*first.at(g + 1))
                for e in range(2):
                    nc.vector.tensor_tensor(batch(yx, g)[:, :, e], idb, batch(yx, g)[:, :, e], ALU.subtract).then_inc(*joined.inc())

            def out_t(n):
                b, g = rounds[n]
                dve.wait_ge(*t_made.at(n + 1))
                if n >= 2:
                    dve.wait_ge(*p_made.at(n - 1))
                if b == P // 2:
                    nc.vector.tensor_copy(tt[0:b, n % 2, :, b:P], k.pm[0:b, n % 2, :].rearrange("p (a b) -> p a b", a=4)[:, :, b:P]).then_inc(*t_out.inc())
                    return
                m = k.const(f"join{b}").unsqueeze(1).broadcast_to([P, 4, P])
                nc.vector.tensor_tensor(tt[:, n % 2], k.pm[:, n % 2, :].rearrange("p (a b) -> p a b", a=4), m, ALU.mult).then_inc(*t_out.inc())

            def out_p(n):
                b, g = rounds[n]
                dve.wait_ge(*p_made.at(n + 1))
                if b == P // 2:
                    new = batch(yx, g)[0:b, :, 0, b:P]
                    nc.vector.tensor_tensor(new, new, k.pl[0:b, 2 * (n % 2), 0:4 * b].rearrange("p (a b) -> p a b", a=4), ALU.subtract).then_inc(*joined.inc())
                    return
                nc.vector.tensor_tensor(batch(yx, g), batch(yx, g), k.pl[:, 2 * (n % 2):2 * (n % 2) + 2, :].rearrange("p h (a e b) -> p (h a) e b", e=2, a=2), ALU.subtract).then_inc(*joined.inc())

            for n in range(len(rounds) + 1):
                if n < len(rounds):
                    out_t(n)
                if n:
                    out_p(n - 1)

        @block.tensor
        def _(pe):
            def first_product(n):
                b, g = rounds[n]
                pe.wait_ge(*joined.at(2 * g + 2 if b == 2 else 12 + n - 6 + 1))
                if n >= 2:
                    pe.wait_ge(*t_out.at(n - 1))
                for a in range(4):
                    q = 4 * g + a
                    if b == P // 2:
                        m = nc.tensor.matmul(k.pm[0:b, n % 2, P * a + b:P * a + P], A[:, q, 0:b], yx[:, q, 0, b:P], start=True, stop=True)
                        continue
                    m = nc.tensor.matmul(k.pm[:, n % 2, P * a:P * a + P], A[:, q], yx[:, q, 0], start=True, stop=True)
                m.then_inc(*t_made.inc())

            def second_product(n):
                b, g = rounds[n]
                pe.wait_ge(*t_out.at(n + 1))
                if n >= 2:
                    pe.wait_ge(*joined.at(12 + n - 1))
                for a in range(4):
                    q = 4 * g + a
                    if b == P // 2:
                        m = nc.tensor.matmul(k.pl[0:b, 2 * (n % 2), b * a:b * a + b], yx[0:b, q, 1, 0:b], tt[0:b, n % 2, a, b:P], start=True, stop=True)
                        continue
                    bank = k.pl[:, 2 * (n % 2) + a // 2, :]
                    at = 2 * P * (a % 2)
                    nc.tensor.matmul(bank[:, at:at + P], yx[:, q, 1], tt[:, n % 2, a], start=True, stop=True)
                    m = nc.tensor.matmul(bank[:, at + P:at + 2 * P], tt[:, n % 2, a], yx[:, q, 1], start=True, stop=True)
                m.then_inc(*p_made.inc())

            for n in range(len(rounds) + 1):
                if n < len(rounds):
                    first_product(n)
                if n:
                    second_product(n - 1)


class HeadNorm:

    def __init__(self, k, ctx, o, tm, bonus, gate):
        def sb(name, shape):
            return ctx.enter_context(k.nc.sbuf_tensor(k.unique("hn_" + name), shape, F32))
        self.k, self.o, self.tm, self.bonus, self.gate = k, o, tm, bonus, gate
        self.gw, self.sq, self.mean, self.extra = sb("gw", [P, 2, RW]), sb("sq", [P, 6, HD]), sb("mean", [P, TB, 2, 6]), sb("extra", [P, RW])
        self.loaded, self.step, self.centred, self.var, self.std, self.inv = (k.sem("hn_" + s) for s in ("loaded", "step", "centred", "var", "std", "inv"))

    def sync(self, sp):
        for n, name in enumerate(("rw_gn_w_2", "rw_gn_b_2")):
            sp.dma_start(self.gw[:, n, :], self.k.io[name].broadcast_to([P, RW])).then_inc(*self.loaded.dma())

    def chunk(self, eng, ns, b, o_out):
        step, mean = self.step, self.mean[:, b]
        ob = self.o[:, b, :]
        oh = ob.rearrange("p (h v) -> p h v", v=HD)

        def done(i):
            i.then_inc(*step.inc())
            eng.wait_ge(*step.at(step.total - step.base))

        def per_head(t):
            return t.unsqueeze(2).broadcast_to([P, 6, HD])

        if b == 0:
            eng.wait_ge(*self.loaded.dma_at(2))
        elif b == TB - 1:
            eng.wait_ge(*step.at(step.total - step.base))
        done(ns.tensor_tensor(self.extra[:].rearrange("p (h v) -> p h v", v=HD), self.tm[:, b, 3, :].rearrange("p (h v) -> p h v", v=HD),
                              per_head(self.bonus[:, b, :]), ALU.mult))
        eng.wait_ge(*o_out.at(6 * b + 6))
        done(ns.tensor_scalar(mean[:, 0, :], mean[:, 0, :], 1.0 / HD, None, ALU.mult))
        ns.tensor_tensor(oh, oh, per_head(mean[:, 0, :]), ALU.subtract).then_inc(*self.centred.inc())
        if b == TB - 1:
            self.invert(eng, b)
        eng.wait_ge(*self.inv.at(b + 1))
        done(ns.tensor_tensor(oh, oh, per_head(mean[:, 1, :]), ALU.mult))
        done(ns.tensor_tensor(ob, ob, self.gw[:, 0, :], ALU.mult))
        done(ns.tensor_tensor(ob, ob, self.gw[:, 1, :], ALU.add))
        done(ns.tensor_tensor(ob, ob, self.extra[:], ALU.add))
        done(ns.tensor_tensor(ob, ob, self.gate[:, b, :], ALU.mult))

    def scalar(self, act, b, source, o_out):
        nc, mean = self.k.nc, self.mean[:, b]
        oh = self.o[:, b, :].rearrange("p (h v) -> p h v", v=HD)
        for h in range(6):
            nc.scalar.activation(oh[:, h], source(h), ACT.Copy, accum_out=mean[:, 0, h:h + 1]).then_inc(*o_out.inc())
        act.wait_ge(*self.centred.at(b + 1))
        for h in range(6):
            nc.scalar.activation(self.sq[:, h], oh[:, h], ACT.Square, accum_out=mean[:, 1, h:h + 1]).then_inc(*self.var.inc())
        act.wait_ge(*self.var.at(6 * b + 6))
        nc.scalar.activation(mean[:, 1, :], mean[:, 1, :], ACT.Sqrt, bias=self.k.eps[:, 1:2], scale=1.0 / HD).then_inc(*self.std.inc())

    def invert(self, dve, b):
        dve.wait_ge(*self.std.at(b + 1))
        v = self.mean[:, b, 1, :]
        self.k.nc.vector.reciprocal(v, v).then_inc(*self.inv.inc())


def compress_buffers(k, ctx):
    def sb(name, shape):
        return ctx.enter_context(k.nc.sbuf_tensor(k.unique("cp_" + name), shape, F32))
    return {name: dict(raw=sb("raw", [CMP_LEN // 2, P]), w1=sb("w1", [P, CMP_LEN // 2, P]), w2=sb("w2", [P, HD])) for name in "kv"}


def load_compress(k, sp, buffers):
    loaded = k.sem("cp_loaded")
    for name, b in buffers.items():
        sp.dma_start(b["raw"][:], k.io[f"cmp_pe_{name}_2"][0].rearrange("(l e) d -> l (e d)", e=2)).then_inc(*loaded.dma())
        w1 = k.io[f"cmp_w1_{name}_2"][0].rearrange("(l p) n -> p l n", p=P)
        for l in (0, CMP_LEN // 4):
            sp.dma_start(b["w1"][:, l:l + CMP_LEN // 4, :], w1[:, l:l + CMP_LEN // 4, :]).then_inc(*loaded.dma())
        sp.dma_start(b["w2"][:], k.io[f"cmp_w2_{name}_2"][0]).then_inc(*loaded.dma())


def compress_phase(k, buffers, kc, vc, kcmp, vcmp):
    nc = k.nc
    k.phase()
    pe_turned, pe_out, doubled, windows, hid_made, hid_out, out_made, out = (k.sem(s) for s in (
        "cp_pe_turned", "cp_pe_out", "cp_doubled", "cp_windows", "cp_hid_made", "cp_hid_out", "cp_out_made", "out_ready"))
    L2 = CMP_LEN // 2
    with nc.sbuf_tensor(k.unique("cp_pe"), [P, 2, L2], F32) as pe_t, nc.sbuf_tensor(k.unique("cp_win"), [P, 2, L2, 2, NC], F32) as win, \
            nc.sbuf_tensor(k.unique("cp_hid"), [P, 2, 2, NC], F32) as hid, nc.Block() as block:
        @block.tensor
        def _(pe):
            pe.wait_ge(*k.sem("cp_loaded").at(0))
            for n, b in enumerate(buffers.values()):
                nc.tensor.transpose(k.pm[:, n, 0:L2], b["raw"][:], k.ident[0:L2, 0:L2]).then_inc(*pe_turned.inc())
            for n, x in enumerate((kc, vc)):
                for g in range(2):
                    m = nc.tensor.matmul(k.pl[:, 2 * n + g, :], k.const(f"twice{g}"), x, start=True, stop=True)
                m.then_inc(*doubled.inc())
            for n, b in enumerate(buffers.values()):
                pe.wait_ge(*windows.at(4 * n + 4))
                for l in range(L2):
                    m = nc.tensor.matmul(k.pm[:, 2 + n, 0:2 * NC], b["w1"][:, l, :], win[:, n, l].rearrange("p g n -> p (g n)"), start=l == 0, stop=l == L2 - 1)
                m.then_inc(*hid_made.inc())
            for n, b in enumerate(buffers.values()):
                pe.wait_ge(*hid_out.at(n + 1))
                for g in range(2):
                    if n:
                        m = nc.tensor.matmul(k.pm[0:NC, 1, HD * g:HD * g + HD], hid[:, n, g, :], b["w2"][:], start=True, stop=True)
                    else:
                        m = nc.tensor.matmul(k.pm[HD * g:HD * g + HD, 0, 0:NC], b["w2"][:], hid[:, n, g, :], start=True, stop=True)
                m.then_inc(*out_made.inc())

        @block.scalar
        def _(act):
            for n in range(2):
                act.wait_ge(*hid_made.at(n + 1))
                nc.scalar.activation(hid[:, n], k.pm[:, 2 + n, 0:2 * NC].rearrange("p (g n) -> p g n", g=2), ACT.Gelu_apprx_tanh).then_inc(*hid_out.inc())

        @block.vector
        def _(dve):
            for n in range(2):
                dve.wait_ge(*pe_turned.at(n + 1))
                nc.vector.tensor_copy(pe_t[:, n], k.pm[:, n, 0:L2]).then_inc(*pe_out.inc())
            dve.wait_ge(*pe_out.at(2))
            for n in range(2):
                dve.wait_ge(*doubled.at(n + 1))
                for odd in range(2):
                    r = slice(HD * odd, HD * odd + HD)
                    x = k.pl[r, 2 * n:2 * n + 2, :].rearrange("p g (n l e) -> p e l g n", e=2, l=CMP_STRIDE // 2)[:, odd]
                    for half in range(2):
                        lo = CMP_STRIDE // 2 * half
                        code = pe_t[r, n, lo:lo + CMP_STRIDE // 2].unsqueeze(2).unsqueeze(3).broadcast_to([HD, CMP_STRIDE // 2, 2, NC])
                        nc.vector.tensor_tensor(win[r, n, lo:lo + CMP_STRIDE // 2], x[:, :, :, half:half + NC], code, ALU.add).then_inc(*windows.inc())
            dve.wait_ge(*out_made.at(1))
            nc.vector.tensor_copy(kcmp, k.pm[:, 0, 0:NC]).then_inc(*out.inc())
            dve.wait_ge(*out_made.at(2))
            nc.vector.tensor_copy(vcmp[0:NC].rearrange("p g d -> p (g d)"), k.pm[0:NC, 1, 0:P]).then_inc(*out.inc())


class S5:

    def __init__(self, k, ctx, spare):
        self.k = k

        def sb(name, shape):
            return ctx.enter_context(k.nc.sbuf_tensor(k.unique("s5_" + name), shape, F32))
        self.par = sb("par", [P, 16, 8])
        self.bt = sb("bt", [P, 2, 2, P])
        self.ct = sb("ct", [P, 2, 2, P])
        self.rot = [sb("rot", [P, 8, S]), spare]

    def work_buffers(self, ctx):
        def sb(name, shape):
            return ctx.enter_context(self.k.nc.sbuf_tensor(self.k.unique("s5_" + name), shape, F32))
        self.scs, self.tmp = sb("sincos", [P, 2, 8]), sb("tmp", [P, 2, 8])
        self.braw, self.bx = sb("braw", [P, 2, 8, 16]), sb("bx", [P, 2, 8, 2, 16])
        self.craw, self.btmp = sb("craw", [P, 2, 2, 2, HD]), sb("btmp", [P, 2, 8, 16])
        self.rt, self.pw = sb("rt", [P, 4, P]), sb("pw", [P, 2, 2, 8])
        self.marks = {}

    def sync(self, sp):
        k, io = self.k, self.k.io
        loaded = k.sem("s5_loaded")
        for g in range(2):
            row = io["s5_log_dt_2"].rearrange("o (i g) -> g o i", g=2)[g]
            sp.dma_start(self.par[HD * g:HD * g + HD, 2, :], row.broadcast_to([HD, 8]), allow_slow_non_contiguous=True)\
                .then_inc(*loaded.dma())
        for n, name in enumerate(("s5_b_re_2", "s5_b_im_2")):
            for g in range(2):
                sp.dma_start(self.braw[HD * g:HD * g + HD, n], io[name][0].rearrange("(i g) p c -> g p i c", g=2)[g]).then_inc(*loaded.dma())
        for n, name in enumerate(("s5_c_re_2", "s5_c_im_2")):
            for g in range(2):
                sp.dma_start(self.craw[:, n, :, g, :], io[name][0].rearrange("(h q) c p -> (q c) h p", h=2)).then_inc(*loaded.dma())

    LOADS = 10

    def vector(self, dve):
        k, par, scs, rot, rt, pw = self.k, self.par, self.scs, self.rot, self.rt, self.pw
        braw, bx, craw, btmp, marks = self.braw, self.bx, self.craw, self.btmp, self.marks
        nc, step, loaded, sines, exps = k.nc, k.sem("s5_step"), k.sem("s5_loaded"), k.sem("s5_sines"), k.sem("s5_exps")
        turned, emptied = k.sem("s5_turned"), k.sem("s5_emptied")

        def st(i):
            i.then_inc(*step.inc())
            dve.wait_ge(*step.at(step.total - step.base))
        V = nc.vector
        M, Ad, Su = ALU.mult, ALU.add, ALU.subtract
        def q(n):
            return (k.vec("s5_lam_re_2"), k.vec("s5_lam_im_2"))[n] if n < 2 else par[:, n, :]
        dve.wait_ge(*loaded.dma_at(self.LOADS))
        dve.wait_ge(*exps.at(1))
        st(V.tensor_tensor(q(4), q(1), q(2), M))
        st(V.tensor_tensor(q(3), q(0), q(2), M))
        marks["exp"] = step.total - step.base
        sincos(k, dve, q(4), scs, self.tmp, step)
        marks["sine"] = step.total - step.base
        dve.wait_ge(*sines.at(2))
        sn, cs = scs[:, 0], scs[:, 1]
        st(V.tensor_tensor(q(5), q(3), cs, M))
        st(V.tensor_tensor(q(6), q(3), sn, M))
        st(V.tensor_tensor(q(7), q(0), q(0), M))
        st(V.tensor_tensor(q(8), q(1), q(1), M))
        st(V.tensor_tensor(q(7), q(7), q(8), Ad))
        st(V.reciprocal(q(7), q(7)))
        st(V.tensor_scalar(q(8), q(5), -1.0, None, Ad))
        st(V.tensor_tensor(q(9), q(8), q(0), M))
        st(V.tensor_tensor(q(10), q(6), q(1), M))
        st(V.tensor_tensor(q(9), q(9), q(10), Ad))
        st(V.tensor_tensor(q(9), q(9), q(7), M))
        st(V.tensor_tensor(q(10), q(6), q(0), M))
        st(V.tensor_tensor(q(11), q(8), q(1), M))
        st(V.tensor_tensor(q(10), q(10), q(11), Su))
        st(V.tensor_tensor(q(10), q(10), q(7), M))
        def over_c(n):
            return q(n).unsqueeze(2).broadcast_to([P, 8, 16])
        st(V.memset(bx[:], 0.0))
        for part in range(2):
            st(V.tensor_tensor(btmp[:, 0], braw[:, part], over_c(9), M))
            st(V.tensor_tensor(btmp[:, 1], braw[:, 1 - part], over_c(10), M))
            for g in range(2):
                r = slice(HD * g, HD * g + HD)
                st(V.tensor_tensor(bx[r, part, :, g, :], btmp[r, 0], btmp[r, 1], Ad if part else Su))
        for part in range(2):
            for g in range(2):
                st(V.tensor_scalar(craw[:, part, :, g, :], craw[:, part, :, g, :], k.const("pairsel")[:, g:g + 1],
                                   -1.0 if part else 1.0, M, M))
        marks["bc"] = step.total - step.base
        dve.wait_ge(*turned.at(1))
        V.tensor_copy(self.bt[:], k.pm[:, 0, :].rearrange("p (a h s) -> p a h s", a=2, h=2)).then_inc(*emptied.inc())
        V.tensor_copy(self.ct[:], k.pm[:, 1, :].rearrange("p (a h s) -> p a h s", a=2, h=2)).then_inc(*emptied.inc())
        st(V.memset(rot[0][:, :, 0:1], 1.0))
        st(V.memset(rot[1][:, :, 0:1], 0.0))
        st(V.tensor_copy(pw[:, 0, 0], cs))
        st(V.tensor_copy(pw[:, 0, 1], sn))
        n, cur = 1, 0
        while n < S:
            size, cols = max(1, min(8, P // n)), min(n, P)
            for i, a in [(i, a) for i in range(0, 8, size) for a in range(0, n, cols)]:
                t = slice(i, i + size)
                ra = [rt[:, x, 0:size * cols].rearrange("p (i n) -> p i n", n=cols) for x in range(4)]
                pr = pw[:, cur, 0, t].unsqueeze(2).broadcast_to([P, size, cols])
                pi = pw[:, cur, 1, t].unsqueeze(2).broadcast_to([P, size, cols])
                c0, s0 = rot[0][:, t, a:a + cols], rot[1][:, t, a:a + cols]
                V.tensor_tensor(ra[0], c0, pr, M).then_inc(*step.inc())
                V.tensor_tensor(ra[1], s0, pi, M).then_inc(*step.inc())
                V.tensor_tensor(ra[2], c0, pi, M).then_inc(*step.inc())
                st(V.tensor_tensor(ra[3], s0, pr, M))
                V.tensor_tensor(rot[0][:, t, n + a:n + a + cols], ra[0], ra[1], Su).then_inc(*step.inc())
                st(V.tensor_tensor(rot[1][:, t, n + a:n + a + cols], ra[2], ra[3], Ad))
            n *= 2
            if n < S:
                o = pw[:, cur]
                V.tensor_tensor(rt[:, 0, 0:8], o[:, 0], o[:, 0], M).then_inc(*step.inc())
                V.tensor_tensor(rt[:, 1, 0:8], o[:, 1], o[:, 1], M).then_inc(*step.inc())
                st(V.scalar_tensor_tensor(out=pw[:, 1 - cur, 1], in0=o[:, 0], scalar=2.0, in1=o[:, 1], op0=M, op1=M))
                st(V.tensor_tensor(pw[:, 1 - cur, 0], rt[:, 0, 0:8], rt[:, 1, 0:8], Su))
                cur = 1 - cur

    def scalar(self, act, i):
        k, par, scs = self.k, self.par, self.scs
        step, sines, exps = k.sem("s5_step"), k.sem("s5_sines"), k.sem("s5_exps")
        if i == 1:
            act.wait_ge(*k.sem("s5_loaded").dma_at(self.LOADS))
            k.nc.scalar.activation(par[:, 2, :], par[:, 2, :], ACT.Exp).then_inc(*exps.inc())
        elif i == 2:
            act.wait_ge(*step.at(self.marks["exp"]))
            k.nc.scalar.activation(par[:, 3, :], par[:, 3, :], ACT.Exp).then_inc(*sines.inc())
        elif i == 3:
            act.wait_ge(*step.at(self.marks["sine"]))
            k.nc.scalar.activation(scs[:], scs[:], ACT.Sin).then_inc(*sines.inc())

    def tensor(self, pe, i):
        if i != 5:
            return
        k = self.k
        pe.wait_ge(*k.sem("s5_step").at(self.marks["bc"]))
        for part in range(2):
            for h in range(2):
                at = P * (2 * part + h)
                k.nc.tensor.transpose(k.pm[:, 0, at:at + P], self.bx[:, part, 4 * h:4 * h + 4].rearrange("p i g c -> p (i g c)"), k.ident)
                m = k.nc.tensor.transpose(k.pm[:, 1, at:at + P], self.craw[:, part, h].rearrange("p g s -> p (g s)"), k.ident)
        m.then_inc(*k.sem("s5_turned").inc())


def s5_phase(k, s5, u, out, z, mu, compress):
    nc = k.nc
    par, bt, ct, rot, dsk = s5.par, s5.bt, s5.ct, s5.rot, k.vec("s5_d_2")
    with ExitStack() as ctx:
        def sb(name, shape):
            return ctx.enter_context(nc.sbuf_tensor(k.unique("s5_" + name), shape, F32))
        bu = sb("bu", [P, 4, S])
        wg = sb("wglu", [P, 2, 2 * CW])
        before, keep = sb("before", [P, 2, S]), sb("keep", [P, 11])
        w = sb("w", [P, 2, 2, S])
        sc = sb("scan", [P, 2, 2, S])
        back, yg = sb("back", [P, 4, S]), sb("y", [P, 2, S])
        k.phase()
        glu_loaded, kept, before_ready, shifted = k.sem("s5_glu_loaded"), k.sem("shift_kept"), k.sem("shift_before"), k.sem("shifted")
        made, prod, scanned, back_re, back_im, read = (k.sem(s) for s in ("s5_made", "products_ready", "s5_scanned", "s5_back_re", "s5_back_im", "s5_read"))
        in_re, in_im, state_re, state_im = (k.sem("s5_" + s) for s in ("in_re", "in_im", "state_re", "state_im"))
        ysum, ygelu, glu_made, gate_ready, out_done = (k.sem(s) for s in ("s5_ysum", "s5_ygelu", "s5_glu_made", "gate_ready", "out_ready"))
        with nc.Block() as block:
            @block.sync
            def _(sp):
                sp.dma_start(wg[:], k.io["s5_w_glu_2"][0].rearrange("(h p) n -> p h n", p=P)).then_inc(*glu_loaded.dma())
                load_compress(k, sp, compress)

            @block.tensor
            def _(pe):
                def project(i):
                    h, r = i // 4, slice(32 * (i % 4), 32 * (i % 4) + 32)
                    if i >= 2:
                        pe.wait_ge(*prod.at(4 * (i - 1)))
                    for part in range(2):
                        m = nc.tensor.matmul(k.pl[:, 2 * (i % 2) + part, :], bt[r, part, h, :], u[r, h, :], start=True, stop=True)
                    m.then_inc(*made.inc())

                def mix(i):
                    h, r = i // 4, slice(32 * (i % 4), 32 * (i % 4) + 32)
                    pe.wait_ge(*state_re.at(i + 1))
                    pe.wait_ge(*state_im.at(i + 1))
                    for part in range(2):
                        m = nc.tensor.matmul(k.pm[r, h, :], ct[:, part, h, r], w[:, i % 2, part, :], start=part == 0, stop=part == 1)
                    m.then_inc(*read.inc())
                project(0)
                project(1)
                for i in range(8):
                    if i < 6:
                        project(i + 2)
                    mix(i)
                pe.wait_ge(*glu_loaded.dma_at(1))
                pe.wait_ge(*ygelu.at(2))
                for c in range(4):
                    for h in range(2):
                        m = nc.tensor.matmul(k.pl[:, c, :], wg[:, h, P * c:P * c + P], yg[:, h, :], start=h == 0, stop=h == 1)
                m.then_inc(*glu_made.inc())

            @block.vector
            def _(dve):
                V, M, Ad, Su = nc.vector, ALU.mult, ALU.add, ALU.subtract

                def shift(i):
                    dve.wait_ge(*before_ready.at(i + 1))
                    V.scalar_tensor_tensor(out=z[:, i, 1:S + 1], in0=z[:, i, 1:S + 1], scalar=keep[:, i:i + 1],
                                           in1=before[:, i % 2, :], op0=M, op1=Ad).then_inc(*shifted.inc())

                V.tensor_scalar(keep[:], mu, -1.0, 1.0, M, Ad).then_inc(*kept.inc())
                dve.wait_ge(*kept.at(1))
                for i in range(3):
                    shift(i)
                for i in range(9):
                    if i:
                        shift(i + 2)
                    if i < 8:
                        c, s = rot[0][:, i, :], rot[1][:, i, :]
                        dve.wait_ge(*made.at(i + 1))
                        re, im = k.pl[:, 2 * (i % 2), :], k.pl[:, 2 * (i % 2) + 1, :]
                        if i:
                            dve.wait_ge(*in_re.at(i))
                            dve.wait_ge(*in_im.at(i))
                        V.tensor_tensor(bu[:, 2], im, c, M).then_inc(*prod.inc())
                        V.tensor_tensor(bu[:, 3], re, s, M).then_inc(*prod.inc())
                        V.tensor_tensor(bu[:, 0], re, c, M).then_inc(*prod.inc())
                        V.tensor_tensor(bu[:, 1], im, s, M).then_inc(*prod.inc())
                    if i:
                        c, s, e = rot[0][:, i - 1, :], rot[1][:, i - 1, :], (i - 1) % 2
                        dve.wait_ge(*scanned.at(2 * i))
                        V.tensor_tensor(back[:, 0], sc[:, e, 0], c, M).then_inc(*back_re.inc())
                        V.tensor_tensor(back[:, 1], sc[:, e, 1], s, M).then_inc(*back_re.inc())
                        dve.wait_ge(*back_re.at(2 * i))
                        V.tensor_tensor(w[:, e, 0], back[:, 0], back[:, 1], Su).then_inc(*state_re.inc())
                    if i < 8:
                        dve.wait_ge(*prod.at(4 * i + 4))
                        if i >= 2:
                            dve.wait_ge(*read.at(i - 1))
                        V.tensor_tensor(w[:, i % 2, 0], bu[:, 0], bu[:, 1], Ad).then_inc(*in_re.inc())
                        dve.wait_ge(*in_re.at(i + 1))
                        if i >= 2:
                            dve.wait_ge(*back_im.at(2 * (i - 1)))
                            dve.wait_ge(*back_re.at(2 * (i - 1)))
                        mag = par[:, 3, i:i + 1].broadcast_to([P, S])
                        V.tensor_tensor_scan(sc[:, i % 2, 0], mag, w[:, i % 2, 0], 0.0, M, Ad).then_inc(*scanned.inc())
                        dve.wait_ge(*in_im.at(i + 1))
                        V.tensor_tensor_scan(sc[:, i % 2, 1], mag, w[:, i % 2, 1], 0.0, M, Ad).then_inc(*scanned.inc())
                dve.wait_ge(*read.at(8))
                for h in range(2):
                    V.scalar_tensor_tensor(out=yg[:, h], in0=u[:, h, :], scalar=dsk[:, h:h + 1], in1=k.pm[:, h, :], op0=M, op1=Ad).then_inc(*ysum.inc())
                dve.wait_ge(*gate_ready.at(2))
                for h in range(2):
                    V.tensor_tensor(out[:, h, :], k.pl[:, h, :], bu[:, h], M).then_inc(*out_done.inc())

            @block.gpsimd
            def _(pool):
                V, M, Ad, Su = nc.gpsimd, ALU.mult, ALU.add, ALU.subtract
                for i in range(9):
                    if i < 8:
                        pool.wait_ge(*prod.at(4 * i + 2))
                        if i >= 2:
                            pool.wait_ge(*read.at(i - 1))
                        V.tensor_tensor(w[:, i % 2, 1], bu[:, 2], bu[:, 3], Su).then_inc(*in_im.inc())
                    if i:
                        c, s, e = rot[0][:, i - 1, :], rot[1][:, i - 1, :], (i - 1) % 2
                        pool.wait_ge(*scanned.at(2 * i))
                        if i > 1:
                            pool.wait_ge(*state_im.at(i - 1))
                        V.tensor_tensor(back[:, 2], sc[:, e, 0], s, M).then_inc(*back_im.inc())
                        V.tensor_tensor(back[:, 3], sc[:, e, 1], c, M).then_inc(*back_im.inc())
                        pool.wait_ge(*back_im.at(2 * i))
                        V.tensor_tensor(w[:, e, 1], back[:, 2], back[:, 3], Ad).then_inc(*state_im.inc())

            @block.scalar
            def _(act):
                for i in range(11):
                    if i >= 2:
                        act.wait_ge(*shifted.at(i - 1))
                    nc.scalar.activation(before[:, i % 2, :], z[:, i, 0:S], ACT.Copy, scale=mu[:, i:i + 1]).then_inc(*before_ready.inc())
                for h in range(2):
                    act.wait_ge(*ysum.at(h + 1))
                    nc.scalar.activation(yg[:, h], yg[:, h], ACT.Gelu_apprx_tanh).then_inc(*ygelu.inc())
                act.wait_ge(*glu_made.at(1))
                act.wait_ge(*in_im.at(8))
                act.wait_ge(*in_re.at(8))
                for h in range(2):
                    nc.scalar.activation(bu[:, h], k.pl[:, 2 + h, :], ACT.Sigmoid).then_inc(*gate_ready.inc())


def gate_phase(k, g0, x, out, e):
    nc = k.nc
    k.phase()
    todo = split_ahead(k, NSLABS)
    x_hi, x_lo = k.sem("x_hi"), k.sem("x_lo")
    gate_ready, prod_ready, added = k.sem("gate_ready"), k.sem("products_ready"), k.sem("out_ready")
    with nc.sbuf_tensor(k.unique("plg"), [P, 2, 2, S], F32) as ga, nc.sbuf_tensor(k.unique("x_hi"), [P, KD, S], F32R) as xh, \
            nc.sbuf_tensor(k.unique("x_lo"), [P, KD, S], F32R) as xl, nc.Block() as block:
        parts = (xh, xl)

        @block.sync
        def _(sp):
            for g in range(g0 + 2, g0 + 4):
                issue_slab(k, sp, g)

        @block.tensor
        def _(pe):
            for i in range(4):
                g = g0 + i
                j = g % 2
                use_slab(k, pe, j, g // 2)
                if i >= 2:
                    pe.wait_ge(*gate_ready.at(i - 1))
                w = [slab_view(k, j, a) for a in range(2)]
                for c in range(2):
                    for q in range(KD):
                        if i == 0 and c == 0:
                            pe.wait_ge(*x_lo.at(q + 1))
                        m = product(nc, k.pl[:, 2 * j + c, :], [([w[a][:, q, P * c:P * c + P] for a in range(2)],
                                                                 [parts[a][:, q, :] for a in range(2)])], q == 0, q == KD - 1)
                m.then_inc(k.slab_done[j], 1)

        @block.scalar
        def _(act):
            split_x(k, act, None, x, parts, x_hi, x_lo)
            for i in range(-2, 4):
                g = g0 + i
                j = g % 2
                if g + 2 in todo:
                    hi_of_slab(k, act, j, g // 2 + 1, loaded_value(g + 2))
                if i >= 0:
                    act.wait_ge(k.slab_done[j], g // 2 + 1)
                    if i >= 2:
                        act.wait_ge(*prod_ready.at(i - 1))
                    nc.scalar.activation(ga[:, j], k.pl[:, 2 * j:2 * j + 2, :], ACT.Sigmoid).then_inc(*gate_ready.inc())

        @block.vector
        def _(dve):
            split_x(k, None, dve, x, parts, x_hi, x_lo)
            for i in range(4):
                t = slice(2 * i, 2 * i + 2)
                dve.wait_ge(*gate_ready.at(i + 1))
                nc.vector.tensor_tensor(e[:, t, :], e[:, t, :], ga[:, (g0 + i) % 2], ALU.mult).then_inc(*prod_ready.inc())
                dve.wait_ge(*prod_ready.at(i + 1))
                nc.vector.tensor_tensor(out[:, t, :], e[:, t, :], x[:, t, :], ALU.add).then_inc(*added.inc())

        @block.gpsimd
        def _(pool):
            for g in todo:
                lo_of_slab(k, pool, g % 2, g // 2)


def two_blocks(nc, io, out):
    ctx = ExitStack()
    with ctx:
        k = Kit(nc, ctx, io)

        def sb(name, shape, dt=F32):
            return ctx.enter_context(nc.sbuf_tensor(name, shape, dt))

        k.tables[0] = sb("table", [P, k.widths[0]])
        k.ring = sb("ring", [P, 2, SLAB])
        xT, hT = sb("xT", [P, KD, S]), sb("hT", [P, KD, S])
        k.eps = sb("eps", [P, 2])
        k.vecs = sb("vecs", [P, 3 * P])
        k.pl = ctx.enter_context(nc.psum_tensor("pl", [P, 4, 512], F32))
        k.pm = ctx.enter_context(nc.psum_tensor("pm", [P, 4, 512], F32))
        k.slab_loaded = [ctx.enter_context(nc.semaphore(f"slab_loaded{j}")) for j in range(2)]
        k.slab_done = [ctx.enter_context(nc.semaphore(f"slab_done{j}")) for j in range(2)]
        k.slab_hi = [ctx.enter_context(nc.semaphore(f"slab_hi{j}")) for j in range(2)]
        k.slab_lo = [ctx.enter_context(nc.semaphore(f"slab_lo{j}")) for j in range(2)]
        k.split_done = 0
        k.ones, k.ident = k.const("ones"), k.const("ident")
        G = {n: k.vec(n) for n in ("g_pre_mix", "g_mem", "g_post_mix", "g_pre_mlp", "g_post_mlp", "pre_mix_norm_2",
                                   "post_mix_norm_2", "pre_ffn_norm_2", "post_ffn_norm_2")}
        G["mix"] = k.vec("g_attn_out", KD)
        gple, mu = k.vec("ple_norm_2"), k.vec("shift_mu_2")

        k.phase()
        eps_set, consts_loaded, rows_turned, rows_out = (k.sem(s) for s in ("eps_set", "consts_loaded", "rows_turned", "rows_out"))
        splitting, projected = ExitStack(), ExitStack()
        splitting.enter_context(k.splitting())
        qkv = projected.enter_context(nc.sbuf_tensor(k.unique("qkv"), [P, TB, 3 * AW], F32))
        flat = qkv[:].rearrange("p b f -> p (b f)")
        xin, memin = (flat[:, at:at + n * D].rearrange("p (b d) -> p b d", d=D) for at, n in ((0, TB), (TB * D, NM // P)))
        input_loaded = k.sem("input_loaded")
        with nc.sbuf_tensor(k.unique("rows"), [P, 3, P], F32) as rows, nc.Block() as block:
            @block.gpsimd
            def _(pool):
                nc.gpsimd.memset(k.eps[:, 0:1], EPS).then_inc(*eps_set.inc())
                nc.gpsimd.memset(k.eps[:, 1:2], GN_EPS).then_inc(*eps_set.inc())
                nc.gpsimd.memset(rows[:], 0.0).then_inc(*eps_set.inc())

            @block.sync
            def _(sp):
                sp.dma_start(k.tables[0][:], io["table"]).then_inc(*consts_loaded.dma())
                sp.dma_start(xin, io["x"][0].rearrange("(b p) d -> p b d", p=P)).then_inc(*input_loaded.dma())
                sp.wait_ge(*eps_set.at(3))
                for name, n in VECTORS:
                    at, flat = k.vec_at[name], io[name]
                    while len(flat.shape) > 1:
                        flat = flat.rearrange("a b -> (a b)") if len(flat.shape) == 2 else flat.rearrange("a b c -> (a b) c")
                    flat = flat.rearrange("(n p) -> n p", p=P)
                    done = 0
                    while done < n:
                        r, c = (at + done) % P, (at + done) // P
                        m = min(n - done, P - r)
                        sp.dma_start(rows[r:r + m, c, :], flat[done:done + m]).then_inc(*consts_loaded.dma())
                        done += m
                sp.dma_start(memin, io["mem"][0].rearrange("(b p) d -> p b d", p=P)).then_inc(*input_loaded.dma())
                for g in range(2):
                    issue_slab(k, sp, g)

            @block.tensor
            def _(pe):
                pe.wait_ge(*consts_loaded.at(consts_loaded.total - consts_loaded.base))
                for r in range(3):
                    m = nc.tensor.transpose(k.pm[:, 0, P * r:P * r + P], rows[:, r, :], k.ident)
                m.then_inc(*rows_turned.inc())

            @block.vector
            def _(dve):
                dve.wait_ge(*rows_turned.at(1))
                nc.vector.tensor_copy(k.vecs[:], k.pm[:, 0, 0:3 * P]).then_inc(*rows_out.inc())

        with nc.sbuf_tensor(k.unique("cz6"), [P, 6, S], F32) as cz6, \
                nc.sbuf_tensor(k.unique("qx"), [P, 2, 2, S], F32) as qx, nc.sbuf_tensor(k.unique("kx"), [P, 2, NM], F32) as kx, \
                nc.sbuf_tensor(k.unique("vx"), [P, 2, XW], F32) as vx:
            def padded(q, i):
                return q[0:HD, 0, i, :], q[HD:P, 1, i, :]

            def other_halves(q):
                return q[HD:P, 0], q[0:HD, 1]

            with nc.sbuf_tensor(k.unique("memT"), [P, KD, NM], F32) as memT:
                banks = [([xin[:, b, P * f:P * f + P] for b in range(TB)], xT[:, f, :]) for f in range(KD)]
                banks += [([memin[:, b, P * f:P * f + P] for b in range(2)], memT[:, f, :]) for f in range(KD)]
                turn_phase(k, banks, after=input_loaded)
                norm_phase(k, [dict(x=xT, out=hT, gain=G["g_pre_mix"]), dict(x=memT, out=memT, gain=G["g_mem"], n=NM)], ahead=2)
                slabs = [dict(kind="tokens", to=qkv[:, :, 256 * i:256 * i + 256]) for i in range(6)]
                slabs += [dict(kind="features", to=lambda c, i=i: cz6[:, 2 * i + c, :]) for i in range(3)]
                slabs += [dict(kind="features", to=lambda c: padded(qx, c))]
                slabs += [dict(kind="features", to=lambda c: kx[:, c, :], source=1)]
                slabs += [dict(kind="tokens", to=vx, source=1)]
                with ExitStack() as work:
                    beside = RopeAndConv(k, work, qkv, cz6, hT[:, 4:6, :])
                    product_phase(k, IN1, slabs, [(hT, KD, S), (memT, KD, NM)], beside=beside, zero=other_halves(qx))
            with nc.sbuf_tensor(k.unique("qT"), [P, 2, 4, S], F32) as qT, nc.sbuf_tensor(k.unique("kT"), [P, 4, S], F32) as kT:
                turn_phase(k, [([qkv[:, b, P * f:P * f + P] for b in range(TB)], padded(qT, f) if f < 4 else kT[:, f - 4, :]) for f in range(8)],
                           zero=other_halves(qT))
                groups = []
                for i in range(4):
                    for b in range(TB):
                        w = P * (b + 1)
                        units = [dict(q=qT[:, e, i, P * b:P * b + P], k=kT[:, i, 0:w], mask=k.const("band")[:, S - w:S], half=e,
                                      v=lambda a, h=2 * i + e: qkv[:, a, 2 * AW + HD * h:2 * AW + HD * h + HD]) for e in range(2)]
                        groups.append((units, hT[:, i, P * b:P * b + P]))
                for i in range(2):
                    for b in range(TB):
                        units = [dict(q=qx[:, e, i, P * b:P * b + P], k=kx[:, i, :], mask=k.const("nomask"), half=e,
                                      v=lambda a, h=2 * i + e: vx[:, a, HD * h:HD * h + HD]) for e in range(2)]
                        groups.append((units, hT[:, 6 + i, P * b:P * b + P]))
                attend(k, groups)
            group_norm_phase(k, hT, G["mix"], [(0, 4), (4, 6), (6, 8)], ahead=2)
        projected.close()
        with nc.sbuf_tensor(k.unique("yT"), [P, KD, S], F32) as yT:
            product_phase(k, WO1, [dict(kind="features", to=lambda c, i=i: yT[:, 2 * i + c, :]) for i in range(4)], [(hT, KD, S)])
            norm_phase(k, [dict(x=yT, add=xT, gain=G["g_post_mix"]), dict(x=xT, out=hT, gain=G["g_pre_mlp"], after=True)], ahead=2)
            ffn1_phase(k, FFN1, hT, yT)
            norm_phase(k, [dict(x=yT, add=xT, gain=G["g_post_mlp"]), dict(x=xT, out=hT, gain=G["pre_mix_norm_2"], after=True)])

        splitting.close()

        with nc.sbuf_tensor(k.unique("z"), [P, 11, S + 1], F32) as z:
            with nc.sbuf_tensor(k.unique("q2"), [P, 2, 3, S], F32) as q2, nc.sbuf_tensor(k.unique("kv2"), [P, 4, S], F32) as kv2, \
                    nc.sbuf_tensor(k.unique("v2"), [P, TB, 256], F32) as v2, nc.sbuf_tensor(k.unique("u5"), [P, 2, S], F32) as u5, \
                    nc.sbuf_tensor(k.unique("gl2"), [P, TB, 18], F32) as gl2:
                tiles = [z[:, n, 1:S + 1] for n in range(11)] + [padded(q2, n) for n in range(3)] + [kv2[:, n, :] for n in range(4)]
                slabs = [dict(kind="features", to=lambda c, i=i: tiles[2 * i + c]) for i in range(9)]
                slabs += [dict(kind="tokens", to=v2)]
                slabs += [dict(kind="features", to=lambda c: u5[:, c, :])]
                slabs += [dict(kind="tokens", to=gl2, width=18)]
                k.phase()
                zeroed = k.sem("zeroed")
                with nc.Block() as block:
                    @block.gpsimd
                    def _(pool):
                        nc.gpsimd.memset(z[:, :, 0:1], 0.0).then_inc(*zeroed.inc())
                with nc.sbuf_tensor(k.unique("kcmp"), [P, NC], F32) as kcmp, nc.sbuf_tensor(k.unique("vcmp"), [NC, 2, HD], F32) as vcmp:
                    with ExitStack() as early:
                        s5 = S5(k, early, hT)
                        with k.splitting(), ExitStack() as work:
                            s5.work_buffers(work)
                            product_phase(k, IN2, slabs, [(hT, KD, S)], beside=s5, zero=other_halves(q2))
                        compress = compress_buffers(k, early)
                        s5_phase(k, s5, u5, hT[:, 6:8, :], z, mu, compress)
                        compress_phase(k, compress, kv2[:, 0, :], kv2[:, 1, :], kcmp[:], vcmp)
                    with nc.sbuf_tensor(k.unique("nsa_table"), [P, k.widths[1]], F32) as k.tables[1]:
                        k.phase()
                        sig, cut, table_loaded = k.sem("nsa_gate"), k.sem("nsa_gate_cut"), k.sem("nsa_table_loaded")
                        with nc.Block() as block:
                            @block.sync
                            def _(sp):
                                sp.dma_start(k.tables[1][:], io["nsa_table"]).then_inc(*table_loaded.dma())
                                sp.wait_ge(*table_loaded.dma_at(1))

                            @block.scalar
                            def _(act):
                                nc.scalar.activation(gl2[:], gl2[:], ACT.Sigmoid).then_inc(*sig.inc())

                            @block.vector
                            def _(dve):
                                dve.wait_ge(*sig.at(1))
                                c = gl2[:, 0, :].rearrange("p (h n) -> p h n", n=3)[:, :, 0]
                                nc.vector.tensor_scalar(c, c, k.const("anycmp"), None, ALU.mult).then_inc(*cut.inc())
                        groups = []
                        for j in range(3):
                            for b in range(TB):
                                units, w = [], P * (b + 1)
                                for branch in range(3):
                                    for half in range(2):
                                        h = 2 * j + half
                                        e = h // 3
                                        un = dict(q=q2[:, e, h % 3, P * b:P * b + P], half=half, gate=gl2[:, b, 3 * h + branch:3 * h + branch + 1])
                                        if branch == 0:
                                            at = NC * (6 * b + h)
                                            un.update(k=kcmp[:], mask=k.const("cmp")[:, at:at + NC], v=lambda a, e=e: vcmp[:, e, :])
                                        else:
                                            un.update(k=kv2[:, 1 + branch, 0:w], mask=k.const(f"causal{h}")[:, S - w:S],
                                                      v=lambda a, e=e, n=branch - 1: v2[:, a, P * n + HD * e:P * n + HD * e + HD])
                                        units.append(un)
                                groups.append((units, hT[:, 3 + j, P * b:P * b + P]))
                        attend(k, groups)
            with nc.sbuf_tensor(k.unique("y3"), [P, TB, RW], F32) as y3:
                rwkv_phases(k, z, y3, hT[:, 0:3, :])
                turn_phase(k, [([y3[:, b, P * f:P * f + P] for b in range(TB)], hT[:, f, :]) for f in range(3)])
        with k.splitting(), nc.sbuf_tensor(k.unique("yT2"), [P, KD, S], F32) as yT:
            product_phase(k, WO2, [dict(kind="features", to=lambda c, i=i: yT[:, 2 * i + c, :]) for i in range(4)], [(hT, KD, S)])
            norm_phase(k, [dict(x=yT, add=xT, gain=G["post_mix_norm_2"]), dict(x=xT, out=hT, gain=G["pre_ffn_norm_2"], after=True)], ahead=2)
            with nc.sbuf_tensor(k.unique("eT"), [P, KD, S], F32) as eT:
                with nc.sbuf_tensor(k.unique("pin"), [P, TB, PLE], F32) as pin, nc.sbuf_tensor(k.unique("pT"), [P, 2, S], F32) as pT:
                    ffn2_phase(k, FFN2, hT, yT, load=(pin[:], io["p_2"][0, 0].rearrange("(b p) d -> p b d", p=P)))
                    turn_phase(k, [([pin[:, b, P * f:P * f + P] for b in range(TB)], pT[:, f, :]) for f in range(2)], after=k.sem("p_loaded"))
                    ple_phase(k, pT, eT)
                norm_phase(k, [dict(x=yT, add=xT, gain=G["post_ffn_norm_2"]), dict(x=eT, out=eT, gain=gple)], ahead=2)
                gate_phase(k, GATEW, xT, hT, eT)
        with nc.sbuf_tensor(k.unique("xout"), [P, TB, D], F32) as xout:
            banks = []
            for b in range(TB):
                for half in range(2):
                    banks.append(([hT[:, 4 * half + f, P * b:P * b + P] for f in range(4)], xout[:, b, 512 * half:512 * half + 512]))
            rows = out[0].rearrange("(b p) d -> p b d", p=P)
            turn_phase(k, banks, store=lambda b: (rows[:, b, :], xout[:, b, :]))


def ple_phase(k, pT, eT):
    nc = k.nc
    k.phase()
    made, out = k.sem("ple_made"), [k.sem("ple_out_act"), k.sem("ple_out_dve")]
    x_hi, x_lo = k.sem("x_hi"), k.sem("x_lo")
    with nc.sbuf_tensor(k.unique("p_hi"), [P, 2, S], F32R) as ph, nc.sbuf_tensor(k.unique("p_lo"), [P, 2, S], F32R) as pl, \
            nc.Block() as block:
        parts = (ph, pl)
        @block.sync
        def _(sp):
            issue_slab(k, sp, PLEW + 2)

        @block.tensor
        def _(pe):
            w = [slab_view(k, PLEW % 2, a, D, 2) for a in range(2)]
            use_slab(k, pe, PLEW % 2, PLEW // 2)
            pe.wait_ge(*x_lo.at(1))
            for n in range(KD):
                if n >= 4:
                    pe.wait_ge(*out[n % 2].at((n - 4) // 2 + 1))
                m = product(nc, k.pl[:, n % 4, :], [([w[a][:, q, P * n:P * n + P] for a in range(2)],
                                                     [parts[a][:, q, :] for a in range(2)]) for q in range(2)])
                if n < KD - 1:
                    m.then_inc(*made.inc())
            m.then_inc(k.slab_done[PLEW % 2], 1)

        def empty(eng, e):
            for n in range(e, KD, 2):
                if n < KD - 1:
                    eng.wait_ge(*made.at(n + 1))
                else:
                    eng.wait_ge(k.slab_done[PLEW % 2], PLEW // 2 + 1)
                if e == 0:
                    nc.scalar.activation(eT[:, n, :], k.pl[:, n % 4, :], ACT.Copy).then_inc(*out[0].inc())
                else:
                    nc.vector.tensor_copy(eT[:, n, :], k.pl[:, n % 4, :]).then_inc(*out[1].inc())

        @block.scalar
        def _(act):
            nc.scalar.activation(ph[:], pT[:], ACT.Copy).then_inc(*x_hi.inc())
            empty(act, 0)

        @block.vector
        def _(dve):
            dve.wait_ge(*x_hi.at(1))
            nc.vector.tensor_tensor(pl[:], pT[:], ph[:].bitcast(F32), ALU.subtract).then_inc(*x_lo.inc())
            empty(dve, 1)



_INS = ["x", "mem", "positions", "g_pre_mix", "g_mem", "w_in", "w_mem_kv", "conv_w", "g_attn_out", "g_conv_out", "g_xattn_out",
        "w_out", "g_post_mix", "g_pre_mlp", "w_up", "w_down", "g_post_mlp", "p_2", "pre_mix_norm_2", "post_mix_norm_2",
        "pre_ffn_norm_2", "post_ffn_norm_2", "w_in_2", "w_out_2", "shift_mu_2", "rw_w0_2", "rw_w2_2", "rw_a0_2", "rw_a2_2",
        "rw_g2_2", "rw_k_k_2", "rw_k_a_2", "rw_r_k_2", "rw_gn_w_2", "rw_gn_b_2", "cmp_pe_k_2", "cmp_pe_v_2", "cmp_w1_k_2",
        "cmp_w2_k_2", "cmp_w1_v_2", "cmp_w2_v_2", "s5_lam_re_2", "s5_lam_im_2", "s5_log_dt_2", "s5_b_re_2", "s5_b_im_2",
        "s5_c_re_2", "s5_c_im_2", "s5_d_2", "s5_w_glu_2", "w_up_2", "conv_w_2", "conv_b_2", "w_down_2", "w_ple_2",
        "ple_norm_2", "w_ple_gate_2"]


def kernel(**inputs):
    import numpy as _np
    import concourse.bacc as _bacc
    from concourse import mybir as _mybir
    from concourse.bass_utils import run_bass_kernel_spmd as _run

    nc = _bacc.Bacc("TRN2", target_bir_lowering=False, num_devices=1)
    arrays, io = {}, {}
    given = {name: _np.ascontiguousarray(inputs[name]) for name in _INS}
    given["table"], given["nsa_table"] = constants()[1]
    for name, a in given.items():
        arrays[f"in_{name}"] = a
        io[name] = nc.dram_tensor(f"in_{name}", a.shape, _mybir.dt.from_np(a.dtype), kind="ExternalInput").ap()
    out = nc.dram_tensor("out_0", (1, S, D), F32, kind="ExternalOutput").ap()
    two_blocks(nc, io, out)
    r = _run(nc, [arrays], core_ids=[0])
    return r.results[0]["out_0"]
```
